# Optimizing a Trainium2 kernel written in Bass

```python
import math
import jax, jax.numpy as jnp
from jax import lax
import numpy as np

D_MODEL = 1024
BATCH = 1
SEQ = 1024
DEPTH = 1

N_MIXERS = 3
MEM_LEN = 256
EPS = 1e-6

A_HEADS = 4
A_DQK = D_MODEL // 8
A_DV = D_MODEL // A_HEADS
A_CHUNK = 64
A_CONV = 4
A_IN = 2 * A_HEADS * A_DQK + 2 * A_HEADS * A_DV + 2 * A_HEADS

B_HEADS = 4
B_DK = D_MODEL // 8
B_DV = D_MODEL // B_HEADS
B_RANK = 16
B_TAU = 16.0
B_CHUNK = 32
B_IN = 2 * B_HEADS * B_DK + 2 * B_HEADS * B_DV + B_RANK

C_GROUP = 16
C_GROUPS = D_MODEL // C_GROUP
C_STATE = 64
DT_MIN = 1e-3
DT_MAX = 1e-1

X_HEADS = 4
X_DH = D_MODEL // X_HEADS

D_FF = ((8 * D_MODEL + 3 * 256 - 1) // (3 * 256)) * 256

kernel_name = 'hybrid_mlstm_gla_s5_xattn_swiglu'

F32 = jnp.float32

def rmsnorm(x, g):
    xf = x.astype(F32)
    xf = xf * lax.rsqrt(jnp.mean(xf * xf, axis=-1, keepdims=True) + EPS)
    return (xf * g.astype(F32)).astype(x.dtype)

def head_rmsnorm(h, g):
    h = h * lax.rsqrt(jnp.mean(h * h, axis=-1, keepdims=True) + EPS)
    return h.reshape(h.shape[0], h.shape[1], -1) * g.astype(F32)

def causal_dwconv(x, w):
    K = w.shape[0]
    S = x.shape[1]
    xp = jnp.pad(x, ((0, 0), (K - 1, 0), (0, 0)))
    y = xp[:, 0:S] * w[0]
    for j in range(1, K):
        y = y + xp[:, j:j + S] * w[j]
    return y

def to_chunks(t, L):
    Bsz, S, H, d = t.shape
    return t.reshape(Bsz, S // L, L, H, d).transpose(1, 0, 3, 2, 4)

def from_chunks(t):
    nc, Bsz, H, L, d = t.shape
    return t.transpose(1, 0, 3, 2, 4).reshape(Bsz, nc * L, H, d)

def mlstm_mix(xn, w_in, conv_w, gate_b, norm_g, w_out):
    Bsz, S, _ = xn.shape
    H, dk, dv, L = A_HEADS, A_DQK, A_DV, A_CHUNK
    nc = S // L
    proj = xn @ w_in
    qk, v, o, g = jnp.split(proj, [2 * H * dk, 2 * H * dk + H * dv, 2 * H * dk + 2 * H * dv], axis=-1)
    qk = jax.nn.silu(causal_dwconv(qk, conv_w)).astype(F32)
    q = qk[..., :H * dk].reshape(Bsz, S, H, dk) * (dk ** -0.5)
    k = qk[..., H * dk:].reshape(Bsz, S, H, dk)
    v = v.astype(F32).reshape(Bsz, S, H, dv)
    g = g.astype(F32) + gate_b.astype(F32)
    i_pre = g[..., :H]
    log_f = jax.nn.log_sigmoid(g[..., H:])
    gate_chunks = lambda t: t.reshape(Bsz, nc, L, H).transpose(1, 0, 3, 2)
    causal = jnp.tril(jnp.ones((L, L), dtype=bool))

    def step(carry, inp):
        C, n, m = carry
        qc, kc, vc, ic, fc = inp
        b = jnp.cumsum(fc, axis=-1)
        dmat = b[..., :, None] - b[..., None, :] + ic[..., None, :]
        dmat = jnp.where(causal, dmat, -jnp.inf)
        inter = b + m[..., None]
        m_t = jnp.maximum(inter, jnp.max(dmat, axis=-1))
        w_intra = jnp.exp(dmat - m_t[..., None])
        w_inter = jnp.exp(inter - m_t)
        s = jnp.einsum('bhtd,bhsd->bhts', qc, kc) * w_intra
        num = jnp.einsum('bhts,bhsv->bhtv', s, vc) + w_inter[..., None] * jnp.einsum('bhtd,bhdv->bhtv', qc, C)
        den = jnp.sum(s, axis=-1) + w_inter * jnp.einsum('bhtd,bhd->bht', qc, n)
        h = num / jnp.maximum(jnp.abs(den), jnp.exp(-m_t))[..., None]
        g_tot = b[..., -1]
        a = g_tot[..., None] - b + ic
        m_new = jnp.maximum(g_tot + m, jnp.max(a, axis=-1))
        decay = jnp.exp(g_tot + m - m_new)
        wa = jnp.exp(a - m_new[..., None])
        C_new = decay[..., None, None] * C + jnp.einsum('bhs,bhsd,bhsv->bhdv', wa, kc, vc)
        n_new = decay[..., None] * n + jnp.einsum('bhs,bhsd->bhd', wa, kc)
        return (C_new, n_new, m_new), h

    init = (jnp.zeros((Bsz, H, dk, dv), F32), jnp.zeros((Bsz, H, dk), F32), jnp.zeros((Bsz, H), F32))
    _, h = lax.scan(step, init, (to_chunks(q, L), to_chunks(k, L), to_chunks(v, L),
                                 gate_chunks(i_pre), gate_chunks(log_f)))
    h = head_rmsnorm(from_chunks(h), norm_g) * jax.nn.sigmoid(o.astype(F32))
    return h.astype(xn.dtype) @ w_out

def gla_mix(xn, w_in, gate_w2, gate_b, norm_g, w_out):
    Bsz, S, _ = xn.shape
    H, dk, dv, L = B_HEADS, B_DK, B_DV, B_CHUNK
    proj = xn @ w_in
    q, k, v, r, g_low = jnp.split(proj, [H * dk, 2 * H * dk, 2 * H * dk + H * dv, 2 * H * dk + 2 * H * dv], axis=-1)
    log_a = jax.nn.log_sigmoid((g_low @ gate_w2 + gate_b).astype(F32)) / B_TAU
    q = q.astype(F32).reshape(Bsz, S, H, dk) * (dk ** -0.5)
    k = k.astype(F32).reshape(Bsz, S, H, dk)
    v = v.astype(F32).reshape(Bsz, S, H, dv)
    log_a = log_a.reshape(Bsz, S, H, dk)
    causal = jnp.tril(jnp.ones((L, L), dtype=bool))

    def step(state, inp):
        qc, kc, vc, lac = inp
        b = jnp.cumsum(lac, axis=2)
        rel = b[:, :, :, None, :] - b[:, :, None, :, :]
        rel = jnp.where(causal[:, :, None], rel, -jnp.inf)
        s = jnp.einsum('bhtd,bhsd,bhtsd->bhts', qc, kc, jnp.exp(rel))
        o = jnp.einsum('bhts,bhsv->bhtv', s, vc) + jnp.einsum('bhtd,bhdv->bhtv', qc * jnp.exp(b), state)
        b_last = b[:, :, -1:, :]
        k_dec = kc * jnp.exp(b_last - b)
        state = jnp.exp(b_last[:, :, 0, :])[..., None] * state + jnp.einsum('bhsd,bhsv->bhdv', k_dec, vc)
        return state, o

    _, o = lax.scan(step, jnp.zeros((Bsz, H, dk, dv), F32),
                    (to_chunks(q, L), to_chunks(k, L), to_chunks(v, L), to_chunks(log_a, L)))
    o = head_rmsnorm(from_chunks(o), norm_g) * jax.nn.silu(r.astype(F32))
    return o.astype(xn.dtype) @ w_out

def complex_affine_combine(e1, e2):
    ar1, ai1, br1, bi1 = e1
    ar2, ai2, br2, bi2 = e2
    ar = ar1 * ar2 - ai1 * ai2
    ai = ar1 * ai2 + ai1 * ar2
    br = ar2 * br1 - ai2 * bi1 + br2
    bi = ar2 * bi1 + ai2 * br1 + bi2
    return ar, ai, br, bi

def s5_mix(xn, w_in, lam_re, lam_im, log_dt, b_re, b_im, c_re, c_im, d_skip, w_gate, b_gate, w_out):
    Bsz, S, _ = xn.shape
    G, P, Hg = C_GROUPS, C_STATE, C_GROUP
    u = (xn @ w_in).astype(F32).reshape(Bsz, S, G, Hg)
    lr = lam_re.astype(F32)
    li = lam_im.astype(F32)
    dt = jnp.exp(log_dt.astype(F32))[:, None]
    mag = jnp.exp(lr * dt)
    ab_re = mag * jnp.cos(li * dt)
    ab_im = mag * jnp.sin(li * dt)
    den = lr * lr + li * li
    z_re = ((ab_re - 1.0) * lr + ab_im * li) / den
    z_im = (ab_im * lr - (ab_re - 1.0) * li) / den
    br = b_re.astype(F32)
    bi = b_im.astype(F32)
    bb_re = z_re[..., None] * br - z_im[..., None] * bi
    bb_im = z_re[..., None] * bi + z_im[..., None] * br
    bu_re = jnp.einsum('bsgh,gph->bsgp', u, bb_re)
    bu_im = jnp.einsum('bsgh,gph->bsgp', u, bb_im)
    a_re = jnp.broadcast_to(ab_re, (1, S, G, P))
    a_im = jnp.broadcast_to(ab_im, (1, S, G, P))
    _, _, s_re, s_im = lax.associative_scan(complex_affine_combine, (a_re, a_im, bu_re, bu_im), axis=1)
    y = (jnp.einsum('bsgp,ghp->bsgh', s_re, c_re.astype(F32))
         - jnp.einsum('bsgp,ghp->bsgh', s_im, c_im.astype(F32)))
    y = y + d_skip.astype(F32).reshape(G, Hg) * u
    y = jax.nn.gelu(y.reshape(Bsz, S, G * Hg)).astype(xn.dtype)
    y = y * jax.nn.sigmoid(y @ w_gate + b_gate)
    return y @ w_out

def cross_attn(xn, memn, w_q, w_kv, w_o):
    Bsz, S, D = xn.shape
    M = memn.shape[1]
    q = (xn @ w_q).reshape(Bsz, S, X_HEADS, X_DH)
    k, v = jnp.split(memn @ w_kv, 2, axis=-1)
    k = k.reshape(Bsz, M, X_HEADS, X_DH)
    v = v.reshape(Bsz, M, X_HEADS, X_DH)
    s = jnp.einsum('bshd,bmhd->bhsm', q, k).astype(F32) * (X_DH ** -0.5)
    p = jax.nn.softmax(s, axis=-1).astype(v.dtype)
    o = jnp.einsum('bhsm,bmhd->bshd', p, v).reshape(Bsz, S, D)
    return o @ w_o

def swiglu(xn, w_gate, w_up, w_down):
    return (jax.nn.silu(xn @ w_gate) * (xn @ w_up)) @ w_down

def setup_inputs(seed: int = 0) -> dict:
    key = jax.random.key(seed)
    ks = iter(jax.random.split(key, 64))

    def nrm(shape, scale):
        return jax.random.normal(next(ks), shape, F32) * scale

    def gain(shape):
        return 1.0 + nrm(shape, 0.02)

    D = D_MODEL
    n_a = len(range(0, DEPTH, N_MIXERS))
    n_b = len(range(1, DEPTH, N_MIXERS))
    n_c = len(range(2, DEPTH, N_MIXERS))
    d = {}
    d['x'] = nrm((BATCH, SEQ, D), 1.0)
    d['mem'] = nrm((BATCH, MEM_LEN, D), 1.0)
    d['norm_mix'] = gain((DEPTH, D))
    d['norm_x'] = gain((DEPTH, D))
    d['norm_ffn'] = gain((DEPTH, D))
    d['norm_mem'] = gain((D,))
    d['norm_final'] = gain((D,))
    d['a_w_in'] = nrm((n_a, D, A_IN), D ** -0.5)
    d['a_conv_w'] = nrm((n_a, A_CONV, 2 * A_HEADS * A_DQK), A_CONV ** -0.5)
    i_bias = nrm((n_a, A_HEADS), 0.1)
    f_bias = jnp.linspace(3.0, 6.0, A_HEADS, dtype=F32)[None, :] + nrm((n_a, A_HEADS), 0.1)
    d['a_gate_b'] = jnp.concatenate([i_bias, f_bias], axis=-1)
    d['a_norm'] = gain((n_a, A_HEADS * A_DV))
    d['a_w_out'] = nrm((n_a, A_HEADS * A_DV, D), (A_HEADS * A_DV) ** -0.5)
    d['b_w_in'] = nrm((n_b, D, B_IN), D ** -0.5)
    d['b_gate_w2'] = nrm((n_b, B_RANK, B_HEADS * B_DK), B_RANK ** -0.5)
    d['b_gate_b'] = nrm((n_b, B_HEADS * B_DK), 0.1)
    d['b_norm'] = gain((n_b, B_HEADS * B_DV))
    d['b_w_out'] = nrm((n_b, B_HEADS * B_DV, D), (B_HEADS * B_DV) ** -0.5)
    d['c_w_in'] = nrm((n_c, D, D), D ** -0.5)
    d['c_lam_re'] = -0.5 + nrm((n_c, C_GROUPS, C_STATE), 0.01)
    d['c_lam_im'] = math.pi * jnp.arange(C_STATE, dtype=F32)[None, None, :] + nrm((n_c, C_GROUPS, C_STATE), 0.01)
    d['c_log_dt'] = jax.random.uniform(next(ks), (n_c, C_GROUPS), F32, math.log(DT_MIN), math.log(DT_MAX))
    d['c_b_re'] = nrm((n_c, C_GROUPS, C_STATE, C_GROUP), (2 * C_GROUP) ** -0.5)
    d['c_b_im'] = nrm((n_c, C_GROUPS, C_STATE, C_GROUP), (2 * C_GROUP) ** -0.5)
    d['c_c_re'] = nrm((n_c, C_GROUPS, C_GROUP, C_STATE), 0.25)
    d['c_c_im'] = nrm((n_c, C_GROUPS, C_GROUP, C_STATE), 0.25)
    d['c_d'] = nrm((n_c, D), 0.5)
    d['c_w_gate'] = nrm((n_c, D, D), D ** -0.5)
    d['c_b_gate'] = nrm((n_c, D), 0.02)
    d['c_w_out'] = nrm((n_c, D, D), D ** -0.5)
    d['x_w_q'] = nrm((DEPTH, D, D), D ** -0.5)
    d['x_w_kv'] = nrm((DEPTH, D, 2 * D), D ** -0.5)
    d['x_w_o'] = nrm((DEPTH, D, D), D ** -0.5)
    d['f_w_gate'] = nrm((DEPTH, D, D_FF), D ** -0.5)
    d['f_w_up'] = nrm((DEPTH, D, D_FF), D ** -0.5)
    d['f_w_down'] = nrm((DEPTH, D_FF, D), D_FF ** -0.5)
    return d

def reference(x, mem, norm_mix, norm_x, norm_ffn, norm_mem, norm_final,
              a_w_in, a_conv_w, a_gate_b, a_norm, a_w_out,
              b_w_in, b_gate_w2, b_gate_b, b_norm, b_w_out,
              c_w_in, c_lam_re, c_lam_im, c_log_dt, c_b_re, c_b_im, c_c_re, c_c_im,
              c_d, c_w_gate, c_b_gate, c_w_out,
              x_w_q, x_w_kv, x_w_o,
              f_w_gate, f_w_up, f_w_down):
    memn = rmsnorm(mem, norm_mem)
    h = x
    for i in range(DEPTH):
        kind = i % N_MIXERS
        j = i // N_MIXERS
        hn = rmsnorm(h, norm_mix[i])
        if kind == 0:
            h = h + mlstm_mix(hn, a_w_in[j], a_conv_w[j], a_gate_b[j], a_norm[j], a_w_out[j])
        elif kind == 1:
            h = h + gla_mix(hn, b_w_in[j], b_gate_w2[j], b_gate_b[j], b_norm[j], b_w_out[j])
        else:
            h = h + s5_mix(hn, c_w_in[j], c_lam_re[j], c_lam_im[j], c_log_dt[j], c_b_re[j], c_b_im[j],
                           c_c_re[j], c_c_im[j], c_d[j], c_w_gate[j], c_b_gate[j], c_w_out[j])
        h = h + cross_attn(rmsnorm(h, norm_x[i]), memn, x_w_q[i], x_w_kv[i], x_w_o[i])
        h = h + swiglu(rmsnorm(h, norm_ffn[i]), f_w_gate[i], f_w_up[i], f_w_down[i])
    return rmsnorm(h, norm_final)


_drawn_inputs = setup_inputs


def setup_inputs(seed=0):
    import zlib

    import numpy as np

    out = dict(_drawn_inputs(seed))
    spreads = {}
    factors = {'norm_mix': 3.052,
     'norm_x': 8.0,
     'norm_ffn': 4.32,
     'norm_mem': 8.0,
     'norm_final': 2.746,
     'a_norm': 5.365}
    for name, (base, spread) in spreads.items():
        noise = np.random.default_rng([zlib.crc32(name.encode()), seed]).standard_normal(out[name].shape)
        drawn = base * np.exp(spread * noise) if base else spread * noise
        out[name] = __import__('jax').numpy.asarray(drawn.astype(out[name].dtype))
    for name, factor in factors.items():
        out[name] = (out[name] * factor).astype(out[name].dtype)
    return out
```

```python
import concourse.bass as bass
from concourse import mybir
from contextlib import ExitStack

F32, F32R = mybir.dt.float32, mybir.dt.float32r
ALU = mybir.AluOpType
ACT = mybir.ActivationFunctionType
AX = mybir.AxisListType.X

P = 128
EPS = 1e-6
LOWEST = -3.0e38


def build_block(nc, x, mem, norm_mix, norm_x, norm_ffn, norm_mem, norm_final, a_w_in, a_conv_w, a_gate_b,
                a_norm, a_w_out, x_w_q, x_w_kv, x_w_o, f_w_gate, f_w_up, f_w_down, out):
    S, D = x.shape[1], x.shape[2]
    M = mem.shape[1]
    KT = D // P
    TT = S // P
    MT = M // P
    HALF = 512
    NHALF = S // HALF
    H = a_gate_b.shape[1] // 2
    DK = a_conv_w.shape[2] // (2 * H)
    DV = D // H
    TAPS = a_conv_w.shape[1]
    SW = 2 * P
    F = f_w_gate.shape[2]
    NJ = F // SW
    QSCALE = float(DK) ** -0.5
    XSCALE = float(DV) ** -0.5
    V0, O0, G0 = 2 * H * DK, 2 * H * DK + H * DV, 2 * H * DK + 2 * H * DV
    R = H * TT
    assert DK == P and DV == SW and NJ % 2 == 1 and MT == 2 and KT == 8 and TT == 8 and H == 4

    STRIPS = [("qk", 0), ("v", 0), ("o", 0)]
    for h in range(1, H):
        STRIPS += [("qk", h), ("v", h), ("o", h), ("wo", h - 1)]
    STRIPS += [("mk", j) for j in range(H)] + [("mv", j) for j in range(H)]
    STRIPS += [("wo", H - 1), ("q", 0)]
    for h in range(1, H):
        STRIPS += [("q", h), ("xo", h - 1)]
    STRIPS += [("xo", H - 1)]
    NF = len(STRIPS)
    STRIPS += [("gate", 0), ("up", 0)]
    for j in range(1, NJ):
        STRIPS += [("gate", j), ("down", j - 1), ("up", j)]
    STRIPS += [("down", NJ - 1)]
    AT = {s: n for n, s in enumerate(STRIPS)}
    assert NF % 2 == 0
    NGROUPS = {"qk": 4, "v": 4, "o": 4, "wo": 16, "mk": 1, "mv": 1, "q": 4, "xo": 16,
               "gate": 4, "up": 4, "down": 16}
    BY_ACT = {"v", "o", "mk", "mv", "q", "gate"}
    FIRST, FREED, took, g = {}, [], {"act": 0, "dve": 0, "up": 0}, 0
    for n, (kind, _) in enumerate(STRIPS):
        FIRST[n] = g
        for _ in range(NGROUPS[kind]):
            who = "act" if kind in BY_ACT else "up" if kind == "up" else "dve"
            took[who] += 1
            FREED.append((who, took[who]))
            g += 1
    used = lambda n: FIRST[n] + NGROUPS[STRIPS[n][0]]
    NB = 4
    DMAS = []
    for kind, _ in STRIPS:
        DMAS.append((DMAS[-1] if DMAS else 0) + (2 if kind == "qk" else 1))
    PER_LOOP = {"strip": 6, "group": 48, "act": 8, "dve": 32, "up": 8}

    PARTS = {}

    def part(kind, h, r, what):
        PARTS.setdefault((AT[kind, h], r), []).append(what)

    for step, (kind, r) in enumerate([("v", 0), ("v", 2), ("v", 3), ("o", 0), ("o", 2)]):
        part(kind, 0, r, ("gates", step, None))
    for h in range(1, H):
        for p in range(10):
            kind, r = [("qk", p), ("v", p - 4), ("o", p - 8)][min(p // 4, 2)]
            part(kind, h, r, ("scan", h - 1, p))
    part("wo", H - 2, 0, ("memnorm", 0, None))
    part("wo", H - 2, 8, ("memturn", 0, None))
    for p in range(8):
        part("mk" if p < H else "mv", p % H, 0, ("scan", H - 1, p))
    part("mv", H - 1, "end", ("scan", H - 1, 8))
    part("mv", H - 1, "end", ("scan", H - 1, 9))
    part("wo", H - 1, 12, ("square", 0, 0))
    part("wo", H - 1, "end", ("square", 0, 1))
    part("wo", H - 1, "end", ("norm", 0, 0))
    part("wo", H - 1, "end", ("norm", 0, 1))
    for h in range(1, H):
        for p in range(4):
            part("q", h, p, ("attn", h - 1, p))
        part("q", h, "end", ("attn", h - 1, 4))
        part("q", h, "end", ("attn", h - 1, 5))
    for p in range(3):
        part("xo", H - 2, 4 + 4 * p, ("attn", H - 1, p))
    for p in range(3, 6):
        part("xo", H - 2, "end", ("attn", H - 1, p))
    part("xo", H - 1, 12, ("square", 1, 0))
    part("xo", H - 1, "end", ("square", 1, 1))
    part("xo", H - 1, "end", ("norm", 1, 0))
    part("xo", H - 1, "end", ("norm", 1, 1))

    def run_parts(n, r, todo):
        for what, a, b in PARTS.get((n, r), []):
            todo[what](a, b)

    x_t = x[0].rearrange("(t p) d -> t p d", p=P)
    mem_t = mem[0].rearrange("(t p) d -> t p d", p=P)
    out_t = out[0].rearrange("(t p) d -> t p d", p=P)

    def cols(w, at, width=SW):
        return w[0, :, at:at + width].rearrange("(k p) n -> p k n", p=P)

    def rows(w, at):
        return w[0, at:at + SW, :].rearrange("(k p) n -> p k n", p=P)

    ctx = ExitStack()
    with ctx:
        def sb(name, shape, dt=F32):
            return ctx.enter_context(nc.sbuf_tensor(name, shape, dt))

        def sem(name):
            return ctx.enter_context(nc.semaphore(name))

        xT = sb("xT", [P, KT, S])
        XH = sb("XH", [P, KT, S], F32R)
        XL = sb("XL", [P, KT, S], F32R)
        raw = sb("raw", [P, KT * SW])
        WH = sb("WH", [P, 2, KT * SW], F32R)
        WL = sb("WL", [P, 2, KT * SW], F32R)
        QK = sb("QK", [P, 2, 2, S])
        VV = sb("VV", [P, 2, TT, DV])
        SG = sb("SG", [P, 2, S])
        YH = sb("YH", [P, 2, S], F32R)
        YL = sb("YL", [P, 2, S], F32R)
        acc = sb("acc", [P, 2, HALF])
        ident = sb("ident", [P, P])
        ones = sb("ones", [P, P])
        vcols = sb("vcols", [P, 56])
        NORM_X, NORM_F, A_NORM, CONV = 0, KT, 2 * KT, 3 * KT
        halo = sb("halo", [P, 2, TAPS - 1])
        wgh = sb("wgh", [P, KT, 2 * H], F32R)
        wgl = sb("wgl", [P, KT, 2 * H], F32R)
        gbias = sb("gbias", [P, 2 * H])
        half_neg = sb("half_neg", [P, 1])
        stat = sb("stat", [P, TT, 3])
        ig = sb("ig", [P, R])
        lf = sb("lf", [P, R])
        gt1 = sb("gt1", [P, R])
        gt2 = sb("gt2", [P, R])
        bcum = sb("bcum", [P, R])
        gtot = sb("gtot", [P, R])
        acol = sb("acol", [P, R])
        mlast = sb("mlast", [P, R])
        mprev = sb("mprev", [P, R])
        mulast = sb("mulast", [P, R])
        decay = sb("decay", [P, R])
        wa = sb("wa", [P, R])
        emm = sb("emm", [P, R])
        murow = sb("murow", [R, P])
        mprow = sb("mprow", [R, 1])
        wT = sb("wT", [P, P])
        wi = sb("wi", [P, P])
        PT = sb("PT", [P, P])
        qs = sb("qs", [P, P])
        ks = sb("ks", [P, DK])
        Cst = sb("Cst", [P, DV])
        nst = sb("nst", [P, 1])
        hs = sb("hs", [P, DV])
        hsj = sb("hsj", [P, DV])
        eps_col = sb("eps_col", [P, 1])
        yf = sb("yf", [P, 2, P])
        ccol = sb("ccol", [P, 8])
        acol8 = sb("acol8", [P, 2, 8])
        PS = ctx.enter_context(nc.psum_tensor("PS", [P, 8, HALF], F32))
        X0, X1, X2, X3 = (PS[:, NB + i, :] for i in range(4))

        xin = VV[:, 0].rearrange("p t d -> p (t d)").rearrange("p (a d) -> p a d", a=2)
        xs = VV[:, 1].rearrange("p t d -> p (t d)").rearrange("p (a d) -> p a d", a=2)
        mxin = QK[:, 0]
        mxs = mxin
        mspare = VV[:, 0].rearrange("p t d -> p (t d)").rearrange("p (a d) -> p a d", a=2)
        gain_mem, mjunk = mspare[:, 0, :], mspare[:, 1, :]
        gain_mix = SG[:, 0, :]
        gain_out = SG[:, 0, :]
        tri = SG[:, 1, 0:P]
        cmax = SG[0:R, 1, HALF:HALF + 2 * (64 + P)].rearrange("r (a t) -> r a t", a=2)
        vrows = QK[0:56, 0, 0, 0:P]
        wg_raw = QK[:, 0, 1, 0:KT * 2 * H].rearrange("p (k g) -> p k g", k=KT)
        MH = XH[:, 0:2, :].rearrange("p k s -> p (k s)").rearrange("p (k m) -> p k m", k=KT)
        ML = XL[:, 0:2, :].rearrange("p k s -> p (k s)").rearrange("p (k m) -> p k m", k=KT)
        KM = QK[:, 0].rearrange("p a s -> p (a s)").rearrange("p (k m) -> p k m", k=KT)
        VM = VV[:, 0].rearrange("p t d -> p (t d)").rearrange("p (a d) -> p a d", a=MT)
        QH = [VV[:, 1].rearrange("p t d -> p (t d)").rearrange("p (a s) -> p a s", a=2), SG[:, :, :]]
        PA = QK[:, 1].rearrange("p a s -> p (a s)").rearrange("p (m s) -> p m s", m=MT)
        ptok = acc[:, :, :]
        sqb = SG[:, 0, :].rearrange("p (a s) -> p a s", a=2)
        xnf = SG[:, 1, :].rearrange("p (a s) -> p a s", a=2)
        rstd = QK[:, 1, 0, :].rearrange("p (a s) -> p a s", a=NHALF)
        rstd2 = QK[:, 1, 1, :].rearrange("p (a s) -> p a s", a=NHALF)
        fout = VV[:, 0].rearrange("p t d -> p (t d)").rearrange("p (a d) -> p a d", a=2)
        junk = QK[:, 1, 1, :]

        s_const = sem("s_const")
        s_vec = sem("s_vec")
        s_gain = sem("s_gain")
        s_wg = sem("s_wg")
        s_gb = sem("s_gb")
        s_xin = [sem(f"s_xin{i}") for i in range(2)]
        s_min = [sem(f"s_min{i}") for i in range(2)]
        s_sq = sem("s_sq")
        s_rs = sem("s_rs")
        s_ms = sem("s_ms")
        s_xs = sem("s_xs")
        s_turn = sem("s_turn")
        s_xt = sem("s_xt")
        s_xh = sem("s_xh")
        s_xl = sem("s_xl")
        s_vturn = sem("s_vturn")
        s_vc = sem("s_vc")
        s_wgs = sem("s_wgs")
        s_wdma = sem("s_wdma")
        s_whi = sem("s_whi")
        s_wlo = sem("s_wlo")
        s_mm = sem("s_mm")
        s_fa = sem("s_fa")
        s_fd = sem("s_fd")
        s_conv = sem("s_conv")
        s_qk = sem("s_qk")
        s_gpe = sem("s_gpe")
        s_gd = sem("s_gd")
        s_ga = sem("s_ga")
        s_mu = sem("s_mu")
        s_st = sem("s_st")
        s_wt = sem("s_wt")
        s_mask = sem("s_mask")
        s_wi = sem("s_wi")
        s_ks = sem("s_ks")
        s_pt = sem("s_pt")
        s_qs = sem("s_qs")
        s_b = sem("s_b")
        s_hs = sem("s_hs")
        s_cst = sem("s_cst")
        s_hsq = sem("s_hsq")
        s_hm = sem("s_hm")
        s_hr = sem("s_hr")
        s_hn = sem("s_hn")
        s_tr = sem("s_tr")
        s_yf = sem("s_yf")
        s_yh = sem("s_yh")
        s_yl = sem("s_yl")
        s_sc = sem("s_sc")
        s_mx = sem("s_mx")
        s_ex = sem("s_ex")
        s_pn = sem("s_pn")
        s_pt2 = sem("s_pt2")
        s_pa = sem("s_pa")
        s_pv = sem("s_pv")
        s_sqn = sem("s_sqn")
        s_ssq = sem("s_ssq")
        s_rt = sem("s_rt")
        s_xnf = sem("s_xnf")
        s_hf = sem("s_hf")
        s_out = [sem(f"s_out{i}") for i in range(2)]
        s_dve = sem("s_dve")

        Y_FFN = H * TT + H * 4

        block = ctx.enter_context(nc.Block())

        def turned(sc, act, t):
            act.wait_ge(s_turn, t + 1)
            for q in range(2):
                sc.activation(XH[:, 4 * q:4 * q + 4, t * P:(t + 1) * P],
                              PS[:, 4 * (t % 2) + 2 + q, :].rearrange("p (k s) -> p k s", k=4), ACT.Copy).then_inc(s_xh, 1)

        def turned_dve(v, dve, t):
            dve.wait_ge(s_turn, t + 1)
            v.tensor_copy(xT[:, :, t * P:(t + 1) * P].rearrange("p (a k) s -> p a k s", a=2),
                          PS[:, 4 * (t % 2):4 * (t % 2) + 2, :].rearrange("p a (k s) -> p a k s", k=4)).then_inc(s_xt, 1)
            for q in range(2):
                dve.wait_ge(s_xh, 2 * t + q + 1)
                at = slice(t * P, (t + 1) * P)
                v.tensor_tensor(XL[:, 4 * q:4 * q + 4, at], PS[:, 4 * (t % 2) + 2 + q, :].rearrange("p (k s) -> p k s", k=4),
                                XH[:, 4 * q:4 * q + 4, at].bitcast(F32), ALU.subtract).then_inc(s_xl, 1)

        def strip_src(kind, h):
            c3 = raw[:, :].rearrange("p (k n) -> p k n", k=KT)
            r3 = raw[:, :].rearrange("p (k n) -> p k n", k=2)
            if kind == "qk":
                return [(c3[:, :, 0:DK], cols(a_w_in, h * DK, DK)),
                        (c3[:, :, DK:SW], cols(a_w_in, (H + h) * DK, DK))]
            if kind in ("wo", "xo"):
                return [(r3, rows(a_w_out if kind == "wo" else x_w_o, h * SW))]
            w, at = {"v": (a_w_in, V0), "o": (a_w_in, O0), "mk": (x_w_kv, 0), "mv": (x_w_kv, D),
                     "q": (x_w_q, 0)}[kind]
            return [(c3, cols(w, at + h * SW))]

        @block.sync
        def _(sp):
            def load_strip(n):
                if n >= 1:
                    sp.wait_ge(s_wlo, n)
                for dst, src in strip_src(*STRIPS[n]):
                    sp.dma_start(dst, src).then_inc(s_wdma, 16)

            sp.dma_start(gain_mix, norm_mix[0:1, :].to_broadcast([P, D])).then_inc(s_gain, 16)
            for t in range(TT):
                if t >= 2:
                    sp.wait_ge(s_turn, t - 1)
                    sp.wait_ge(s_xs, t - 1)
                    sp.wait_ge(s_sq, t - 1)
                sp.dma_start(xin[:, t % 2, :], x_t[t]).then_inc(s_xin[t % 2], 16)
                if t == 1:
                    for v, at, n in ((norm_x, NORM_X, KT), (norm_ffn, NORM_F, KT), (a_norm, A_NORM, KT)):
                        sp.dma_start(vrows[at:at + n, :], v[0].rearrange("(k p) -> k p", p=P)).then_inc(s_vec, 16)
                    sp.dma_start(vrows[CONV:CONV + TAPS * KT, :],
                                 a_conv_w[0].rearrange("j (k p) -> (j k) p", p=P)).then_inc(s_vec, 16)
                    sp.dma_start(wg_raw, cols(a_w_in, G0, 2 * H)).then_inc(s_wg, 16)
                    sp.dma_start(gbias[:, :], a_gate_b[0:1, :].to_broadcast([P, 2 * H])).then_inc(s_gb, 16)
                    load_strip(0)
            for n in range(1, NF):
                if n == AT["wo", H - 2]:
                    sp.wait_ge(s_b, TT * (H - 1))
                    sp.dma_start(gain_mem, norm_mem.rearrange("(o d) -> o d", o=1).to_broadcast([P, D])).then_inc(s_gain, 16)
                    for t in range(MT):
                        sp.dma_start(mxin[:, t, :], mem_t[t]).then_inc(s_min[t], 16)
                load_strip(n)

            def load_ffn(n, w, j, is_rows, i=None):
                k = 0 if i is None else i
                sp.wait_ge(s_wlo, n + PER_LOOP["strip"] * k)
                at = (j + 2 * k) * SW
                if is_rows:
                    src = w[0, bass.ds(at, SW), :].rearrange("(k p) n -> p k n", p=P)
                    dst = raw[:, :].rearrange("p (k n) -> p k n", k=2)
                else:
                    src = w[0, :, bass.ds(at, SW)].rearrange("(k p) n -> p k n", p=P)
                    dst = raw[:, :].rearrange("p (k n) -> p k n", k=KT)
                sp.dma_start(dst, src).then_inc(s_wdma, 16)

            load_ffn(NF, f_w_gate, 0, False)
            load_ffn(NF + 1, f_w_up, 0, False)
            with sp.Fori(0, NJ // 2) as i:
                for u in range(2):
                    n = NF + 2 + 3 * u
                    load_ffn(n, f_w_gate, 1 + u, False, i)
                    load_ffn(n + 1, f_w_down, u, True, i)
                    load_ffn(n + 2, f_w_up, 1 + u, False, i)
            load_ffn(len(STRIPS) - 1, f_w_down, NJ - 1, True)
            sp.wait_ge(s_hf, 4 * NJ)
            sp.dma_start(gain_out, norm_final.rearrange("(o d) -> o d", o=1).to_broadcast([P, D])).then_inc(s_gain, 16)
            for t in range(TT):
                sp.wait_ge(s_xs, TT + MT + t + 1)
                sp.dma_start(out_t[t], fout[:, t % 2, :]).then_inc(s_out[t % 2], 16)
            for t in range(2):
                sp.wait_ge(s_out[t], 16 * TT // 2)

        @block.gpsimd
        def _(pool):
            gp = nc.gpsimd
            gp.memset(ident[:, :], 0.0).then_inc(s_const, 1)
            gp.memset(ones[:, :], 1.0).then_inc(s_const, 1)
            gp.memset(tri, 1.0).then_inc(s_const, 1)
            gp.memset(half_neg[:, :], -0.5).then_inc(s_const, 1)
            gp.memset(eps_col[:, :], EPS).then_inc(s_const, 1)
            gp.memset(cmax, LOWEST).then_inc(s_const, 1)
            pool.wait_ge(s_const, 6)
            gp.affine_select(out=ident[:, :], in_=ident[:, :], compare_op=ALU.not_equal, fill=1.0, base=0,
                             pattern=[[-1, P]], channel_multiplier=1).then_inc(s_const, 1)
            gp.affine_select(out=tri, in_=tri, compare_op=ALU.is_ge, fill=0.0, base=0,
                             pattern=[[1, P]], channel_multiplier=-1).then_inc(s_const, 1)

            def rms(t, src, mean, dst, count, width):
                pool.wait_ge(s_sq, count)
                gp.tensor_scalar(mean, src, 1.0 / width, EPS, ALU.mult, ALU.add).then_inc(s_ms, 1)
                pool.wait_ge(s_ms, count)
                gp.tensor_tensor(dst, mean, half_neg[:, :], ALU.pow).then_inc(s_rs, 1)

            def split_lo(n, i=None):
                k = 0 if i is None else i
                pool.wait_ge(s_whi, n + 1 + PER_LOOP["strip"] * k)
                gp.tensor_tensor(WL[:, n % 2, :], raw[:, :], WH[:, n % 2, :].bitcast(F32),
                                 ALU.subtract).then_inc(s_wlo, 1)

            def scan(h, p):
                if p < TT:
                    e = h * TT + p
                    pool.wait_ge(s_wt, e + 1)
                    gp.affine_select(out=wT[:, :], in_=wT[:, :], compare_op=ALU.is_ge, fill=0.0, base=0,
                                     pattern=[[1, P]], channel_multiplier=-1).then_inc(s_mask, 1)
                if 1 <= p <= TT:
                    e = h * TT + p - 1
                    pool.wait_ge(s_hsq, e + 1)
                    gp.tensor_scalar(ccol[:, 3:4], ccol[:, 2:3], 1.0 / DV, EPS, ALU.mult, ALU.add).then_inc(s_hm, 1)
                    pool.wait_ge(s_hm, e + 1)
                    if e >= 1:
                        pool.wait_ge(s_hn, e)
                    gp.tensor_tensor(ccol[:, 4:5], ccol[:, 3:4], half_neg[:, :], ALU.pow).then_inc(s_hr, 1)
                if p >= 2:
                    e = h * TT + p - 2
                    pool.wait_ge(s_yh, e + 1)
                    at = (p - 2) * P
                    gp.tensor_tensor(YL[:, :, at:at + P], yf[:, :, :], YH[:, :, at:at + P].bitcast(F32),
                                     ALU.subtract).then_inc(s_yl, 1)

            def memnorm(a, b):
                for t in range(MT):
                    rms(t, stat[:, t, 0:1], stat[:, t, 1:2], stat[:, t, 2:3], TT + t + 1, D)

            def norm(which, half):
                for k in range(KT):
                    c = KT * (NHALF * which + half) + k
                    pool.wait_ge(s_xh, 2 * TT + 2 * MT + c + 1)
                    at = half * HALF
                    gp.tensor_tensor(XL[:, k, at:at + HALF], xnf[:, k % 2, :],
                                     XH[:, k, at:at + HALF].bitcast(F32), ALU.subtract).then_inc(s_xl, 1)

            todo = {"scan": scan, "memnorm": memnorm, "norm": norm}
            for what in ("gates", "memturn", "square", "attn"):
                todo[what] = lambda a, b: None

            for t in range(TT):
                rms(t, stat[:, t, 0:1], stat[:, t, 1:2], stat[:, t, 2:3], t + 1, D)
                if t == 3:
                    split_lo(0)
            for n in range(NF):
                split_lo(n + 1)
                for r in [*range(NGROUPS[STRIPS[n][0]]), "end"]:
                    run_parts(n, r, todo)

            def ffn_lo(j, i=None):
                k = 0 if i is None else i
                for r in range(4):
                    c = 4 * j + r
                    pool.wait_ge(s_yh, Y_FFN + c + 1 + 8 * k)
                    nt, at = r % 2, (r // 2) * HALF
                    gp.tensor_tensor(YL[:, nt, at:at + HALF], acc[:, r % 2, :],
                                     YH[:, nt, at:at + HALF].bitcast(F32), ALU.subtract).then_inc(s_yl, 1)

            split_lo(NF + 1)
            split_lo(NF + 2)
            ffn_lo(0)
            with pool.Fori(0, NJ // 2) as i:
                for u in range(2):
                    n = NF + 2 + 3 * u
                    split_lo(n + 1, i)
                    split_lo(n + 2, i)
                    split_lo(n + 3, i)
                    ffn_lo(1 + u, i)
            for t in range(TT):
                rms(t, stat[:, t, 0:1], stat[:, t, 1:2], stat[:, t, 2:3], TT + MT + t + 1, D)

        @block.scalar
        def _(act):
            sc = nc.scalar

            def split_hi(n, i=None):
                k = 0 if i is None else i
                act.wait_ge(s_wdma, 16 * DMAS[n] + 16 * PER_LOOP["strip"] * k)
                if n >= 2:
                    act.wait_ge(s_mm, used(n - 2) + PER_LOOP["group"] * k)
                sc.activation(WH[:, n % 2, :], raw[:, :], ACT.Copy).then_inc(s_whi, 1)

            def square_tile(t, src, junk_out, count):
                if count > 1:
                    act.wait_ge(s_sq, count - 1)
                sc.activation(junk_out, src, ACT.Square, accum_out=stat[:, t, 0:1]).then_inc(s_sq, 1)

            def gates(step, b):
                if step == 1:
                    act.wait_ge(s_gd, 1)
                    sc.activation(gt1[:, :], gt2[:, :], ACT.Exp).then_inc(s_ga, 1)
                    act.wait_ge(s_ga, 1)
                    sc.activation(gt2[:, :], gt1[:, :], ACT.Ln, bias=1.0).then_inc(s_ga, 1)
                if step == 3:
                    act.wait_ge(s_gd, 5)
                    sc.activation(decay[:, :], gt1[:, :], ACT.Exp).then_inc(s_ga, 1)
                    sc.activation(wa[:, :], gt2[:, :], ACT.Exp).then_inc(s_ga, 1)
                if step == 4:
                    act.wait_ge(s_gd, 6)
                    sc.activation(emm[:, :], mulast[:, :], ACT.Exp, scale=-1.0).then_inc(s_ga, 1)

            def scan(h, p):
                if p < TT:
                    e = h * TT + p
                    if e == 0:
                        act.wait_ge(s_ga, 5)
                        act.wait_ge(s_gd, 6)
                    act.wait_ge(s_mu, e + 1)
                    if e >= 1:
                        act.wait_ge(s_pt, e)
                        act.wait_ge(s_qs, e)
                        act.wait_ge(s_b, e)
                    sc.activation(wT[:, :], X0[:, 0:P], ACT.Exp, scale=-1.0, bias=acol[:, e:e + 1]).then_inc(s_wt, 1)
                    sc.activation(wi[:, :], X0[:, 0:P], ACT.Exp, scale=-1.0, bias=mprev[:, e:e + 1]).then_inc(s_wi, 1)
                    sc.activation(ks[:, :], X0[:, P:2 * P], ACT.Copy, scale=wa[:, e:e + 1]).then_inc(s_ks, 1)
                if 1 <= p <= TT:
                    e = h * TT + p - 1
                    act.wait_ge(s_hs, e + 1)
                    if e >= 1:
                        act.wait_ge(s_hm, e)
                        act.wait_ge(s_hsq, e)
                    sc.activation(hsj[:, :], hs[:, :], ACT.Square, accum_out=ccol[:, 2:3]).then_inc(s_hsq, 1)
                if p >= 2:
                    e = h * TT + p - 2
                    act.wait_ge(s_yf, e + 1)
                    if p == 2 and h >= 1:
                        act.wait_ge(s_mm, used(AT["wo", h - 1]))
                    at = (p - 2) * P
                    sc.activation(YH[:, :, at:at + P], yf[:, :, :], ACT.Copy).then_inc(s_yh, 1)

            def memnorm(a, b):
                for t in range(MT):
                    act.wait_ge(s_min[t], 16)
                    if t == 0:
                        act.wait_ge(s_b, TT * (H - 1))
                    square_tile(t, mxin[:, t, :], mjunk, TT + t + 1)

            def memturn(a, b):
                act.wait_ge(s_mm, used(AT["o", H - 1]))
                for t in range(MT):
                    act.wait_ge(s_turn, TT + t + 1)
                    for q in range(2):
                        sc.activation(MH[:, 4 * q:4 * q + 4, t * P:(t + 1) * P],
                                      PS[:, NB + 2 * t + q, :].rearrange("p (k s) -> p k s", k=4),
                                      ACT.Copy).then_inc(s_xh, 1)

            def square(which, half):
                last = FREED[FIRST[AT[("wo", "xo")[which], H - 1]] + 8 * half + 7][1]
                for k in range(KT):
                    c = KT * (NHALF * which + half) + k
                    if k == 0:
                        act.wait_ge(s_fd, last)
                        if which == 1:
                            act.wait_ge(s_sc, H * 4)
                    if c >= 2:
                        act.wait_ge(s_ssq, c - 1)
                    sc.activation(sqb[:, k % 2, :], xT[:, k, half * HALF:(half + 1) * HALF],
                                  ACT.Square).then_inc(s_sqn, 1)

            def norm(which, half):
                c0 = NHALF * which + half
                act.wait_ge(s_ssq, KT * (c0 + 1))
                if which == 1 and half == 0:
                    act.wait_ge(s_pv, H * 4)
                sc.activation(rstd2[:, half, :], PS[:, NB + half, :], ACT.Sqrt, scale=1.0 / D,
                              bias=eps_col[:, 0:1]).then_inc(s_rt, 1)
                if half == 0:
                    act.wait_ge(s_mm, used(AT["mv", H - 1] if which == 0 else AT["q", H - 1]))
                for k in range(KT):
                    act.wait_ge(s_xnf, KT * c0 + k + 1)
                    at = half * HALF
                    sc.activation(XH[:, k, at:at + HALF], xnf[:, k % 2, :], ACT.Copy).then_inc(s_xh, 1)

            def attn(h, p):
                if p < 4:
                    e = 4 * h + p
                    act.wait_ge(s_mx, e + 1)
                    if e >= 2:
                        act.wait_ge(s_pt2, e - 1)
                    for j in range(2):
                        sc.activation(ptok[:, e % 2, j * M:(j + 1) * M], PS[:, NB + e % 2, j * M:(j + 1) * M], ACT.Exp,
                                      scale=XSCALE, bias=acol8[:, e % 2, 2 + j:3 + j],
                                      accum_out=acol8[:, e % 2, 4 + j:5 + j]).then_inc(s_ex, 1)
                if p in (3, 5):
                    for dt in range(2):
                        c = 4 * h + 2 * (p // 2 - 1) + dt
                        act.wait_ge(s_pv, c + 1)
                        if p == 3 and dt == 0:
                            act.wait_ge(s_mm, used(AT["wo", H - 1] if h == 0 else AT["xo", h - 1]))
                        at = (p // 2 - 1) * HALF
                        sc.activation(YH[:, dt, at:at + HALF], X3[:, :], ACT.Copy).then_inc(s_yh, 1)

            todo = {"gates": gates, "scan": scan, "memnorm": memnorm, "memturn": memturn, "square": square,
                    "norm": norm, "attn": attn}

            def evac(n, r):
                kind, h = STRIPS[n]
                g = FIRST[n] + r
                bank = PS[:, g % NB, :]
                if kind == "qk":
                    c = 4 * h + r
                    act.wait_ge(s_conv, c + 1)
                    if r == 0 and h >= 2:
                        act.wait_ge(s_b, TT * (h - 1))
                    at = (r // 2) * HALF
                    sc.activation(QK[:, h % 2, r % 2, at:at + HALF], acc[:, r % 2, :], ACT.Silu).then_inc(s_qk, 1)
                    return
                if kind not in BY_ACT:
                    return
                act.wait_ge(s_mm, g + 1)
                if kind == "v":
                    if r == 0 and h == 0:
                        act.wait_ge(s_turn, TT)
                    if r == 0 and h >= 2:
                        act.wait_ge(s_b, TT * (h - 1))
                    sc.activation(VV[:, h % 2, 2 * r:2 * r + 2, :], bank.rearrange("p (t d) -> p t d", t=2),
                                  ACT.Copy).then_inc(s_fa, 1)
                elif kind == "o":
                    if r == 0 and h == 0:
                        act.wait_ge(s_gd, 5)
                    if r == 0 and h >= 1:
                        act.wait_ge(s_yf, TT * h)
                    sc.activation(SG[:, r % 2, (r // 2) * HALF:(r // 2 + 1) * HALF], bank,
                                  ACT.Sigmoid).then_inc(s_fa, 1)
                elif kind == "mk":
                    if h == 0:
                        act.wait_ge(s_turn, TT + MT)
                        act.wait_ge(s_xs, TT + MT)
                    sc.activation(KM[:, 2 * h:2 * h + 2, :], bank.rearrange("p (t d) -> p t d", t=2),
                                  ACT.Copy).then_inc(s_fa, 1)
                elif kind == "mv":
                    sc.activation(VM[:, :, h * SW:(h + 1) * SW], bank.rearrange("p (t d) -> p t d", t=2),
                                  ACT.Copy).then_inc(s_fa, 1)
                elif kind == "q":
                    if r == 0 and h == 0:
                        act.wait_ge(s_b, TT * H)
                    if r == 0 and h == 1:
                        act.wait_ge(s_xl, 2 * TT + 2 * MT + 2 * KT)
                    if r == 0 and h >= 2:
                        act.wait_ge(s_sc, 4 * (h - 1))
                    sc.activation(QH[h % 2][:, r % 2, (r // 2) * HALF:(r // 2 + 1) * HALF], bank,
                                  ACT.Copy).then_inc(s_fa, 1)

            act.wait_ge(s_const, 8)
            for t in range(TT):
                act.wait_ge(s_xin[t % 2], 16 * (t // 2 + 1))
                square_tile(t, xin[:, t % 2, :], junk, t + 1)
                if t >= 1:
                    turned(sc, act, t - 1)
                if t == 3:
                    split_hi(0)
            turned(sc, act, TT - 1)
            for n in range(NF):
                kind, h = STRIPS[n]
                split_hi(n + 1)
                for r in range(NGROUPS[kind]):
                    run_parts(n, r, todo)
                    if kind == "o" and h >= 1 and r < 2:
                        if r == 1:
                            evac(n, 0)
                            evac(n, 1)
                    else:
                        evac(n, r)
                run_parts(n, "end", todo)

            def gate_evac(n, j, i=None):
                k = 0 if i is None else i
                for r in range(4):
                    g = FIRST[n] + r
                    act.wait_ge(s_mm, g + 1 + PER_LOOP["group"] * k)
                    if j >= 1:
                        if r == 0:
                            act.wait_ge(s_hf, 4 * j + 8 * k)
                    else:
                        act.wait_ge(s_xl, 2 * TT + 2 * MT + 4 * KT)
                    sc.activation(SG[:, r % 2, (r // 2) * HALF:(r // 2 + 1) * HALF], PS[:, g % NB, :],
                                  ACT.Silu).then_inc(s_fa, 1)

            def ffn_hi(j, down, i=None):
                k = 0 if i is None else i
                for r in range(4):
                    act.wait_ge(s_hf, 4 * j + r + 1 + 8 * k)
                    if r == 0:
                        act.wait_ge(s_mm, used(down) + PER_LOOP["group"] * k)
                    nt, at = r % 2, (r // 2) * HALF
                    sc.activation(YH[:, nt, at:at + HALF], acc[:, r % 2, :], ACT.Copy).then_inc(s_yh, 1)

            split_hi(NF + 1)
            gate_evac(NF, 0)
            split_hi(NF + 2)
            ffn_hi(0, AT["xo", H - 1])
            with act.Fori(0, NJ // 2) as i:
                for u in range(2):
                    n = NF + 2 + 3 * u
                    split_hi(n + 1, i)
                    gate_evac(n, 1 + u, i)
                    split_hi(n + 2, i)
                    split_hi(n + 3, i)
                    ffn_hi(1 + u, n + 1, i)
            for t in range(TT):
                act.wait_ge(s_turn, TT + MT + t + 1)
                square_tile(t, PS[:, 2 * (t % 4):2 * (t % 4) + 2, :].rearrange("p a s -> p (a s)"), junk, TT + MT + t + 1)

        @block.vector
        def _(dve):
            v = nc.vector
            steps = [0]

            def link(ins):
                steps[0] += 1
                ins.then_inc(s_dve, 1)
                dve.wait_ge(s_dve, steps[0])

            def gates(step, b):
                if step == 0:
                    dve.wait_ge(s_gpe, 1)
                    dve.wait_ge(s_gb, 16)
                    z = X0[:, 0:TT * 2 * H].rearrange("p (c g) -> p g c", g=2 * H)
                    gb = gbias[:, :].rearrange("p (g o) -> p g o", o=1).to_broadcast([P, 2 * H, TT])
                    v.tensor_tensor(ig[:, :].rearrange("p (g c) -> p g c", g=H), z[:, 0:H], gb[:, 0:H], ALU.add)
                    link(v.tensor_tensor(lf[:, :].rearrange("p (g c) -> p g c", g=H), z[:, H:], gb[:, H:], ALU.add))
                    v.scalar_tensor_tensor(out=gt2[:, :], in0=lf[:, :], scalar=-1.0, in1=lf[:, :], op0=ALU.mult,
                                           op1=ALU.min).then_inc(s_gd, 1)
                    link(v.tensor_scalar(lf[:, :], lf[:, :], 0.0, None, ALU.min))
                    dve.wait_ge(s_ga, 2)
                    v.tensor_tensor(lf[:, :], lf[:, :], gt2[:, :], ALU.subtract).then_inc(s_gd, 1)
                if step == 1:
                    dve.wait_ge(s_gpe, 2)
                    v.tensor_copy(bcum[:, :], X1[:, 0:R])
                    link(v.tensor_copy(gtot[:, :], X1[:, R:2 * R]))
                    v.tensor_tensor(acol[:, :], ig[:, :], bcum[:, :], ALU.subtract).then_inc(s_gd, 1)
                if step == 2:
                    dve.wait_ge(s_gpe, 3)
                    link(v.tensor_copy(cmax[:, 0, 64:], X2[0:R, 0:P]))
                    s, a = 1, 0
                    while s < P:
                        link(v.tensor_tensor(cmax[:, 1 - a, 64:], cmax[:, a, 64:], cmax[:, a, 64 - s:64 + P - s], ALU.max))
                        s, a = 2 * s, 1 - a
                    v.tensor_scalar(gt1[0:R, :], ident[0:R, 0:R], cmax[:, a, 64 + P - 1:64 + P], None,
                                    ALU.mult).then_inc(s_gd, 1)
                if step == 3:
                    dve.wait_ge(s_gpe, 4)
                    link(v.tensor_copy(mlast[:, :], X3[:, 0:R]))
                    hc = lambda t: t[:, :].rearrange("p (h c) -> p h c", h=H)
                    link(v.memset(hc(mprev)[:, :, 0:1], 0.0))
                    for c in range(TT - 1):
                        link(v.tensor_tensor(hc(mulast)[:, :, c:c + 1], hc(mprev)[:, :, c:c + 1], hc(mlast)[:, :, c:c + 1], ALU.max))
                        link(v.tensor_tensor(hc(mprev)[:, :, c + 1:c + 2], hc(mulast)[:, :, c:c + 1], hc(gtot)[:, :, c:c + 1], ALU.add))
                    link(v.tensor_tensor(mulast[:, :], mprev[:, :], mlast[:, :], ALU.max))
                    v.tensor_tensor(gt1[:, :], mprev[:, :], mulast[:, :], ALU.subtract)
                    link(v.tensor_tensor(gt2[:, :], acol[:, :], mulast[:, :], ALU.subtract))
                    link(v.tensor_tensor(ig[0:R, :], mprev[0:R, :], ident[0:R, 0:R], ALU.mult))
                    link(v.tensor_reduce(mprow[:, :], ig[0:R, :], AX, ALU.add))
                    a = 1
                    v.tensor_scalar(murow[:, :], cmax[:, a, 64:], mprow[:, 0:1], None, ALU.max).then_inc(s_gd, 1)
                if step == 4:
                    dve.wait_ge(s_gpe, 5)
                    v.tensor_tensor(mulast[:, :], bcum[:, :], X3[:, R:2 * R], ALU.add).then_inc(s_gd, 1)

            def scan(h, p):
                if p >= 2:
                    e = h * TT + p - 2
                    dve.wait_ge(s_hr, e + 1)
                    v.tensor_scalar(hs[:, :], hs[:, :], ccol[:, 4:5], None, ALU.mult).then_inc(s_hn, 1)
                if p < TT:
                    e = h * TT + p
                    dve.wait_ge(s_st, e + 1)
                    dve.wait_ge(s_mask, e + 1)
                    if e >= 1:
                        dve.wait_ge(s_b, e)
                    v.scalar_tensor_tensor(out=PT[:, :], in0=X1[:, 0:P], scalar=QSCALE, in1=wT[:, :], op0=ALU.mult,
                                           op1=ALU.mult).then_inc(s_pt, 1)
                    dve.wait_ge(s_wi, e + 1)
                    dve.wait_ge(s_qk, 4 * (h + 1))
                    v.scalar_tensor_tensor(out=qs[:, :], in0=QK[:, h % 2, 0, p * P:(p + 1) * P], scalar=QSCALE,
                                           in1=wi[:, :], op0=ALU.mult, op1=ALU.mult).then_inc(s_qs, 1)
                if 1 <= p <= TT:
                    e, c = h * TT + p - 1, p - 1
                    dve.wait_ge(s_b, e + 1)
                    if c < TT - 1:
                        if c == 0:
                            v.tensor_copy(Cst[:, :], X2[:, DV:2 * DV])
                            v.tensor_copy(nst[:, :], X3[:, 257:258]).then_inc(s_cst, 1)
                        else:
                            dve.wait_ge(s_cst, e)
                            v.scalar_tensor_tensor(out=Cst[:, :], in0=Cst[:, :], scalar=decay[:, e:e + 1],
                                                   in1=X2[:, DV:2 * DV], op0=ALU.mult, op1=ALU.add)
                            v.scalar_tensor_tensor(out=nst[:, :], in0=nst[:, :], scalar=decay[:, e:e + 1],
                                                   in1=X3[:, 257:258], op0=ALU.mult, op1=ALU.add).then_inc(s_cst, 1)
                    else:
                        v.tensor_copy(ccol[:, 5:6], X3[:, 256:257]).then_inc(s_cst, 1)
                    if e == 0:
                        dve.wait_ge(s_ga, 5)
                    link(v.tensor_scalar(ccol[:, 6:7], X3[:, 256:257], -1.0, emm[:, e:e + 1], ALU.mult, ALU.max))
                    link(v.tensor_tensor(ccol[:, 0:1], X3[:, 256:257], ccol[:, 6:7], ALU.max))
                    link(v.reciprocal(ccol[:, 1:2], ccol[:, 0:1]))
                    if e >= 1:
                        dve.wait_ge(s_tr, e)
                    v.tensor_scalar(hs[:, :], X2[:, 0:DV], ccol[:, 1:2], None, ALU.mult).then_inc(s_hs, 1)
                if p >= 2:
                    e, at = h * TT + p - 2, (p - 2) * P
                    dve.wait_ge(s_tr, e + 1)
                    dve.wait_ge(s_fa, FREED[FIRST[AT["o", h]] + 3][1])
                    if e >= 1:
                        dve.wait_ge(s_yl, e)
                    for kk in range(2):
                        gain = vcols[:, A_NORM + 2 * h + kk:A_NORM + 2 * h + kk + 1]
                        last = v.scalar_tensor_tensor(out=yf[:, kk, :], in0=X3[:, kk * P:(kk + 1) * P], scalar=gain,
                                                      in1=SG[:, kk, at:at + P], op0=ALU.mult, op1=ALU.mult)
                    last.then_inc(s_yf, 1)

            def memnorm(a, b):
                dve.wait_ge(s_gain, 32)
                for t in range(MT):
                    dve.wait_ge(s_rs, TT + t + 1)
                    v.scalar_tensor_tensor(out=mxs[:, t, :], in0=mxin[:, t, :], scalar=stat[:, t, 2:3], in1=gain_mem,
                                           op0=ALU.mult, op1=ALU.mult).then_inc(s_xs, 1)

            def memturn(a, b):
                for t in range(MT):
                    for q in range(2):
                        dve.wait_ge(s_xh, 2 * TT + 2 * t + q + 1)
                        at = slice(t * P, (t + 1) * P)
                        v.tensor_tensor(ML[:, 4 * q:4 * q + 4, at], PS[:, NB + 2 * t + q, :].rearrange("p (k s) -> p k s", k=4),
                                        MH[:, 4 * q:4 * q + 4, at].bitcast(F32), ALU.subtract).then_inc(s_xl, 1)

            def norm(which, half):
                c0 = NHALF * which + half
                dve.wait_ge(s_rt, c0 + 1)
                link(v.reciprocal(rstd[:, half, :], rstd2[:, half, :]))
                for k in range(KT):
                    c = KT * c0 + k
                    if c >= 2:
                        dve.wait_ge(s_xl, 2 * TT + 2 * MT + c - 1)
                    gain = (NORM_X, NORM_F)[which] + k
                    v.scalar_tensor_tensor(out=xnf[:, k % 2, :], in0=xT[:, k, half * HALF:(half + 1) * HALF],
                                           scalar=vcols[:, gain:gain + 1], in1=rstd[:, half, :], op0=ALU.mult,
                                           op1=ALU.mult).then_inc(s_xnf, 1)

            def attn(h, p):
                if 1 <= p <= 4:
                    e = 4 * h + p - 1
                    dve.wait_ge(s_ex, 2 * (e + 1))
                    link(v.reciprocal(acol8[:, e % 2, 6:8], acol8[:, e % 2, 4:6]))
                    for j in range(2):
                        last = v.tensor_scalar(ptok[:, e % 2, j * M:(j + 1) * M], ptok[:, e % 2, j * M:(j + 1) * M],
                                               acol8[:, e % 2, 6 + j:7 + j], None, ALU.mult)
                    last.then_inc(s_pn, 1)
                if p < 4:
                    e = 4 * h + p
                    dve.wait_ge(s_sc, e + 1)
                    link(v.tensor_reduce(acol8[:, e % 2, 0:2], PS[:, NB + e % 2, :].rearrange("p (j m) -> p j m", j=2), AX, ALU.max))
                    v.tensor_scalar(acol8[:, e % 2, 2:4], acol8[:, e % 2, 0:2], -XSCALE, None, ALU.mult).then_inc(s_mx, 1)
                if 1 <= p <= 4:
                    e = 4 * h + p - 1
                    dve.wait_ge(s_pt2, e + 1)
                    if h >= 1 and p == 1:
                        dve.wait_ge(s_pv, 4 * h)
                    if h == 0 and p == 1:
                        dve.wait_ge(s_xnf, 2 * KT)
                    v.tensor_copy(PA[:, :, (p - 1) * SW:p * SW], X2[:, :].rearrange("p (m s) -> p m s", m=MT)).then_inc(s_pa, 1)
                if p in (3, 5):
                    for dt in range(2):
                        c = 4 * h + 2 * (p // 2 - 1) + dt
                        dve.wait_ge(s_yh, H * TT + c + 1)
                        at = (p // 2 - 1) * HALF
                        v.tensor_tensor(YL[:, dt, at:at + HALF], X3[:, :], YH[:, dt, at:at + HALF].bitcast(F32),
                                        ALU.subtract).then_inc(s_yl, 1)

            todo = {"gates": gates, "scan": scan, "memnorm": memnorm, "memturn": memturn,
                    "square": lambda a, b: None, "norm": norm, "attn": attn}

            def add_residual(g, r, k=0):
                dve.wait_ge(s_mm, g + 1 + PER_LOOP["group"] * k)
                xt = xT[:, r % KT, (r // KT) * HALF:(r // KT + 1) * HALF]
                v.tensor_tensor(xt, PS[:, g % NB, :], xt, ALU.add).then_inc(s_fd, 1)

            def evac(n, r):
                kind, h = STRIPS[n]
                g = FIRST[n] + r
                if kind == "qk":
                    c, a, half = 4 * h + r, acc[:, r % 2, :], r // 2
                    bank = PS[:, g % NB, :]
                    tap = lambda j: vcols[:, CONV + KT * j + (r % 2) * H + h:CONV + KT * j + (r % 2) * H + h + 1]
                    dve.wait_ge(s_mm, g + 1)
                    if c >= 2:
                        dve.wait_ge(s_qk, c - 1)
                    link(v.tensor_scalar(a, bank, tap(TAPS - 1), None, ALU.mult))
                    for j in range(TAPS - 2, -1, -1):
                        lag = TAPS - 1 - j
                        ins = v.scalar_tensor_tensor(out=a[:, lag:], in0=bank[:, 0:HALF - lag], scalar=tap(j),
                                                     in1=a[:, lag:], op0=ALU.mult, op1=ALU.add)
                        if half:
                            link(ins)
                            ins = v.scalar_tensor_tensor(out=a[:, 0:lag], in0=halo[:, r % 2, TAPS - 1 - lag:], scalar=tap(j),
                                                         in1=a[:, 0:lag], op0=ALU.mult, op1=ALU.add)
                        if j:
                            link(ins)
                    ins.then_inc(s_conv, 1)
                    dve.wait_ge(s_conv, c + 1)
                    v.tensor_copy(halo[:, r % 2, :], bank[:, HALF - TAPS + 1:]).then_inc(s_fd, 1)
                elif kind not in BY_ACT:
                    add_residual(g, r)

            for t in range(TT):
                if t == 0:
                    dve.wait_ge(s_gain, 16)
                dve.wait_ge(s_rs, t + 1)
                if t >= 2:
                    dve.wait_ge(s_turn, t - 1)
                v.scalar_tensor_tensor(out=xs[:, t % 2, :], in0=xin[:, t % 2, :], scalar=stat[:, t, 2:3], in1=gain_mix,
                                       op0=ALU.mult, op1=ALU.mult).then_inc(s_xs, 1)
                if t >= 1:
                    turned_dve(v, dve, t - 1)
                if t == 3:
                    dve.wait_ge(s_vturn, 1)
                    v.tensor_copy(vcols[:, :], X3[:, 0:56]).then_inc(s_vc, 1)
                    dve.wait_ge(s_wg, 16)
                    link(v.tensor_copy(wgh[:, :, :], wg_raw))
                    v.tensor_tensor(wgl[:, :, :], wg_raw, wgh[:, :, :].bitcast(F32), ALU.subtract).then_inc(s_wgs, 1)
            turned_dve(v, dve, TT - 1)
            dve.wait_ge(s_vc, 1)
            for n in range(NF):
                for r in [*range(NGROUPS[STRIPS[n][0]])]:
                    run_parts(n, r, todo)
                    evac(n, r)
                run_parts(n, "end", todo)

            def up_evac(n, j, i=None):
                k = 0 if i is None else i
                for r in range(4):
                    g = FIRST[n] + r
                    dve.wait_ge(s_mm, g + 1 + PER_LOOP["group"] * k)
                    dve.wait_ge(s_fa, FREED[FIRST[n] - (4 if j == 0 else 20) + r][1] + PER_LOOP["act"] * k)
                    if j >= 1 or r >= 2:
                        dve.wait_ge(s_yl, Y_FFN + 4 * j + r - 1 + 8 * k)
                    ins = v.tensor_tensor(acc[:, r % 2, :], PS[:, g % NB, :],
                                          SG[:, r % 2, (r // 2) * HALF:(r // 2 + 1) * HALF], ALU.mult)
                    ins.then_inc(s_hf, 1)

            def down_evac(n, i=None):
                for r in range(16):
                    add_residual(FIRST[n] + r, r, 0 if i is None else i)

            up_evac(NF + 1, 0)
            with dve.Fori(0, NJ // 2) as i:
                for u in range(2):
                    n = NF + 2 + 3 * u
                    down_evac(n + 1, i)
                    up_evac(n + 2, 1 + u, i)
            down_evac(len(STRIPS) - 1)
            dve.wait_ge(s_gain, 48)
            for t in range(TT):
                c = TT + MT + t + 1
                dve.wait_ge(s_rs, c)
                if t >= 2:
                    dve.wait_ge(s_out[t % 2], 16 * (t // 2))
                v.scalar_tensor_tensor(out=fout[:, t % 2, :],
                                       in0=PS[:, 2 * (t % 4):2 * (t % 4) + 2, :].rearrange("p a s -> p (a s)"),
                                       scalar=stat[:, t, 2:3], in1=gain_out, op0=ALU.mult, op1=ALU.mult).then_inc(s_xs, 1)

        @block.tensor
        def _(pe):
            mm = nc.tensor.matmul

            def wait_strip(n, k=0):
                pe.wait_ge(s_whi, n + 1 + PER_LOOP["strip"] * k)
                pe.wait_ge(s_wlo, n + 1 + PER_LOOP["strip"] * k)

            def wait_bank(g, k=0):
                if g >= NB:
                    who, count = FREED[g - NB]
                    pe.wait_ge({"act": s_fa, "dve": s_fd, "up": s_hf}[who], count + PER_LOOP[who] * k)

            def product(dst, tiles):
                for k, ((wh, wl), (xh, xl)) in enumerate(tiles):
                    mm(dst, wh, xh, start=(k == 0), stop=False)
                    mm(dst, wh, xl, start=False, stop=False)
                    last = mm(dst, wl, xh, start=False, stop=(k == len(tiles) - 1))
                return last

            def col(n, k, nt, width=P):
                at = k * SW + nt * width
                return WH[:, n % 2, at:at + width], WL[:, n % 2, at:at + width]

            def rowt(n, kk, ft):
                at = kk * D + ft * P
                return WH[:, n % 2, at:at + P], WL[:, n % 2, at:at + P]

            def xpart(k, at, width):
                return XH[:, k, at:at + width], XL[:, k, at:at + width]

            def mpart(k, at, width):
                return MH[:, k, at:at + width], ML[:, k, at:at + width]

            def group(n, r, k=0):
                kind, h = STRIPS[n]
                g = FIRST[n] + r
                bank = PS[:, g % NB, :]
                wait_bank(g, k)
                if kind in ("wo", "xo", "down"):
                    at = (r // KT) * HALF
                    last = product(bank, [(rowt(n, kk, r % KT), (YH[:, kk, at:at + HALF], YL[:, kk, at:at + HALF]))
                                          for kk in range(2)])
                elif kind == "v":
                    for t in range(2):
                        at = (2 * r + t) * P
                        last = product(bank[:, t * DV:(t + 1) * DV], [(xpart(kk, at, P), col(n, kk, 0, SW)) for kk in range(KT)])
                elif kind == "mv":
                    for t in range(2):
                        last = product(bank[:, t * DV:(t + 1) * DV], [(mpart(kk, t * P, P), col(n, kk, 0, SW)) for kk in range(KT)])
                elif kind == "mk":
                    for t in range(2):
                        last = product(bank[:, t * M:(t + 1) * M], [(col(n, kk, t), mpart(kk, 0, M)) for kk in range(KT)])
                else:
                    at = (r // 2) * HALF
                    last = product(bank, [(col(n, kk, r % 2), xpart(kk, at, HALF)) for kk in range(KT)])
                last.then_inc(s_mm, 1)
                return last

            def gates(step, b):
                if step == 0:
                    pe.wait_ge(s_wgs, 1)
                    pe.wait_ge(s_xh, 2 * TT)
                    pe.wait_ge(s_xl, 2 * TT)
                    for t in range(TT):
                        last = product(X0[:, t * 2 * H:(t + 1) * 2 * H],
                                       [(xpart(kk, t * P, P), (wgh[:, kk, :], wgl[:, kk, :])) for kk in range(KT)])
                    last.then_inc(s_gpe, 1)
                if step == 1:
                    pe.wait_ge(s_gd, 2)
                    mm(X1[:, 0:R], tri, lf[:, :], start=True, stop=True)
                    mm(X1[:, R:2 * R], ones[:, :], lf[:, :], start=True, stop=True).then_inc(s_gpe, 1)
                if step == 2:
                    pe.wait_ge(s_gd, 3)
                    nc.tensor.transpose(X2[0:R, 0:P], acol[:, :], ident[:, :]).then_inc(s_gpe, 1)
                if step == 3:
                    pe.wait_ge(s_gd, 4)
                    mm(X3[:, 0:R], ones[0:R, :], gt1[0:R, :], start=True, stop=True).then_inc(s_gpe, 1)
                if step == 4:
                    pe.wait_ge(s_gd, 5)
                    nc.tensor.transpose(X3[:, R:2 * R], murow[:, :], ident[0:R, 0:R]).then_inc(s_gpe, 1)

            def scan(h, p):
                if p < TT:
                    e, at, c = h * TT + p, slice(p * P, (p + 1) * P), p
                    if e >= 1:
                        pe.wait_ge(s_ks, e)
                        pe.wait_ge(s_pt, e)
                    if e == 0:
                        pe.wait_ge(s_gd, 6)
                    if p == 0:
                        pe.wait_ge(s_qk, 4 * (h + 1))
                    k_t = QK[:, h % 2, 1, at]
                    mm(X0[:, 0:P], ident[0:R, e:e + 1].to_broadcast([R, P]), murow[:, :], start=True, stop=True)
                    nc.tensor.transpose(X0[:, P:2 * P], k_t, ident[:, :]).then_inc(s_mu, 1)
                    mm(X1[:, 0:P], k_t, QK[:, h % 2, 0, at], start=True, stop=True).then_inc(s_st, 1)
                if p >= 2:
                    e = h * TT + p - 2
                    pe.wait_ge(s_hn, e + 1)
                    if e >= 1:
                        pe.wait_ge(s_yf, e)
                    for kk in range(2):
                        last = nc.tensor.transpose(X3[:, kk * P:(kk + 1) * P], hs[:, kk * P:(kk + 1) * P], ident[:, :])
                    last.then_inc(s_tr, 1)
                if 1 <= p <= TT:
                    e, c = h * TT + p - 1, p - 1
                    pe.wait_ge(s_pt, e + 1)
                    pe.wait_ge(s_qs, e + 1)
                    pe.wait_ge(s_ks, e + 1)
                    if e >= 1:
                        pe.wait_ge(s_cst, e)
                        pe.wait_ge(s_hs, e)
                    if c == 0:
                        pe.wait_ge(s_fa, FREED[FIRST[AT["v", h]] + 3][1])
                        if h >= 1:
                            pe.wait_ge(s_yf, h * TT)
                    vc, one = VV[:, h % 2, c, :], ones[:, 0:1]
                    mm(X2[:, 0:DV], PT[:, :], vc, start=True, stop=(c == 0))
                    if c:
                        mm(X2[:, 0:DV], qs[:, :], Cst[:, :], start=False, stop=True)
                    mm(X3[:, 256:257], PT[:, :], one, start=True, stop=(c == 0))
                    if c:
                        last = mm(X3[:, 256:257], qs[:, :], nst[:, :], start=False, stop=True)
                    if c < TT - 1:
                        mm(X2[:, DV:2 * DV], ks[:, :], vc, start=True, stop=True)
                        last = mm(X3[:, 257:258], ks[:, :], one, start=True, stop=True)
                    last.then_inc(s_b, 1)

            def memturn(a, b):
                for t in range(MT):
                    pe.wait_ge(s_xs, TT + t + 1)
                    if t == 0:
                        pe.wait_ge(s_yf, TT * (H - 1))
                    for q in range(KT):
                        last = nc.tensor.transpose(PS[:, NB + 2 * t + q // 4, (q % 4) * P:(q % 4 + 1) * P],
                                                   mxs[:, t, q * P:(q + 1) * P], ident[:, :])
                    last.then_inc(s_turn, 1)

            def square(which, half):
                for k in range(KT):
                    c = KT * (NHALF * which + half) + k
                    pe.wait_ge(s_sqn, c + 1)
                    if which == 0 and half == 0 and k == 0:
                        pe.wait_ge(s_ks, H * TT)
                        pe.wait_ge(s_pt, H * TT)
                    if which == 1 and half == 0 and k == 0:
                        pe.wait_ge(s_ex, 8 * H)
                    mm(PS[:, NB + half, :], ones[:, :], sqb[:, k % 2, :], start=(k == 0), stop=(k == KT - 1)).then_inc(s_ssq, 1)

            def attn(h, p):
                if p < 4:
                    e = 4 * h + p
                    if e >= 2:
                        pe.wait_ge(s_ex, 2 * (e - 1))
                    else:
                        pe.wait_ge(s_rt, 2)
                    if p == 0:
                        pe.wait_ge(s_fa, FREED[FIRST[AT["q", h]] + 3][1])
                    for j in range(2):
                        at = slice((2 * p + j) * P, (2 * p + j + 1) * P)
                        for kk in range(2):
                            last = mm(PS[:, NB + e % 2, j * M:(j + 1) * M], QH[h % 2][:, kk, at], KM[:, 2 * h + kk, :],
                                      start=(kk == 0), stop=(kk == 1))
                    last.then_inc(s_sc, 1)
                if 1 <= p <= 4:
                    e = 4 * h + p - 1
                    pe.wait_ge(s_pn, e + 1)
                    if e >= 1:
                        pe.wait_ge(s_pa, e)
                    for j in range(2):
                        for m in range(MT):
                            last = nc.tensor.transpose(X2[:, m * SW + j * P:m * SW + (j + 1) * P],
                                                       ptok[:, e % 2, j * M + m * P:j * M + (m + 1) * P], ident[:, :])
                    last.then_inc(s_pt2, 1)
                if p in (3, 5):
                    half = p // 2 - 1
                    pe.wait_ge(s_pa, 4 * h + 2 * half + 2)
                    for dt in range(2):
                        c = 4 * h + 2 * half + dt
                        if c == 0:
                            pe.wait_ge(s_yf, H * TT)
                        pe.wait_ge(s_yl, H * TT + c)
                        for m in range(MT):
                            last = mm(X3[:, :], VM[:, m, h * DV + dt * P:h * DV + (dt + 1) * P],
                                      PA[:, m, half * HALF:(half + 1) * HALF], start=(m == 0), stop=(m == MT - 1))
                        last.then_inc(s_pv, 1)

            todo = {"gates": gates, "scan": scan, "memnorm": lambda a, b: None, "memturn": memturn, "square": square,
                    "norm": lambda a, b: None, "attn": attn}

            pe.wait_ge(s_const, 8)
            for t in range(TT):
                pe.wait_ge(s_xin[t % 2], 16 * (t // 2 + 1))
                if t >= 2:
                    pe.wait_ge(s_xt, t - 1)
                    pe.wait_ge(s_xl, 2 * (t - 1))
                if t == 3:
                    pe.wait_ge(s_vc, 1)
                for q in range(KT):
                    nc.tensor.transpose(PS[:, 4 * (t % 2) + q // 4, (q % 4) * P:(q % 4 + 1) * P],
                                        xin[:, t % 2, q * P:(q + 1) * P], ident[:, :])
                pe.wait_ge(s_xs, t + 1)
                for q in range(KT):
                    last = nc.tensor.transpose(PS[:, 4 * (t % 2) + 2 + q // 4, (q % 4) * P:(q % 4 + 1) * P],
                                               xs[:, t % 2, q * P:(q + 1) * P], ident[:, :])
                last.then_inc(s_turn, 1)
                if t == 2:
                    pe.wait_ge(s_vec, 64)
                    pe.wait_ge(s_xl, 4)
                    nc.tensor.transpose(X3[:, 0:56], vrows, ident[0:56, 0:56]).then_inc(s_vturn, 1)
            pe.wait_ge(s_xl, 2 * TT)
            pe.wait_ge(s_xh, 2 * TT)
            pe.wait_ge(s_xt, TT)

            for n in range(NF):
                kind, h = STRIPS[n]
                for r in range(NGROUPS[kind]):
                    run_parts(n, r, todo)
                    if r == 0:
                        wait_strip(n)
                        if kind == "mk" and h == 0:
                            pe.wait_ge(s_xl, 2 * TT + 2 * MT)
                        if kind == "wo":
                            pe.wait_ge(s_yl, TT * (h + 1))
                        if kind == "xo":
                            pe.wait_ge(s_yl, H * TT + 4 * (h + 1))
                    if kind == "q" and h == 0 and r % 2 == 0:
                        pe.wait_ge(s_xl, 2 * TT + 2 * MT + KT * (r // 2 + 1))
                    group(n, r)
                run_parts(n, "end", todo)

            def ffn_strip(n, i=None, lo=None):
                k = 0 if i is None else i
                wait_strip(n, k)
                if lo is not None:
                    pe.wait_ge(s_yl, lo + 8 * k)
                for r in range(NGROUPS[STRIPS[n][0]]):
                    if n == NF and r % 2 == 0:
                        pe.wait_ge(s_xl, 2 * TT + 2 * MT + 2 * KT + KT * (r // 2 + 1))
                    group(n, r, k)

            ffn_strip(NF)
            ffn_strip(NF + 1)
            with pe.Fori(0, NJ // 2) as i:
                for u in range(2):
                    n = NF + 2 + 3 * u
                    ffn_strip(n, i)
                    ffn_strip(n + 1, i, lo=Y_FFN + 4 * (u + 1))
                    ffn_strip(n + 2, i)
            ffn_strip(len(STRIPS) - 1, lo=Y_FFN + 4 * NJ)

            for t in range(TT):
                if t == 0:
                    pe.wait_ge(s_fd, FREED[-1][1])
                if t >= 4:
                    pe.wait_ge(s_xs, TT + MT + t - 3)
                for q in range(KT):
                    last = nc.tensor.transpose(PS[:, 2 * (t % 4) + q // 4, (q % 4) * P:(q % 4 + 1) * P],
                                               xT[:, q, t * P:(t + 1) * P], ident[:, :])
                last.then_inc(s_turn, 1)


_INS = ["x", "mem", "norm_mix", "norm_x", "norm_ffn", "norm_mem", "norm_final", "a_w_in", "a_conv_w", "a_gate_b",
        "a_norm", "a_w_out", "x_w_q", "x_w_kv", "x_w_o", "f_w_gate", "f_w_up", "f_w_down"]


def kernel(**inputs):
    import numpy as _np
    import concourse.bacc as _bacc
    from concourse import mybir as _mybir
    from concourse.bass_utils import run_bass_kernel_spmd as _run

    nc = _bacc.Bacc("TRN2", target_bir_lowering=False, num_devices=1)
    arrays, args = {}, []
    for name in _INS:
        a = _np.ascontiguousarray(inputs[name])
        arrays[f"in_{name}_dram"] = a
        args.append(nc.dram_tensor(f"in_{name}_dram", a.shape, _mybir.dt.from_np(a.dtype), kind="ExternalInput").ap())
    args.append(nc.dram_tensor("out_0_dram", inputs["x"].shape, _mybir.dt.float32, kind="ExternalOutput").ap())
    build_block(nc, *args)
    r = _run(nc, [arrays], core_ids=[0])
    return r.results[0]["out_0_dram"]
```

```python
import concourse.bass as bass
from concourse import mybir
from contextlib import ExitStack

F32, F32R = mybir.dt.float32, mybir.dt.float32r
ALU = mybir.AluOpType
ACT = mybir.ActivationFunctionType
AX = mybir.AxisListType.X

P = 128
EPS = 1e-6
LOWEST = -3.0e38


def build_block(nc, x, mem, norm_mix, norm_x, norm_ffn, norm_mem, norm_final, a_w_in, a_conv_w, a_gate_b,
                a_norm, a_w_out, x_w_q, x_w_kv, x_w_o, f_w_gate, f_w_up, f_w_down, out):
    S, D = x.shape[1], x.shape[2]
    M = mem.shape[1]
    KT = D // P
    TT = S // P
    MT = M // P
    HALF = 512
    NHALF = S // HALF
    H = a_gate_b.shape[1] // 2
    DK = a_conv_w.shape[2] // (2 * H)
    DV = D // H
    TAPS = a_conv_w.shape[1]
    SW = 2 * P
    F = f_w_gate.shape[2]
    NJ = F // SW
    QSCALE = float(DK) ** -0.5 / 4
    XSCALE = float(DV) ** -0.5
    V0, O0, G0 = 2 * H * DK, 2 * H * DK + H * DV, 2 * H * DK + 2 * H * DV
    R = H * TT
    assert DK == P and DV == SW and NJ % 2 == 1 and MT == 2 and KT == 8 and TT == 8 and H == 4

    STRIPS = [("qk", 0), ("v", 0), ("o", 0)]
    for h in range(1, H):
        STRIPS += [("qk", h), ("v", h), ("o", h), ("wo", h - 1)]
    STRIPS += [("mk", j) for j in range(H)] + [("mv", j) for j in range(H)]
    STRIPS += [("wo", H - 1), ("q", 0)]
    for h in range(1, H):
        STRIPS += [("q", h), ("xo", h - 1)]
    STRIPS += [("xo", H - 1)]
    NF = len(STRIPS)
    STRIPS += [("gate", 0), ("up", 0)]
    for j in range(1, NJ):
        STRIPS += [("gate", j), ("down", j - 1), ("up", j)]
    STRIPS += [("down", NJ - 1)]
    AT = {s: n for n, s in enumerate(STRIPS)}
    assert NF % 2 == 0
    NGROUPS = {"qk": 4, "v": 4, "o": 4, "wo": 16, "mk": 1, "mv": 1, "q": 4, "xo": 16,
               "gate": 4, "up": 4, "down": 16}
    BY_ACT = {"v", "o", "mk", "mv", "q", "gate"}
    FIRST, FREED, took, g = {}, [], {"act": 0, "dve": 0, "up": 0}, 0
    for n, (kind, _) in enumerate(STRIPS):
        FIRST[n] = g
        for _ in range(NGROUPS[kind]):
            who = "act" if kind in BY_ACT else "up" if kind == "up" else "dve"
            took[who] += 1
            FREED.append((who, took[who]))
            g += 1
    used = lambda n: FIRST[n] + NGROUPS[STRIPS[n][0]]
    NB = 4
    DMAS = []
    for kind, _ in STRIPS:
        DMAS.append((DMAS[-1] if DMAS else 0) + (2 if kind == "qk" else 1))
    PER_LOOP = {"strip": 6, "group": 48, "act": 8, "dve": 32, "up": 8}

    PARTS = {}

    def part(kind, h, r, what):
        PARTS.setdefault((AT[kind, h], r), []).append(what)

    for step, (kind, r) in enumerate([("v", 0), ("v", 1), ("v", 3), ("o", 0), ("o", 1), ("o", 3)]):
        part(kind, 0, r, ("gates", step, None))
    NP = TT + 3
    for h in range(1, H):
        for p in range(NP):
            kind, r = [("qk", p), ("v", p - 4), ("o", p - 8)][p // 4]
            part(kind, h, r, ("scan", h - 1, p))
    part("wo", H - 2, 0, ("memnorm", 0, None))
    part("wo", H - 2, 4, ("memturn", 0, None))
    part("wo", H - 2, 8, ("scan", H - 1, 0))
    part("wo", H - 2, 12, ("scan", H - 1, 1))
    for p in range(2, 10):
        part("mk" if p < 6 else "mv", (p - 2) % H, 0, ("scan", H - 1, p))
    part("mv", H - 1, "end", ("scan", H - 1, 10))
    for which, kind, nxt in ((0, "wo", ("q", 0)), (1, "xo", ("gate", 0))):
        part(kind, H - 1, 12, ("sumsq", which, 0))
        part(kind, H - 1, "end", ("norm", which, 0))
        part(*nxt, 1, ("sumsq", which, 1))
        part(*nxt, 1, ("norm", which, 1))
    for h in range(1, H):
        for p in range(4):
            part("q", h, p, ("attn", h - 1, p))
    for p in range(3):
        part("xo", H - 2, 4 + 4 * p, ("attn", H - 1, p))
    part("xo", H - 2, "end", ("attn", H - 1, 3))
    for h in range(H):
        part("xo", h, 0, ("attn", h, 4))
        part("xo", h, 3, ("attn", h, 5))

    def run_parts(n, r, todo):
        for what, a, b in PARTS.get((n, r), []):
            todo[what](a, b)

    x_t = x[0].rearrange("(t p) d -> t p d", p=P)
    mem_t = mem[0].rearrange("(t p) d -> t p d", p=P)
    out_t = out[0].rearrange("(t p) d -> t p d", p=P)

    def cols(w, at, width=SW):
        return w[0, :, at:at + width].rearrange("(k p) n -> p k n", p=P)

    def rows(w, at):
        return w[0, at:at + SW, :].rearrange("(k p) n -> p k n", p=P)

    ctx = ExitStack()
    with ctx:
        def sb(name, shape, dt=F32):
            return ctx.enter_context(nc.sbuf_tensor(name, shape, dt))

        def sem(name):
            return ctx.enter_context(nc.semaphore(name))

        xT = sb("xT", [P, KT, S])
        XH = sb("XH", [P, KT, S], F32R)
        XL = sb("XL", [P, KT, S], F32R)
        raw = sb("raw", [P, KT * SW])
        WH = sb("WH", [P, 2, KT * SW], F32R)
        WL = sb("WL", [P, 2, KT * SW], F32R)
        QK = sb("QK", [P, 2, 2, S])
        VV = sb("VV", [P, 2, TT, DV + 1])
        SG = sb("SG", [P, 2, S])
        YH = sb("YH", [P, 2, S], F32R)
        YL = sb("YL", [P, 2, S], F32R)
        acc = sb("acc", [P, 2, HALF])
        ident = sb("ident", [P, P])
        ones = sb("ones", [P, P])
        vcols = sb("vcols", [P, 56])
        NORM_X, NORM_F, A_NORM, CONV = 0, KT, 2 * KT, 3 * KT
        halo = sb("halo", [P, 2, TAPS - 1])
        gbias = sb("gbias", [P, 2 * H])
        half_neg = sb("half_neg", [P, 1])
        stat = sb("stat", [P, TT, 3])
        ig = sb("ig", [P, R])
        lf = sb("lf", [P, R])
        gt1 = sb("gt1", [P, R])
        gt2 = sb("gt2", [P, R])
        bcum = sb("bcum", [P, R])
        gtot = sb("gtot", [P, R])
        acol = sb("acol", [P, R])
        mlast = sb("mlast", [P, R])
        mprev = sb("mprev", [P, R])
        mulast = sb("mulast", [P, R])
        decay = sb("decay", [P, R])
        wa = sb("wa", [P, R])
        emm = sb("emm", [P, R])
        murow = sb("murow", [R, P])
        mprow = sb("mprow", [R, 1])
        wT = sb("wT", [P, P])
        wi = sb("wi", [P, P])
        PT = sb("PT", [P, P])
        qs = sb("qs", [P, P])
        ks = sb("ks", [P, DK])
        Cst = sb("Cst", [P, DV + 1])
        hs = sb("hs", [P, 2, DV])
        hsj = sb("hsj", [P, DV])
        nstat = sb("nstat", [P, 4 * HALF // P])
        yf = sb("yf", [P, 2, P])
        ccol = sb("ccol", [P, 2, 6])
        acol8 = sb("acol8", [P, 2, 8])
        PS = ctx.enter_context(nc.psum_tensor("PS", [P, 8, HALF], F32))
        X0, X1, X2, X3 = (PS[:, NB + i, :] for i in range(4))

        xin = VV[:, 0].rearrange("p t d -> p (t d)")[:, 0:2 * S].rearrange("p (a d) -> p a d", a=2)
        xs = VV[:, 1].rearrange("p t d -> p (t d)")[:, 0:2 * S].rearrange("p (a d) -> p a d", a=2)
        mxin = QK[:, 0]
        mxs = mxin
        mspare = VV[:, 0].rearrange("p t d -> p (t d)")[:, 0:2 * S].rearrange("p (a d) -> p a d", a=2)
        gain_mem, mjunk = mspare[:, 0, :], mspare[:, 1, :]
        gain_mix = SG[:, 0, :]
        gain_out = SG[:, 0, :]
        tri = SG[:, 1, 0:P]
        cmax = SG[0:R, 1, HALF:HALF + 2 * (64 + P)].rearrange("r (a t) -> r a t", a=2)
        vrows = QK[0:56, 0, 0, 0:P]
        wg_raw = QK[:, 0, 1, 0:KT * 2 * H].rearrange("p (k g) -> p k g", k=KT)
        MH = XH[:, 0:2, :].rearrange("p k s -> p (k s)").rearrange("p (k m) -> p k m", k=KT)
        ML = XL[:, 0:2, :].rearrange("p k s -> p (k s)").rearrange("p (k m) -> p k m", k=KT)
        KM = QK[:, 0].rearrange("p a s -> p (a s)").rearrange("p (k m) -> p k m", k=KT)
        VM = VV[:, 0].rearrange("p t d -> p (t d)")[:, 0:2 * S].rearrange("p (a d) -> p a d", a=MT)
        QH = [VV[:, 1].rearrange("p t d -> p (t d)")[:, 0:2 * S].rearrange("p (a s) -> p a s", a=2), SG[:, :, :]]
        PA = QK[:, 1].rearrange("p a s -> p (a s)").rearrange("p (m s) -> p m s", m=MT)
        ptok = acc[:, :, :]
        sqb = SG[:, 0, :].rearrange("p (a s) -> p a s", a=2)
        xnf = SG[:, 1, :].rearrange("p (a s) -> p a s", a=2)
        rdiag = QK[:, 1, 0, 0:HALF].rearrange("p (t s) -> p t s", t=HALF // P)
        sqsum = QK[:, 1, 1, :].rearrange("p (a s) -> p a s", a=NHALF)
        wgp = [t[:, 0, :].rearrange("p (k g) -> p k g", k=KT) for t in (YH, YL)]
        grow = VV[0:2 * H, 1].rearrange("p t d -> p (t d)")[:, 0:S]
        fout = VV[:, 0].rearrange("p t d -> p (t d)")[:, 0:2 * S].rearrange("p (a d) -> p a d", a=2)
        junk = QK[:, 1, 1, :]

        s_const = sem("s_const")
        s_vec = sem("s_vec")
        s_gain = sem("s_gain")
        s_wg = sem("s_wg")
        s_gb = sem("s_gb")
        s_xin = [sem(f"s_xin{i}") for i in range(2)]
        s_min = [sem(f"s_min{i}") for i in range(2)]
        s_sq = sem("s_sq")
        s_rs = sem("s_rs")
        s_ms = sem("s_ms")
        s_xs = sem("s_xs")
        s_turn = sem("s_turn")
        s_xt = sem("s_xt")
        s_xh = sem("s_xh")
        s_xl = sem("s_xl")
        s_vturn = sem("s_vturn")
        s_vc = sem("s_vc")
        s_wgs = sem("s_wgs")
        s_wdma = sem("s_wdma")
        s_whi = sem("s_whi")
        s_wlo = sem("s_wlo")
        s_mm = sem("s_mm")
        s_fa = sem("s_fa")
        s_fd = sem("s_fd")
        s_conv = sem("s_conv")
        s_qk = sem("s_qk")
        s_gpe = sem("s_gpe")
        s_gd = sem("s_gd")
        s_ga = sem("s_ga")
        s_ones = sem("s_ones")
        s_gr = sem("s_gr")
        s_xg = sem("s_xg")
        s_xta = sem("s_xta")
        s_ex1 = sem("s_ex1")
        s_sg = sem("s_sg")
        s_sacc = sem("s_sacc")
        s_mu = sem("s_mu")
        s_st = sem("s_st")
        s_wt = sem("s_wt")
        s_mask = sem("s_mask")
        s_wi = sem("s_wi")
        s_ks = sem("s_ks")
        s_pt = sem("s_pt")
        s_qs = sem("s_qs")
        s_b = sem("s_b")
        s_hs = sem("s_hs")
        s_cst = sem("s_cst")
        s_hsq = sem("s_hsq")
        s_hm = sem("s_hm")
        s_hr = sem("s_hr")
        s_hn = sem("s_hn")
        s_tr = sem("s_tr")
        s_yf = sem("s_yf")
        s_yh = sem("s_yh")
        s_yl = sem("s_yl")
        s_sc = sem("s_sc")
        s_mx = sem("s_mx")
        s_ex = sem("s_ex")
        s_pn = sem("s_pn")
        s_pt2 = sem("s_pt2")
        s_pa = sem("s_pa")
        s_pv = sem("s_pv")
        s_sqn = sem("s_sqn")
        s_ssq = sem("s_ssq")
        s_nm = sem("s_nm")
        s_ns = sem("s_ns")
        s_nr = sem("s_nr")
        s_rd = sem("s_rd")
        s_rt = sem("s_rt")
        s_xnf = sem("s_xnf")
        s_hf = sem("s_hf")
        s_out = [sem(f"s_out{i}") for i in range(2)]
        s_dve = sem("s_dve")

        Y_FFN = H * TT + H * 4

        block = ctx.enter_context(nc.Block())

        def out_banks(t):
            b = NB + 2 * (t % 2) if t < 4 else 2 * (t - 4)
            return PS[:, b:b + 2, :].rearrange("p a s -> p (a s)")

        def turned(sc, act, t):
            act.wait_ge(s_turn, t + 1)
            at = slice(t * P, (t + 1) * P)
            sc.activation(xT[:, 0:4, at], PS[:, 4 * (t % 2), :].rearrange("p (k s) -> p k s", k=4), ACT.Copy).then_inc(s_xta, 1)
            for q in range(2):
                sc.activation(XH[:, 4 * q:4 * q + 4, at],
                              PS[:, 4 * (t % 2) + 2 + q, :].rearrange("p (k s) -> p k s", k=4), ACT.Copy).then_inc(s_xh, 1)

        def turned_dve(v, dve, t):
            dve.wait_ge(s_turn, t + 1)
            at = slice(t * P, (t + 1) * P)
            v.tensor_copy(xT[:, 4:8, at], PS[:, 4 * (t % 2) + 1, :].rearrange("p (k s) -> p k s", k=4)).then_inc(s_xt, 1)
            for q in range(2):
                dve.wait_ge(s_xh, 2 * t + q + 1)
                v.tensor_tensor(XL[:, 4 * q:4 * q + 4, at], PS[:, 4 * (t % 2) + 2 + q, :].rearrange("p (k s) -> p k s", k=4),
                                XH[:, 4 * q:4 * q + 4, at].bitcast(F32), ALU.subtract).then_inc(s_xl, 1)

        def strip_src(kind, h):
            c3 = raw[:, :].rearrange("p (k n) -> p k n", k=KT)
            r3 = raw[:, :].rearrange("p (k n) -> p k n", k=2)
            if kind == "qk":
                return [(c3[:, :, 0:DK], cols(a_w_in, h * DK, DK)),
                        (c3[:, :, DK:SW], cols(a_w_in, (H + h) * DK, DK))]
            if kind in ("wo", "xo"):
                return [(r3, rows(a_w_out if kind == "wo" else x_w_o, h * SW))]
            w, at = {"v": (a_w_in, V0), "o": (a_w_in, O0), "mk": (x_w_kv, 0), "mv": (x_w_kv, D),
                     "q": (x_w_q, 0)}[kind]
            return [(c3, cols(w, at + h * SW))]

        @block.sync
        def _(sp):
            def load_strip(n):
                if n >= 1:
                    sp.wait_ge(s_wlo, n)
                for dst, src in strip_src(*STRIPS[n]):
                    sp.dma_start(dst, src).then_inc(s_wdma, 16)

            sp.dma_start(gain_mix, norm_mix[0:1, :].to_broadcast([P, D])).then_inc(s_gain, 16)
            for t in range(TT):
                if t >= 2:
                    sp.wait_ge(s_turn, t - 1)
                    sp.wait_ge(s_xg, t - 1)
                    sp.wait_ge(s_sq, t - 1)
                sp.dma_start(xin[:, t % 2, :], x_t[t]).then_inc(s_xin[t % 2], 16)
                if t == 1:
                    for v, at, n in ((norm_x, NORM_X, KT), (norm_ffn, NORM_F, KT), (a_norm, A_NORM, KT)):
                        sp.dma_start(vrows[at:at + n, :], v[0].rearrange("(k p) -> k p", p=P)).then_inc(s_vec, 16)
                    sp.dma_start(vrows[CONV:CONV + TAPS * KT, :],
                                 a_conv_w[0].rearrange("j (k p) -> (j k) p", p=P)).then_inc(s_vec, 16)
                    sp.dma_start(wg_raw, cols(a_w_in, G0, 2 * H)).then_inc(s_wg, 16)
                    sp.dma_start(gbias[:, :], a_gate_b[0:1, :].to_broadcast([P, 2 * H])).then_inc(s_gb, 16)
                    load_strip(0)
            for n in range(1, NF):
                if n == AT["wo", H - 2]:
                    sp.wait_ge(s_b, TT * (H - 1))
                    sp.dma_start(gain_mem, norm_mem.rearrange("(o d) -> o d", o=1).to_broadcast([P, D])).then_inc(s_gain, 16)
                    for t in range(MT):
                        sp.dma_start(mxin[:, t, :], mem_t[t]).then_inc(s_min[t], 16)
                load_strip(n)

            def load_ffn(n, w, j, is_rows, i=None):
                k = 0 if i is None else i
                sp.wait_ge(s_wlo, n + PER_LOOP["strip"] * k)
                at = (j + 2 * k) * SW
                if is_rows:
                    src = w[0, bass.ds(at, SW), :].rearrange("(k p) n -> p k n", p=P)
                    dst = raw[:, :].rearrange("p (k n) -> p k n", k=2)
                else:
                    src = w[0, :, bass.ds(at, SW)].rearrange("(k p) n -> p k n", p=P)
                    dst = raw[:, :].rearrange("p (k n) -> p k n", k=KT)
                sp.dma_start(dst, src).then_inc(s_wdma, 16)

            load_ffn(NF, f_w_gate, 0, False)
            load_ffn(NF + 1, f_w_up, 0, False)
            with sp.Fori(0, NJ // 2) as i:
                for u in range(2):
                    n = NF + 2 + 3 * u
                    load_ffn(n, f_w_gate, 1 + u, False, i)
                    load_ffn(n + 1, f_w_down, u, True, i)
                    load_ffn(n + 2, f_w_up, 1 + u, False, i)
            load_ffn(len(STRIPS) - 1, f_w_down, NJ - 1, True)
            sp.wait_ge(s_hf, 4 * NJ)
            sp.dma_start(gain_out, norm_final.rearrange("(o d) -> o d", o=1).to_broadcast([P, D])).then_inc(s_gain, 16)
            for t in range(TT):
                sp.wait_ge(s_xs, TT + MT + t + 1)
                sp.dma_start(out_t[t], fout[:, t % 2, :]).then_inc(s_out[t % 2], 16)
            for t in range(2):
                sp.wait_ge(s_out[t], 16 * TT // 2)

        @block.gpsimd
        def _(pool):
            gp = nc.gpsimd
            gp.memset(ident[:, :], 0.0).then_inc(s_const, 1)
            gp.memset(ones[:, :], 1.0).then_inc(s_const, 1)
            gp.memset(tri, 1.0).then_inc(s_const, 1)
            gp.memset(half_neg[:, :], -0.5).then_inc(s_const, 1)
            gp.memset(nstat[:, 3 * HALF // P:], -0.5).then_inc(s_const, 1)
            gp.memset(cmax, LOWEST).then_inc(s_const, 1)
            pool.wait_ge(s_const, 6)
            gp.affine_select(out=ident[:, :], in_=ident[:, :], compare_op=ALU.not_equal, fill=1.0, base=0,
                             pattern=[[-1, P]], channel_multiplier=1).then_inc(s_const, 1)
            gp.affine_select(out=tri, in_=tri, compare_op=ALU.is_ge, fill=0.0, base=0,
                             pattern=[[1, P]], channel_multiplier=-1).then_inc(s_const, 1)

            def rms(t, src, mean, dst, count, width):
                pool.wait_ge(s_sq, count)
                gp.tensor_scalar(mean, src, 1.0 / width, EPS, ALU.mult, ALU.add).then_inc(s_ms, 1)
                pool.wait_ge(s_ms, count)
                gp.tensor_tensor(dst, mean, half_neg[:, :], ALU.pow).then_inc(s_rs, 1)

            def split_lo_half(n, u):
                pool.wait_ge(s_whi, n + 1)
                at = slice(u * KT * P, (u + 1) * KT * P)
                last = gp.tensor_tensor(WL[:, n % 2, at], raw[:, at], WH[:, n % 2, at].bitcast(F32), ALU.subtract)
                if u:
                    last.then_inc(s_wlo, 1)

            def split_lo(n, i=None):
                k = 0 if i is None else i
                pool.wait_ge(s_whi, n + 1 + PER_LOOP["strip"] * k)
                gp.tensor_tensor(WL[:, n % 2, :], raw[:, :], WH[:, n % 2, :].bitcast(F32),
                                 ALU.subtract).then_inc(s_wlo, 1)

            def scan(h, p):
                if p < TT:
                    e = h * TT + p
                    pool.wait_ge(s_wt, e + 1)
                    gp.affine_select(out=wT[:, :], in_=wT[:, :], compare_op=ALU.is_ge, fill=0.0, base=0,
                                     pattern=[[1, P]], channel_multiplier=-1).then_inc(s_mask, 1)
                if 1 <= p <= TT:
                    e = h * TT + p - 1
                    cc = ccol[:, e % 2, :]
                    pool.wait_ge(s_hsq, e + 1)
                    gp.tensor_scalar(cc[:, 3:4], cc[:, 2:3], 1.0 / DV, EPS, ALU.mult, ALU.add).then_inc(s_hm, 1)
                    pool.wait_ge(s_hm, e + 1)
                    if e >= 2:
                        pool.wait_ge(s_hn, e - 1)
                    gp.tensor_tensor(cc[:, 4:5], cc[:, 3:4], half_neg[:, :], ALU.pow).then_inc(s_hr, 1)
                if p >= 3:
                    e = h * TT + p - 3
                    pool.wait_ge(s_yh, e + 1)
                    at = (p - 3) * P
                    gp.tensor_tensor(YL[:, :, at:at + P], yf[:, :, :], YH[:, :, at:at + P].bitcast(F32),
                                     ALU.subtract).then_inc(s_yl, 1)

            def memnorm(a, b):
                for t in range(MT):
                    rms(t, stat[:, t, 0:1], stat[:, t, 1:2], stat[:, t, 2:3], TT + t + 1, D)

            def norm(which, half):
                c0, nt = NHALF * which + half, HALF // P
                pool.wait_ge(s_ns, c0 + 1)
                gp.tensor_scalar(nstat[:, nt:2 * nt], nstat[:, 0:nt], 1.0 / D, EPS, ALU.mult, ALU.add).then_inc(s_nm, 1)
                pool.wait_ge(s_nm, c0 + 1)
                if c0:
                    pool.wait_ge(s_rd, c0)
                gp.tensor_tensor(nstat[:, 2 * nt:3 * nt], nstat[:, nt:2 * nt], nstat[:, 3 * nt:], ALU.pow).then_inc(s_nr, 1)
                for k in range(KT):
                    c = KT * (NHALF * which + half) + k
                    pool.wait_ge(s_xh, 2 * TT + 2 * MT + c + 1)
                    at = half * HALF
                    gp.tensor_tensor(XL[:, k, at:at + HALF], xnf[:, k % 2, :],
                                     XH[:, k, at:at + HALF].bitcast(F32), ALU.subtract).then_inc(s_xl, 1)

            def add_squares(n, r):
                which, half, k = ("wo", "xo").index(STRIPS[n][0]), r // KT, r % KT
                c = KT * (NHALF * which + half) + k
                pool.wait_ge(s_sqn, c + 1)
                if k:
                    if k > 1:
                        pool.wait_ge(s_sacc, c - c // KT - 1)
                    gp.tensor_tensor(sqsum[:, half, :], sqsum[:, half, :], sqb[:, k % 2, :], ALU.add).then_inc(s_sacc, 1)

            todo = {"scan": scan, "memnorm": memnorm, "norm": norm}
            for what in ("gates", "memturn", "sumsq", "attn"):
                todo[what] = lambda a, b: None

            for t in range(TT):
                if t == 0:
                    pool.wait_ge(s_gain, 16)
                pool.wait_ge(s_xin[t % 2], 16 * (t // 2 + 1))
                if t >= 2:
                    pool.wait_ge(s_turn, t - 1)
                gp.tensor_tensor(xs[:, t % 2, :], xin[:, t % 2, :], gain_mix, ALU.mult).then_inc(s_xg, 1)
                rms(t, stat[:, t, 0:1], stat[:, t, 1:2], stat[:, t, 2:3], t + 1, D)
                if t == 3:
                    split_lo(0)
            for n in range(NF):
                kind, h = STRIPS[n]
                for r in range(NGROUPS[kind]):
                    run_parts(n, r, todo)
                    if NGROUPS[kind] == 1:
                        split_lo(n + 1)
                    elif r < 2:
                        split_lo_half(n + 1, r)
                    if kind in ("wo", "xo") and h == H - 1:
                        add_squares(n, r)
                run_parts(n, "end", todo)

            def ffn_lo(j, i=None):
                k = 0 if i is None else i
                for r in range(4):
                    c = 4 * j + r
                    pool.wait_ge(s_yh, Y_FFN + c + 1 + 8 * k)
                    nt, at = r % 2, (r // 2) * HALF
                    gp.tensor_tensor(YL[:, nt, at:at + HALF], acc[:, r % 2, :],
                                     YH[:, nt, at:at + HALF].bitcast(F32), ALU.subtract).then_inc(s_yl, 1)

            split_lo(NF + 1)
            norm(1, 1)
            split_lo(NF + 2)
            ffn_lo(0)
            with pool.Fori(0, NJ // 2) as i:
                for u in range(2):
                    n = NF + 2 + 3 * u
                    split_lo(n + 1, i)
                    split_lo(n + 2, i)
                    split_lo(n + 3, i)
                    ffn_lo(1 + u, i)
            for t in range(TT):
                rms(t, stat[:, t, 0:1], stat[:, t, 1:2], stat[:, t, 2:3], TT + MT + t + 1, D)

        @block.scalar
        def _(act):
            sc = nc.scalar

            def split_hi(n, i=None):
                k = 0 if i is None else i
                act.wait_ge(s_wdma, 16 * DMAS[n] + 16 * PER_LOOP["strip"] * k)
                if n >= 2:
                    act.wait_ge(s_mm, used(n - 2) + PER_LOOP["group"] * k)
                sc.activation(WH[:, n % 2, :], raw[:, :], ACT.Copy).then_inc(s_whi, 1)

            def square_tile(t, src, junk_out, count):
                if count > 1:
                    act.wait_ge(s_sq, count - 1)
                sc.activation(junk_out, src, ACT.Square, accum_out=stat[:, t, 0:1]).then_inc(s_sq, 1)

            def gates(step, b):
                if step == 1:
                    act.wait_ge(s_gd, 1)
                    sc.activation(gt1[:, :], gt2[:, :], ACT.Exp).then_inc(s_ga, 1)
                    act.wait_ge(s_ga, 1)
                    sc.activation(gt2[:, :], gt1[:, :], ACT.Ln, bias=1.0).then_inc(s_ga, 1)
                if step == 4:
                    act.wait_ge(s_gd, 5)
                    sc.activation(decay[:, :], gt1[:, :], ACT.Exp).then_inc(s_ga, 1)
                    sc.activation(wa[:, :], gt2[:, :], ACT.Exp).then_inc(s_ga, 1)
                if step == 5:
                    act.wait_ge(s_gd, 6)
                    sc.activation(emm[:, :], mulast[:, :], ACT.Exp, scale=-1.0).then_inc(s_ga, 1)

            def scan(h, p):
                if p < TT:
                    e = h * TT + p
                    if e == 0:
                        act.wait_ge(s_ga, 5)
                        act.wait_ge(s_gd, 6)
                    act.wait_ge(s_mu, e + 1)
                    if e >= 1:
                        act.wait_ge(s_pt, e)
                        act.wait_ge(s_qs, e)
                        act.wait_ge(s_b, e)
                    sc.activation(wT[:, :], X0[:, 0:P], ACT.Exp, scale=-1.0, bias=acol[:, e:e + 1]).then_inc(s_wt, 1)
                    sc.activation(wi[:, :], X0[:, 0:P], ACT.Exp, scale=-1.0, bias=mprev[:, e:e + 1]).then_inc(s_wi, 1)
                    sc.activation(ks[:, :], X0[:, P:2 * P], ACT.Copy, scale=wa[:, e:e + 1]).then_inc(s_ks, 1)
                if 1 <= p <= TT:
                    e = h * TT + p - 1
                    act.wait_ge(s_hs, e + 1)
                    if e >= 1:
                        act.wait_ge(s_hsq, e)
                    if e >= 2:
                        act.wait_ge(s_hm, e - 1)
                    sc.activation(hsj[:, :], hs[:, e % 2, :], ACT.Square, accum_out=ccol[:, e % 2, 2:3]).then_inc(s_hsq, 1)
                if p >= 3:
                    e = h * TT + p - 3
                    act.wait_ge(s_yf, e + 1)
                    if p == 3 and h >= 1:
                        act.wait_ge(s_mm, used(AT["wo", h - 1]))
                    at = (p - 3) * P
                    sc.activation(YH[:, :, at:at + P], yf[:, :, :], ACT.Copy).then_inc(s_yh, 1)

            def memnorm(a, b):
                for t in range(MT):
                    act.wait_ge(s_min[t], 16)
                    if t == 0:
                        act.wait_ge(s_b, TT * (H - 1))
                    square_tile(t, mxin[:, t, :], mjunk, TT + t + 1)

            def memturn(a, b):
                act.wait_ge(s_mm, used(AT["o", H - 1]))
                for t in range(MT):
                    act.wait_ge(s_turn, TT + t + 1)
                    for q in range(2):
                        sc.activation(MH[:, 4 * q:4 * q + 4, t * P:(t + 1) * P],
                                      PS[:, NB + 2 * t + q, :].rearrange("p (k s) -> p k s", k=4),
                                      ACT.Copy).then_inc(s_xh, 1)

            def square(n, r):
                which, half, k = ("wo", "xo").index(STRIPS[n][0]), r // KT, r % KT
                c = KT * (NHALF * which + half) + k
                act.wait_ge(s_fd, FREED[FIRST[n] + r][1])
                if r == 0 and which == 0:
                    act.wait_ge(s_yf, H * TT)
                if r == 0 and which == 1:
                    act.wait_ge(s_sc, H * 4)
                    act.wait_ge(s_pv, H * 4)
                if k >= 3:
                    act.wait_ge(s_sacc, c - c // KT - 2)
                if k in (1, 2) and c > KT:
                    act.wait_ge(s_sacc, (KT - 1) * (c // KT))
                sc.activation(sqb[:, k % 2, :] if k else sqsum[:, half, :], xT[:, k, half * HALF:(half + 1) * HALF],
                              ACT.Square).then_inc(s_sqn, 1)

            def norm(which, half):
                c0 = NHALF * which + half
                if half == 0:
                    act.wait_ge(s_mm, used(AT["mv", H - 1] if which == 0 else AT["q", H - 1]))
                for k in range(KT):
                    act.wait_ge(s_xnf, KT * c0 + k + 1)
                    at = half * HALF
                    sc.activation(XH[:, k, at:at + HALF], xnf[:, k % 2, :], ACT.Copy).then_inc(s_xh, 1)

            def attn(h, p):
                if p < 4:
                    e = 4 * h + p
                    act.wait_ge(s_mx, e + 1)
                    if e >= 2:
                        act.wait_ge(s_pt2, e - 1)
                    for j in range(2):
                        sc.activation(ptok[:, e % 2, j * M:(j + 1) * M], PS[:, NB + e % 2, j * M:(j + 1) * M], ACT.Exp,
                                      scale=XSCALE, bias=acol8[:, e % 2, 2 + j:3 + j],
                                      accum_out=acol8[:, e % 2, 4 + j:5 + j]).then_inc(s_ex, 1)
                if p in (3, 5):
                    for dt in range(2):
                        c = 4 * h + 2 * (p // 2 - 1) + dt
                        act.wait_ge(s_pv, c + 1)
                        if p == 3 and dt == 0:
                            act.wait_ge(s_mm, used(AT["wo", H - 1] if h == 0 else AT["xo", h - 1]))
                        at = (p // 2 - 1) * HALF
                        sc.activation(YH[:, dt, at:at + HALF], X3[:, :], ACT.Copy).then_inc(s_yh, 1)

            todo = {"gates": gates, "scan": scan, "memnorm": memnorm, "memturn": memturn,
                    "sumsq": lambda a, b: None, "norm": norm, "attn": attn}

            def evac(n, r):
                kind, h = STRIPS[n]
                g = FIRST[n] + r
                bank = PS[:, g % NB, :]
                if kind == "qk":
                    c = 4 * h + r
                    act.wait_ge(s_conv, c + 1)
                    if r == 0 and h >= 2:
                        act.wait_ge(s_b, TT * (h - 1))
                    at = (r // 2) * HALF
                    sc.activation(QK[:, h % 2, r % 2, at:at + HALF], acc[:, r % 2, :], ACT.Tanh, scale=0.5).then_inc(s_ex1, 1)
                    return
                if kind not in BY_ACT:
                    return
                act.wait_ge(s_mm, g + 1)
                if kind == "v":
                    if r == 0 and h == 0:
                        act.wait_ge(s_turn, TT)
                    if r == 0 and h >= 2:
                        act.wait_ge(s_b, TT * (h - 1))
                    sc.activation(VV[:, h % 2, 2 * r:2 * r + 2, 0:DV], bank.rearrange("p (t d) -> p t d", t=2),
                                  ACT.Copy).then_inc(s_fa, 1)
                elif kind == "o":
                    if r == 0 and h == 0:
                        act.wait_ge(s_gd, 5)
                    if r == 0 and h >= 1:
                        act.wait_ge(s_yf, TT * h)
                    sc.activation(SG[:, r % 2, (r // 2) * HALF:(r // 2 + 1) * HALF], bank,
                                  ACT.Tanh, scale=0.5).then_inc(s_fa, 1)
                elif kind == "mk":
                    if h == 0:
                        act.wait_ge(s_turn, TT + MT)
                        act.wait_ge(s_xs, TT + MT)
                    sc.activation(KM[:, 2 * h:2 * h + 2, :], bank.rearrange("p (t d) -> p t d", t=2),
                                  ACT.Copy).then_inc(s_fa, 1)
                elif kind == "mv":
                    sc.activation(VM[:, :, h * SW:(h + 1) * SW], bank.rearrange("p (t d) -> p t d", t=2),
                                  ACT.Copy).then_inc(s_fa, 1)
                elif kind == "q":
                    if r == 0 and h == 0:
                        act.wait_ge(s_b, TT * H)
                    if r == 0 and h == 1:
                        act.wait_ge(s_xl, 2 * TT + 2 * MT + 2 * KT)
                    if r == 0 and h >= 2:
                        act.wait_ge(s_sc, 4 * (h - 1))
                    sc.activation(QH[h % 2][:, r % 2, (r // 2) * HALF:(r // 2 + 1) * HALF], bank,
                                  ACT.Copy).then_inc(s_fa, 1)

            act.wait_ge(s_const, 8)
            for t in range(TT):
                act.wait_ge(s_xin[t % 2], 16 * (t // 2 + 1))
                square_tile(t, xin[:, t % 2, :], junk, t + 1)
                if t >= 1:
                    turned(sc, act, t - 1)
                if t == 3:
                    split_hi(0)
            turned(sc, act, TT - 1)
            for n in range(NF):
                kind, h = STRIPS[n]
                for r in range(NGROUPS[kind]):
                    run_parts(n, r, todo)
                    if r == 0:
                        split_hi(n + 1)
                    if kind == "o" and h >= 1 and r < 3:
                        if r == 2:
                            for q in range(3):
                                evac(n, q)
                    elif (kind, h) == ("xo", H - 1) and r < 4:
                        if r == 3:
                            for q in range(4):
                                square(n, q)
                    elif kind in ("wo", "xo") and h == H - 1:
                        square(n, r)
                    else:
                        evac(n, r)
                run_parts(n, "end", todo)

            def silu_out(g, r):
                act.wait_ge(s_mm, g + r + 1)
                act.wait_ge(s_xl, 2 * TT + 2 * MT + 4 * KT)
                sc.activation(SG[:, r % 2, (r // 2) * HALF:(r // 2 + 1) * HALF], PS[:, (g + r) % NB, :],
                              ACT.Silu).then_inc(s_fa, 1)

            def gate_evac(n, j, i=None):
                k = 0 if i is None else i
                for r in range(4):
                    g = FIRST[n] + r
                    if j == 0 and r == 0:
                        continue
                    if j == 0 and r == 1:
                        norm(1, 1)
                        silu_out(FIRST[n], 0)
                    act.wait_ge(s_mm, g + 1 + PER_LOOP["group"] * k)
                    if j >= 1:
                        if r == 0:
                            act.wait_ge(s_hf, 4 * j + 8 * k)
                    elif r >= 1:
                        act.wait_ge(s_xl, 2 * TT + 2 * MT + 4 * KT)
                    sc.activation(SG[:, r % 2, (r // 2) * HALF:(r // 2 + 1) * HALF], PS[:, g % NB, :],
                                  ACT.Silu).then_inc(s_fa, 1)

            def ffn_hi(j, down, i=None):
                k = 0 if i is None else i
                for r in range(4):
                    act.wait_ge(s_hf, 4 * j + r + 1 + 8 * k)
                    if r == 0:
                        act.wait_ge(s_mm, used(down) + PER_LOOP["group"] * k)
                    nt, at = r % 2, (r // 2) * HALF
                    sc.activation(YH[:, nt, at:at + HALF], acc[:, r % 2, :], ACT.Copy).then_inc(s_yh, 1)

            split_hi(NF + 1)
            gate_evac(NF, 0)
            split_hi(NF + 2)
            ffn_hi(0, AT["xo", H - 1])
            with act.Fori(0, NJ // 2) as i:
                for u in range(2):
                    n = NF + 2 + 3 * u
                    split_hi(n + 1, i)
                    gate_evac(n, 1 + u, i)
                    split_hi(n + 2, i)
                    split_hi(n + 3, i)
                    ffn_hi(1 + u, n + 1, i)
            for t in range(TT):
                act.wait_ge(s_turn, TT + MT + t + 1)
                square_tile(t, out_banks(t), junk, TT + MT + t + 1)

        @block.vector
        def _(dve):
            v = nc.vector
            steps = [0]

            def link(ins):
                steps[0] += 1
                ins.then_inc(s_dve, 1)
                dve.wait_ge(s_dve, steps[0])

            def gates(step, b):
                if step == 0:
                    dve.wait_ge(s_gpe, 1)
                    v.tensor_copy(grow.rearrange("p (a s) -> p a s", a=NHALF), PS[0:2 * H, NB:NB + 2, :]).then_inc(s_gr, 1)
                if step == 1:
                    dve.wait_ge(s_gpe, 2)
                    dve.wait_ge(s_gb, 16)
                    z = X2[:, 0:TT * 2 * H].rearrange("p (c g) -> p g c", g=2 * H)
                    gb = gbias[:, :].rearrange("p (g o) -> p g o", o=1).to_broadcast([P, 2 * H, TT])
                    v.tensor_tensor(ig[:, :].rearrange("p (g c) -> p g c", g=H), z[:, 0:H], gb[:, 0:H], ALU.add)
                    link(v.tensor_tensor(lf[:, :].rearrange("p (g c) -> p g c", g=H), z[:, H:], gb[:, H:], ALU.add))
                    v.scalar_tensor_tensor(out=gt2[:, :], in0=lf[:, :], scalar=-1.0, in1=lf[:, :], op0=ALU.mult,
                                           op1=ALU.min).then_inc(s_gd, 1)
                    link(v.tensor_scalar(lf[:, :], lf[:, :], 0.0, None, ALU.min))
                    dve.wait_ge(s_ga, 2)
                    v.tensor_tensor(lf[:, :], lf[:, :], gt2[:, :], ALU.subtract).then_inc(s_gd, 1)
                if step == 2:
                    dve.wait_ge(s_gpe, 3)
                    v.tensor_copy(bcum[:, :], X1[:, 0:R])
                    link(v.tensor_copy(gtot[:, :], X1[:, R:2 * R]))
                    v.tensor_tensor(acol[:, :], ig[:, :], bcum[:, :], ALU.subtract).then_inc(s_gd, 1)
                if step == 3:
                    dve.wait_ge(s_gpe, 4)
                    link(v.tensor_copy(cmax[:, 0, 64:], X2[0:R, 0:P]))
                    s, a = 1, 0
                    while s < P:
                        link(v.tensor_tensor(cmax[:, 1 - a, 64:], cmax[:, a, 64:], cmax[:, a, 64 - s:64 + P - s], ALU.max))
                        s, a = 2 * s, 1 - a
                    v.tensor_scalar(gt1[0:R, :], ident[0:R, 0:R], cmax[:, a, 64 + P - 1:64 + P], None,
                                    ALU.mult).then_inc(s_gd, 1)
                if step == 4:
                    dve.wait_ge(s_gpe, 5)
                    link(v.tensor_copy(mlast[:, :], X3[:, 0:R]))
                    hc = lambda t: t[:, :].rearrange("p (h c) -> p h c", h=H)
                    link(v.memset(hc(mprev)[:, :, 0:1], 0.0))
                    for c in range(TT - 1):
                        link(v.tensor_tensor(hc(mulast)[:, :, c:c + 1], hc(mprev)[:, :, c:c + 1], hc(mlast)[:, :, c:c + 1], ALU.max))
                        link(v.tensor_tensor(hc(mprev)[:, :, c + 1:c + 2], hc(mulast)[:, :, c:c + 1], hc(gtot)[:, :, c:c + 1], ALU.add))
                    link(v.tensor_tensor(mulast[:, :], mprev[:, :], mlast[:, :], ALU.max))
                    v.tensor_tensor(gt1[:, :], mprev[:, :], mulast[:, :], ALU.subtract)
                    link(v.tensor_tensor(gt2[:, :], acol[:, :], mulast[:, :], ALU.subtract))
                    link(v.tensor_tensor(ig[0:R, :], mprev[0:R, :], ident[0:R, 0:R], ALU.mult))
                    link(v.tensor_reduce(mprow[:, :], ig[0:R, :], AX, ALU.add))
                    a = 1
                    v.tensor_scalar(murow[:, :], cmax[:, a, 64:], mprow[:, 0:1], None, ALU.max).then_inc(s_gd, 1)
                if step == 5:
                    dve.wait_ge(s_gpe, 6)
                    v.tensor_tensor(mulast[:, :], bcum[:, :], X3[:, R:2 * R], ALU.add).then_inc(s_gd, 1)

            def scan(h, p):
                if p < TT:
                    e = h * TT + p
                    dve.wait_ge(s_st, e + 1)
                    dve.wait_ge(s_mask, e + 1)
                    if e >= 1:
                        dve.wait_ge(s_b, e)
                    v.scalar_tensor_tensor(out=PT[:, :], in0=X1[:, 2 * P:3 * P], scalar=QSCALE, in1=wT[:, :], op0=ALU.mult,
                                           op1=ALU.mult).then_inc(s_pt, 1)
                    dve.wait_ge(s_wi, e + 1)
                    if p == 0:
                        dve.wait_ge(s_qk, 4 * (h + 1))
                    v.scalar_tensor_tensor(out=qs[:, :], in0=QK[:, h % 2, 0, p * P:(p + 1) * P], scalar=QSCALE,
                                           in1=wi[:, :], op0=ALU.mult, op1=ALU.mult).then_inc(s_qs, 1)
                if 1 <= p <= TT:
                    e, c = h * TT + p - 1, p - 1
                    cc = ccol[:, e % 2, :]
                    dve.wait_ge(s_b, e + 1)
                    if c == 0:
                        v.tensor_copy(Cst[:, :], X3[:, 0:DV + 1]).then_inc(s_cst, 1)
                    elif c < TT - 1:
                        dve.wait_ge(s_cst, h * (TT - 1) + c)
                        v.scalar_tensor_tensor(out=Cst[:, :], in0=Cst[:, :], scalar=decay[:, e:e + 1],
                                               in1=X3[:, 0:DV + 1], op0=ALU.mult, op1=ALU.add).then_inc(s_cst, 1)
                    link(v.tensor_scalar(cc[:, 0:1], X2[:, DV:DV + 1], -1.0, emm[:, e:e + 1], ALU.mult, ALU.max))
                    link(v.tensor_tensor(cc[:, 1:2], X2[:, DV:DV + 1], cc[:, 0:1], ALU.max))
                    link(v.reciprocal(cc[:, 5:6], cc[:, 1:2]))
                    if e >= 2:
                        dve.wait_ge(s_tr, e - 1)
                    v.tensor_scalar(hs[:, e % 2, :], X2[:, 0:DV], cc[:, 5:6], None, ALU.mult).then_inc(s_hs, 1)
                if p >= 3:
                    e, at = h * TT + p - 3, (p - 3) * P
                    dve.wait_ge(s_tr, e + 1)
                    if p == 3:
                        dve.wait_ge(s_sg, 4 * (h + 1))
                    if e >= 1:
                        dve.wait_ge(s_yl, e)
                    for kk in range(2):
                        gain = vcols[:, A_NORM + 2 * h + kk:A_NORM + 2 * h + kk + 1]
                        last = v.scalar_tensor_tensor(out=yf[:, kk, :], in0=X1[:, kk * P:(kk + 1) * P], scalar=gain,
                                                      in1=SG[:, kk, at:at + P], op0=ALU.mult, op1=ALU.mult)
                    last.then_inc(s_yf, 1)
                if 2 <= p <= TT + 1:
                    e = h * TT + p - 2
                    dve.wait_ge(s_hr, e + 1)
                    v.tensor_scalar(hs[:, e % 2, :], hs[:, e % 2, :], ccol[:, e % 2, 4:5], None, ALU.mult).then_inc(s_hn, 1)

            def finish_qk(h, r):
                c, at = 4 * h + r, (r // 2) * HALF
                dst = QK[:, h % 2, r % 2, at:at + HALF]
                dve.wait_ge(s_ex1, c + 1)
                v.scalar_tensor_tensor(out=dst, in0=dst, scalar=1.0, in1=acc[:, r % 2, :], op0=ALU.add,
                                       op1=ALU.mult).then_inc(s_qk, 1)

            def finish_o(n, r):
                dst = SG[:, r % 2, (r // 2) * HALF:(r // 2 + 1) * HALF]
                dve.wait_ge(s_fa, FREED[FIRST[n] + r][1])
                v.tensor_scalar(dst, dst, 0.5, 0.5, ALU.mult, ALU.add).then_inc(s_sg, 1)

            def memnorm(a, b):
                dve.wait_ge(s_gain, 32)
                for t in range(MT):
                    dve.wait_ge(s_rs, TT + t + 1)
                    v.scalar_tensor_tensor(out=mxs[:, t, :], in0=mxin[:, t, :], scalar=stat[:, t, 2:3], in1=gain_mem,
                                           op0=ALU.mult, op1=ALU.mult).then_inc(s_xs, 1)

            def memturn(a, b):
                for t in range(MT):
                    for q in range(2):
                        dve.wait_ge(s_xh, 2 * TT + 2 * t + q + 1)
                        at = slice(t * P, (t + 1) * P)
                        v.tensor_tensor(ML[:, 4 * q:4 * q + 4, at], PS[:, NB + 2 * t + q, :].rearrange("p (k s) -> p k s", k=4),
                                        MH[:, 4 * q:4 * q + 4, at].bitcast(F32), ALU.subtract).then_inc(s_xl, 1)

            def norm(which, half):
                c0 = NHALF * which + half
                nt = HALF // P
                dve.wait_ge(s_ssq, c0 + 1)
                if c0:
                    dve.wait_ge(s_nm, c0)
                v.tensor_copy(nstat[:, 0:nt], X2[:, 0:nt]).then_inc(s_ns, 1)
                dve.wait_ge(s_nr, c0 + 1)
                if c0:
                    dve.wait_ge(s_rt, c0)
                v.tensor_tensor(rdiag, ident[:, :].rearrange("p (o s) -> p o s", o=1).to_broadcast([P, nt, P]),
                                nstat[:, 2 * nt:3 * nt].rearrange("p (t o) -> p t o", o=1).to_broadcast([P, nt, P]),
                                ALU.mult).then_inc(s_rd, 1)
                dve.wait_ge(s_rt, c0 + 1)
                for k in range(KT):
                    c = KT * c0 + k
                    if c >= 2:
                        dve.wait_ge(s_xl, 2 * TT + 2 * MT + c - 1)
                    gain = (NORM_X, NORM_F)[which] + k
                    v.scalar_tensor_tensor(out=xnf[:, k % 2, :], in0=xT[:, k, half * HALF:(half + 1) * HALF],
                                           scalar=vcols[:, gain:gain + 1], in1=PS[:, NB + half, :], op0=ALU.mult,
                                           op1=ALU.mult).then_inc(s_xnf, 1)

            def attn(h, p):
                if 1 <= p <= 4:
                    e = 4 * h + p - 1
                    dve.wait_ge(s_ex, 2 * (e + 1))
                    link(v.reciprocal(acol8[:, e % 2, 6:8], acol8[:, e % 2, 4:6]))
                    for j in range(2):
                        last = v.tensor_scalar(ptok[:, e % 2, j * M:(j + 1) * M], ptok[:, e % 2, j * M:(j + 1) * M],
                                               acol8[:, e % 2, 6 + j:7 + j], None, ALU.mult)
                    last.then_inc(s_pn, 1)
                if p < 4:
                    e = 4 * h + p
                    dve.wait_ge(s_sc, e + 1)
                    link(v.tensor_reduce(acol8[:, e % 2, 0:2], PS[:, NB + e % 2, :].rearrange("p (j m) -> p j m", j=2), AX, ALU.max))
                    v.tensor_scalar(acol8[:, e % 2, 2:4], acol8[:, e % 2, 0:2], -XSCALE, None, ALU.mult).then_inc(s_mx, 1)
                if 1 <= p <= 4:
                    e = 4 * h + p - 1
                    dve.wait_ge(s_pt2, e + 1)
                    if h >= 1 and p == 1:
                        dve.wait_ge(s_pv, 4 * h)
                    if h == 0 and p == 1:
                        dve.wait_ge(s_xnf, 2 * KT)
                    v.tensor_copy(PA[:, :, (p - 1) * SW:p * SW], X2[:, :].rearrange("p (m s) -> p m s", m=MT)).then_inc(s_pa, 1)
                if p in (3, 5):
                    for dt in range(2):
                        c = 4 * h + 2 * (p // 2 - 1) + dt
                        dve.wait_ge(s_yh, H * TT + c + 1)
                        at = (p // 2 - 1) * HALF
                        v.tensor_tensor(YL[:, dt, at:at + HALF], X3[:, :], YH[:, dt, at:at + HALF].bitcast(F32),
                                        ALU.subtract).then_inc(s_yl, 1)

            todo = {"gates": gates, "scan": scan, "memnorm": memnorm, "memturn": memturn,
                    "sumsq": lambda a, b: None, "norm": norm, "attn": attn}

            def add_residual(g, r, k=0):
                dve.wait_ge(s_mm, g + 1 + PER_LOOP["group"] * k)
                xt = xT[:, r % KT, (r // KT) * HALF:(r // KT + 1) * HALF]
                v.tensor_tensor(xt, PS[:, g % NB, :], xt, ALU.add).then_inc(s_fd, 1)

            def evac(n, r):
                kind, h = STRIPS[n]
                g = FIRST[n] + r
                if kind == "qk":
                    c, a, half = 4 * h + r, acc[:, r % 2, :], r // 2
                    bank = PS[:, g % NB, :]
                    tap = lambda j: vcols[:, CONV + KT * j + (r % 2) * H + h:CONV + KT * j + (r % 2) * H + h + 1]
                    dve.wait_ge(s_mm, g + 1)
                    if c >= 2:
                        dve.wait_ge(s_qk, c - 1)
                    link(v.tensor_scalar(a, bank, tap(TAPS - 1), None, ALU.mult))
                    for j in range(TAPS - 2, -1, -1):
                        lag = TAPS - 1 - j
                        ins = v.scalar_tensor_tensor(out=a[:, lag:], in0=bank[:, 0:HALF - lag], scalar=tap(j),
                                                     in1=a[:, lag:], op0=ALU.mult, op1=ALU.add)
                        if half:
                            link(ins)
                            ins = v.scalar_tensor_tensor(out=a[:, 0:lag], in0=halo[:, r % 2, TAPS - 1 - lag:], scalar=tap(j),
                                                         in1=a[:, 0:lag], op0=ALU.mult, op1=ALU.add)
                        if j:
                            link(ins)
                    ins.then_inc(s_conv, 1)
                    dve.wait_ge(s_conv, c + 1)
                    v.tensor_copy(halo[:, r % 2, :], bank[:, HALF - TAPS + 1:]).then_inc(s_fd, 1)
                    if r:
                        finish_qk(h, r - 1)
                elif kind == "v" and r == 0:
                    finish_qk(h, 3)
                elif kind == "o" and r == 3:
                    for q in range(4):
                        finish_o(n, q)
                elif kind not in BY_ACT:
                    add_residual(g, r)

            for t in range(TT):
                dve.wait_ge(s_rs, t + 1)
                dve.wait_ge(s_xg, t + 1)
                v.tensor_scalar(xs[:, t % 2, :], xs[:, t % 2, :], stat[:, t, 2:3], None, ALU.mult).then_inc(s_xs, 1)
                if t >= 1:
                    turned_dve(v, dve, t - 1)
                if t == 3:
                    dve.wait_ge(s_vturn, 1)
                    v.tensor_copy(vcols[:, :], X3[:, 0:56]).then_inc(s_vc, 1)
                    dve.wait_ge(s_wg, 16)
                    v.memset(YH[:, 0, :].bitcast(F32), 0.0)
                    link(v.memset(YL[:, 0, :].bitcast(F32), 0.0))
                    link(v.tensor_copy(wgp[0][:, :, 0:2 * H], wg_raw))
                    v.tensor_tensor(wgp[1][:, :, 0:2 * H], wg_raw, wgp[0][:, :, 0:2 * H].bitcast(F32), ALU.subtract).then_inc(s_wgs, 1)
            turned_dve(v, dve, TT - 1)
            for par in range(2):
                v.memset(VV[:, par, :, DV:DV + 1], 1.0).then_inc(s_ones, 1)
            dve.wait_ge(s_vc, 1)
            for n in range(NF):
                for r in [*range(NGROUPS[STRIPS[n][0]])]:
                    run_parts(n, r, todo)
                    evac(n, r)
                run_parts(n, "end", todo)

            def up_evac(n, j, i=None):
                k = 0 if i is None else i
                for r in range(4):
                    g = FIRST[n] + r
                    dve.wait_ge(s_mm, g + 1 + PER_LOOP["group"] * k)
                    dve.wait_ge(s_fa, FREED[FIRST[n] - (4 if j == 0 else 20) + r][1] + PER_LOOP["act"] * k)
                    if j >= 1 or r >= 2:
                        dve.wait_ge(s_yl, Y_FFN + 4 * j + r - 1 + 8 * k)
                    ins = v.tensor_tensor(acc[:, r % 2, :], PS[:, g % NB, :],
                                          SG[:, r % 2, (r // 2) * HALF:(r // 2 + 1) * HALF], ALU.mult)
                    ins.then_inc(s_hf, 1)

            def down_evac(n, i=None):
                for r in range(16):
                    add_residual(FIRST[n] + r, r, 0 if i is None else i)

            norm(1, 1)
            up_evac(NF + 1, 0)
            with dve.Fori(0, NJ // 2) as i:
                for u in range(2):
                    n = NF + 2 + 3 * u
                    down_evac(n + 1, i)
                    up_evac(n + 2, 1 + u, i)
            def finish_out(t):
                dve.wait_ge(s_rs, TT + MT + t + 1)
                if t >= 2:
                    dve.wait_ge(s_out[t % 2], 16 * (t // 2))
                v.scalar_tensor_tensor(out=fout[:, t % 2, :], in0=out_banks(t), scalar=stat[:, t, 2:3], in1=gain_out,
                                       op0=ALU.mult, op1=ALU.mult).then_inc(s_xs, 1)

            n = len(STRIPS) - 1
            for r in range(16):
                add_residual(FIRST[n] + r, r)
                if r == 12:
                    dve.wait_ge(s_gain, 48)
                    finish_out(0)
                if r == 14:
                    finish_out(1)
            for t in range(2, TT):
                finish_out(t)

        @block.tensor
        def _(pe):
            mm = nc.tensor.matmul

            def wait_strip(n, k=0):
                pe.wait_ge(s_whi, n + 1 + PER_LOOP["strip"] * k)
                pe.wait_ge(s_wlo, n + 1 + PER_LOOP["strip"] * k)

            def wait_bank(g, k=0):
                if g >= NB:
                    who, count = FREED[g - NB]
                    pe.wait_ge({"act": s_fa, "dve": s_fd, "up": s_hf}[who], count + PER_LOOP[who] * k)

            def product(dst, tiles, before=None):
                for k, ((wh, wl), (xh, xl)) in enumerate(tiles):
                    if before is not None:
                        pe.wait_ge(s_xl, before + k + 1)
                    mm(dst, wh, xh, start=(k == 0), stop=False)
                    mm(dst, wh, xl, start=False, stop=False)
                    last = mm(dst, wl, xh, start=False, stop=(k == len(tiles) - 1))
                return last

            def col(n, k, nt, width=P):
                at = k * SW + nt * width
                return WH[:, n % 2, at:at + width], WL[:, n % 2, at:at + width]

            def rowt(n, kk, ft):
                at = kk * D + ft * P
                return WH[:, n % 2, at:at + P], WL[:, n % 2, at:at + P]

            def xpart(k, at, width):
                return XH[:, k, at:at + width], XL[:, k, at:at + width]

            def mpart(k, at, width):
                return MH[:, k, at:at + width], ML[:, k, at:at + width]

            def group(n, r, k=0, before=None):
                kind, h = STRIPS[n]
                g = FIRST[n] + r
                bank = PS[:, g % NB, :]
                wait_bank(g, k)
                if kind in ("wo", "xo", "down"):
                    at = (r // KT) * HALF
                    last = product(bank, [(rowt(n, kk, r % KT), (YH[:, kk, at:at + HALF], YL[:, kk, at:at + HALF]))
                                          for kk in range(2)])
                elif kind == "v":
                    for t in range(2):
                        at = (2 * r + t) * P
                        last = product(bank[:, t * DV:(t + 1) * DV], [(xpart(kk, at, P), col(n, kk, 0, SW)) for kk in range(KT)])
                elif kind == "mv":
                    for t in range(2):
                        last = product(bank[:, t * DV:(t + 1) * DV], [(mpart(kk, t * P, P), col(n, kk, 0, SW)) for kk in range(KT)])
                elif kind == "mk":
                    for t in range(2):
                        last = product(bank[:, t * M:(t + 1) * M], [(col(n, kk, t), mpart(kk, 0, M)) for kk in range(KT)])
                else:
                    at = (r // 2) * HALF
                    last = product(bank, [(col(n, kk, r % 2), xpart(kk, at, HALF)) for kk in range(KT)], before)
                last.then_inc(s_mm, 1)
                return last

            def gates(step, b):
                if step == 0:
                    pe.wait_ge(s_wgs, 1)
                    for half in range(NHALF):
                        last = product(PS[:, NB + half, :], [((wgp[0][:, kk, :], wgp[1][:, kk, :]), xpart(kk, half * HALF, HALF))
                                                             for kk in range(KT)])
                    last.then_inc(s_gpe, 1)
                if step == 1:
                    pe.wait_ge(s_gr, 1)
                    for t in range(TT):
                        last = nc.tensor.transpose(X2[:, t * 2 * H:(t + 1) * 2 * H], grow[:, t * P:(t + 1) * P],
                                                   ident[0:2 * H, 0:2 * H])
                    last.then_inc(s_gpe, 1)
                if step == 2:
                    pe.wait_ge(s_gd, 2)
                    mm(X1[:, 0:R], tri, lf[:, :], start=True, stop=True)
                    mm(X1[:, R:2 * R], ones[:, :], lf[:, :], start=True, stop=True).then_inc(s_gpe, 1)
                if step == 3:
                    pe.wait_ge(s_gd, 3)
                    nc.tensor.transpose(X2[0:R, 0:P], acol[:, :], ident[:, :]).then_inc(s_gpe, 1)
                if step == 4:
                    pe.wait_ge(s_gd, 4)
                    mm(X3[:, 0:R], ones[0:R, :], gt1[0:R, :], start=True, stop=True).then_inc(s_gpe, 1)
                if step == 5:
                    pe.wait_ge(s_gd, 5)
                    nc.tensor.transpose(X3[:, R:2 * R], murow[:, :], ident[0:R, 0:R]).then_inc(s_gpe, 1)

            def scan(h, p):
                if p >= 3:
                    e = h * TT + p - 3
                    pe.wait_ge(s_hn, e + 1)
                    pe.wait_ge(s_pt, h * TT + min(p, TT))
                    if e >= 1:
                        pe.wait_ge(s_yf, e)
                    for kk in range(2):
                        last = nc.tensor.transpose(X1[:, kk * P:(kk + 1) * P], hs[:, e % 2, kk * P:(kk + 1) * P], ident[:, :])
                    last.then_inc(s_tr, 1)
                if p < TT:
                    e, at = h * TT + p, slice(p * P, (p + 1) * P)
                    if e >= 1:
                        pe.wait_ge(s_ks, e)
                        pe.wait_ge(s_pt, e)
                    if e == 0:
                        pe.wait_ge(s_gd, 6)
                    if p == 0:
                        pe.wait_ge(s_qk, 4 * (h + 1))
                        if h >= 1:
                            pe.wait_ge(s_yf, h * TT)
                        if h == H - 1:
                            pe.wait_ge(s_xl, 2 * TT + 2 * MT)
                    k_t = QK[:, h % 2, 1, at]
                    mm(X0[:, 0:P], ident[0:R, e:e + 1].to_broadcast([R, P]), murow[:, :], start=True, stop=True)
                    nc.tensor.transpose(X0[:, P:2 * P], k_t, ident[:, :]).then_inc(s_mu, 1)
                    mm(X1[:, 2 * P:3 * P], k_t, QK[:, h % 2, 0, at], start=True, stop=True).then_inc(s_st, 1)
                if 1 <= p <= TT:
                    e, c = h * TT + p - 1, p - 1
                    pe.wait_ge(s_pt, e + 1)
                    pe.wait_ge(s_qs, e + 1)
                    pe.wait_ge(s_ks, e + 1)
                    if e >= 1:
                        pe.wait_ge(s_hs, e)
                    pe.wait_ge(s_cst, h * (TT - 1) + c) if c or h else None
                    if c == 0:
                        pe.wait_ge(s_fa, FREED[FIRST[AT["v", h]] + 3][1])
                        pe.wait_ge(s_ones, 2)
                    vc = VV[:, h % 2, c, :]
                    last = mm(X2[:, 0:DV + 1], PT[:, :], vc, start=True, stop=(c == 0))
                    if c:
                        last = mm(X2[:, 0:DV + 1], qs[:, :], Cst[:, :], start=False, stop=True)
                    if c < TT - 1:
                        last = mm(X3[:, 0:DV + 1], ks[:, :], vc, start=True, stop=True)
                    last.then_inc(s_b, 1)

            def memturn(a, b):
                for t in range(MT):
                    pe.wait_ge(s_xs, TT + t + 1)
                    if t == 0:
                        pe.wait_ge(s_yf, TT * (H - 1))
                    for q in range(KT):
                        last = nc.tensor.transpose(PS[:, NB + 2 * t + q // 4, (q % 4) * P:(q % 4 + 1) * P],
                                                   mxs[:, t, q * P:(q + 1) * P], ident[:, :])
                    last.then_inc(s_turn, 1)

            def sumsq(which, half):
                c0 = NHALF * which + half
                pe.wait_ge(s_sacc, (KT - 1) * (c0 + 1))
                if which == 0 and half == 0:
                    pe.wait_ge(s_ks, H * TT)
                    pe.wait_ge(s_yf, H * TT)
                if which == 1 and half == 0:
                    pe.wait_ge(s_ex, 8 * H)
                for t in range(HALF // P):
                    last = mm(X2[:, t:t + 1], sqsum[:, half, t * P:(t + 1) * P], ones[:, 0:1], start=True, stop=True)
                last.then_inc(s_ssq, 1)

            def norm(which, half):
                pe.wait_ge(s_rd, NHALF * which + half + 1)
                mm(PS[:, NB + half, :], ones[:, :], rdiag.rearrange("p t s -> p (t s)"), start=True, stop=True).then_inc(s_rt, 1)

            def attn(h, p):
                if p < 4:
                    e = 4 * h + p
                    if e >= 2:
                        pe.wait_ge(s_ex, 2 * (e - 1))
                    else:
                        pe.wait_ge(s_xnf, 2 * KT)
                    if p == 0:
                        pe.wait_ge(s_fa, FREED[FIRST[AT["q", h]] + 3][1])
                    for j in range(2):
                        at = slice((2 * p + j) * P, (2 * p + j + 1) * P)
                        for kk in range(2):
                            last = mm(PS[:, NB + e % 2, j * M:(j + 1) * M], QH[h % 2][:, kk, at], KM[:, 2 * h + kk, :],
                                      start=(kk == 0), stop=(kk == 1))
                    last.then_inc(s_sc, 1)
                if 1 <= p <= 4:
                    e = 4 * h + p - 1
                    pe.wait_ge(s_pn, e + 1)
                    if e >= 1:
                        pe.wait_ge(s_pa, e)
                    for j in range(2):
                        for m in range(MT):
                            last = nc.tensor.transpose(X2[:, m * SW + j * P:m * SW + (j + 1) * P],
                                                       ptok[:, e % 2, j * M + m * P:j * M + (m + 1) * P], ident[:, :])
                    last.then_inc(s_pt2, 1)
                if p in (3, 5):
                    half = p // 2 - 1
                    pe.wait_ge(s_pa, 4 * h + 2 * half + 2)
                    for dt in range(2):
                        c = 4 * h + 2 * half + dt
                        if c == 0:
                            pe.wait_ge(s_yf, H * TT)
                        pe.wait_ge(s_yl, H * TT + c)
                        for m in range(MT):
                            last = mm(X3[:, :], VM[:, m, h * DV + dt * P:h * DV + (dt + 1) * P],
                                      PA[:, m, half * HALF:(half + 1) * HALF], start=(m == 0), stop=(m == MT - 1))
                        last.then_inc(s_pv, 1)

            todo = {"gates": gates, "scan": scan, "memnorm": lambda a, b: None, "memturn": memturn, "sumsq": sumsq,
                    "norm": norm, "attn": attn}

            pe.wait_ge(s_const, 8)
            for t in range(TT):
                pe.wait_ge(s_xin[t % 2], 16 * (t // 2 + 1))
                if t >= 2:
                    pe.wait_ge(s_xt, t - 1)
                    pe.wait_ge(s_xta, t - 1)
                    pe.wait_ge(s_xl, 2 * (t - 1))
                if t == 3:
                    pe.wait_ge(s_vc, 1)
                for q in range(KT):
                    nc.tensor.transpose(PS[:, 4 * (t % 2) + q // 4, (q % 4) * P:(q % 4 + 1) * P],
                                        xin[:, t % 2, q * P:(q + 1) * P], ident[:, :])
                pe.wait_ge(s_xs, t + 1)
                for q in range(KT):
                    last = nc.tensor.transpose(PS[:, 4 * (t % 2) + 2 + q // 4, (q % 4) * P:(q % 4 + 1) * P],
                                               xs[:, t % 2, q * P:(q + 1) * P], ident[:, :])
                last.then_inc(s_turn, 1)
                if t == 2:
                    pe.wait_ge(s_vec, 64)
                    pe.wait_ge(s_xl, 4)
                    nc.tensor.transpose(X3[:, 0:56], vrows, ident[0:56, 0:56]).then_inc(s_vturn, 1)
            pe.wait_ge(s_xl, 2 * TT)
            pe.wait_ge(s_xh, 2 * TT)
            pe.wait_ge(s_xt, TT)
            pe.wait_ge(s_xta, TT)

            for n in range(NF):
                kind, h = STRIPS[n]
                for r in range(NGROUPS[kind]):
                    run_parts(n, r, todo)
                    if r == 0:
                        wait_strip(n)
                        if kind == "mk" and h == 0:
                            pe.wait_ge(s_xl, 2 * TT + 2 * MT)
                    if kind == "wo" and r in (0, KT):
                        pe.wait_ge(s_yl, TT * h + TT // 2 * (r // KT + 1))
                    if kind == "xo" and r in (0, KT):
                        pe.wait_ge(s_yl, H * TT + 4 * h + 2 * (r // KT + 1))
                    if kind == "q" and h == 0 and r % 2 == 0:
                        group(n, r, before=2 * TT + 2 * MT + KT * (r // 2))
                    else:
                        group(n, r)
                run_parts(n, "end", todo)

            def ffn_strip(n, i=None, lo=None):
                k = 0 if i is None else i
                wait_strip(n, k)
                if lo is not None:
                    pe.wait_ge(s_yl, lo + 8 * k)
                for r in range(NGROUPS[STRIPS[n][0]]):
                    if n == NF and r == 1:
                        sumsq(1, 1)
                        norm(1, 1)
                    if n == NF and r % 2 == 0:
                        group(n, r, before=2 * TT + 2 * MT + 2 * KT + KT * (r // 2))
                    else:
                        group(n, r, k)

            ffn_strip(NF)
            ffn_strip(NF + 1)
            with pe.Fori(0, NJ // 2) as i:
                for u in range(2):
                    n = NF + 2 + 3 * u
                    ffn_strip(n, i)
                    ffn_strip(n + 1, i, lo=Y_FFN + 4 * (u + 1))
                    ffn_strip(n + 2, i)
            def turn_back(t):
                pe.wait_ge(s_fd, FREED[FIRST[len(STRIPS) - 1] + (7 if t < 4 else 15)][1])
                if t in (2, 3):
                    pe.wait_ge(s_xs, TT + MT + t - 1)
                if t in (6, 7):
                    pe.wait_ge(s_xs, TT + MT + t - 3)
                for q in range(KT):
                    last = nc.tensor.transpose(out_banks(t)[:, q * P:(q + 1) * P], xT[:, q, t * P:(t + 1) * P], ident[:, :])
                last.then_inc(s_turn, 1)

            n = len(STRIPS) - 1
            wait_strip(n)
            pe.wait_ge(s_yl, Y_FFN + 4 * NJ)
            for r in range(16):
                if r == 10:
                    turn_back(0)
                if r == 11:
                    turn_back(1)
                if r == 14:
                    turn_back(2)
                if r == 15:
                    turn_back(3)
                group(n, r)
            for t in range(4, TT):
                turn_back(t)


_INS = ["x", "mem", "norm_mix", "norm_x", "norm_ffn", "norm_mem", "norm_final", "a_w_in", "a_conv_w", "a_gate_b",
        "a_norm", "a_w_out", "x_w_q", "x_w_kv", "x_w_o", "f_w_gate", "f_w_up", "f_w_down"]


def kernel(**inputs):
    import numpy as _np
    import concourse.bacc as _bacc
    from concourse import mybir as _mybir
    from concourse.bass_utils import run_bass_kernel_spmd as _run

    nc = _bacc.Bacc("TRN2", target_bir_lowering=False, num_devices=1)
    arrays, args = {}, []
    for name in _INS:
        a = _np.ascontiguousarray(inputs[name])
        arrays[f"in_{name}_dram"] = a
        args.append(nc.dram_tensor(f"in_{name}_dram", a.shape, _mybir.dt.from_np(a.dtype), kind="ExternalInput").ap())
    args.append(nc.dram_tensor("out_0_dram", inputs["x"].shape, _mybir.dt.float32, kind="ExternalOutput").ap())
    build_block(nc, *args)
    r = _run(nc, [arrays], core_ids=[0])
    return r.results[0]["out_0_dram"]
```

```python
import concourse.bass as bass
from concourse import mybir
from contextlib import ExitStack

F32, F32R = mybir.dt.float32, mybir.dt.float32r
ALU = mybir.AluOpType
ACT = mybir.ActivationFunctionType
AX = mybir.AxisListType.X

P = 128
EPS = 1e-6
LOWEST = -3.0e38


def build_block(nc, x, mem, norm_mix, norm_x, norm_ffn, norm_mem, norm_final, a_w_in, a_conv_w, a_gate_b,
                a_norm, a_w_out, x_w_q, x_w_kv, x_w_o, f_w_gate, f_w_up, f_w_down, out):
    S, D = x.shape[1], x.shape[2]
    M = mem.shape[1]
    KT = D // P
    TT = S // P
    MT = M // P
    HALF = 512
    NHALF = S // HALF
    H = a_gate_b.shape[1] // 2
    DK = a_conv_w.shape[2] // (2 * H)
    DV = D // H
    TAPS = a_conv_w.shape[1]
    SW = 2 * P
    F = f_w_gate.shape[2]
    NJ = F // SW
    QSCALE = float(DK) ** -0.5 / 4
    XSCALE = float(DV) ** -0.5
    V0, O0, G0 = 2 * H * DK, 2 * H * DK + H * DV, 2 * H * DK + 2 * H * DV
    R = H * TT
    assert DK == P and DV == SW and NJ % 2 == 1 and MT == 2 and KT == 8 and TT == 8 and H == 4

    STRIPS = [("qk", 0), ("v", 0), ("o", 0)]
    for h in range(1, H):
        STRIPS += [("qk", h), ("v", h), ("o", h), ("wo", h - 1)]
    STRIPS += [("mk", j) for j in range(H)] + [("wo", H - 1)] + [("mv", j) for j in range(H)] + [("q", 0)]
    for h in range(1, H):
        STRIPS += [("q", h), ("xo", h - 1)]
    STRIPS += [("xo", H - 1)]
    NF = len(STRIPS)
    STRIPS += [("gate", 0), ("up", 0)]
    for j in range(1, NJ):
        STRIPS += [("gate", j), ("down", j - 1), ("up", j)]
    STRIPS += [("last", NJ - 1)]
    AT = {s: n for n, s in enumerate(STRIPS)}
    assert NF % 2 == 0
    NGROUPS = {"qk": 4, "v": 4, "o": 4, "wo": 16, "mk": 1, "mv": 1, "q": 4, "xo": 16,
               "gate": 4, "up": 4, "down": 16, "last": 24}
    BY_ACT = {"v", "o", "mk", "mv", "q", "gate"}
    FIRST, FREED, took = {}, [], {"act": 0, "dve": 0, "up": 0}
    GROUPS = [(n, r) for n, (kind, _) in enumerate(STRIPS) for r in range(NGROUPS[kind])]
    at = GROUPS.index((NF, 0))
    GROUPS[at:at + 8] = [(NF + (r // 2) % 2, r % 2 + 2 * (r // 4)) for r in range(8)]
    GI = {nr: g for g, nr in enumerate(GROUPS)}
    for n, r in GROUPS:
        kind = STRIPS[n][0]
        if r == 0:
            FIRST[n] = GI[n, 0]
        who = "act" if kind in BY_ACT else "up" if kind == "up" else "dve"
        took[who] += 1
        FREED.append((who, took[who]))
    used = lambda n: GI[n, NGROUPS[STRIPS[n][0]] - 1] + 1
    NB = 4
    RAW2 = {AT["mk", 1]: 0, AT["mk", 3]: 0, AT["mv", 0]: 1, AT["mv", 2]: 1, AT["q", 0]: 1}
    LO_SHARED = [AT["mk", 1], AT["mk", 2], AT["mk", 3], AT["wo", H - 1], AT["mv", 1], AT["mv", 2], AT["mv", 3], AT["q", 0]]
    DMAS, dmas = [], [0, 0]
    for n, (kind, _) in enumerate(STRIPS):
        dmas[n in RAW2] += 2 if kind == "qk" else 1
        DMAS.append((int(n in RAW2), dmas[n in RAW2]))
    PER_LOOP = {"strip": 6, "group": 48, "act": 8, "dve": 32, "up": 8}

    PARTS = {}

    def part(kind, h, r, what):
        PARTS.setdefault((AT[kind, h], r), []).append(what)

    for step, (kind, r) in enumerate([("v", 0), ("v", 2), ("v", 3), ("o", 0), ("o", 1), ("o", 3)]):
        part(kind, 0, r, ("gates", step, None))
    NP = TT + 3
    for h in range(1, H):
        for p in range(NP):
            kind, r = ("qk", p) if p < 4 else ("v", p - 3) if p < 7 else ("o", p - 7)
            part(kind, h, r, ("scan", h - 1, p))
    part("o", H - 1, 3, ("memnorm", 0, None))
    part("wo", H - 2, 3, ("memturn", 0, None))
    for p in range(3):
        part("wo", H - 2, 5 + 4 * p, ("scan", H - 1, p))
    for p in range(3, NP):
        part("mk", (p - 3) // 2, (0, "mid")[(p - 3) % 2], ("scan", H - 1, p))

    LATE = (0, 1)
    EARLY = tuple(range(2, KT))
    PIECES = [(c, k) for c in (0, 1) for k in range(KT)]
    PIECES += [(2, k) for k in EARLY] + [(3, k) for k in EARLY[:4]]
    PIECES += [(2, k) for k in LATE] + [(3, k) for k in EARLY[4:]] + [(3, k) for k in LATE]
    PIECES += [(c, k) for c in (4, 5) for k in range(KT)]
    PAT = {ck: i for i, ck in enumerate(PIECES)}
    LO, los = {}, {"dve": 0, "pool": 0}
    for c, k in PIECES:
        who = "dve" if c in (2, 3) or (c < 2 and k % 2 == 0) else "pool"
        los[who] += 1
        LO[c, k] = (who, los[who])
    BC = [3, 5, 4, 5, 4, 5]
    X_BANK = [0, 4, 6, 0, 4, 6, 4, 6]
    X_BEFORE = [None, None, None, 0, 1, 2, 4, 5]
    part("wo", H - 1, 10, ("sumsq", 1, 0))
    part("wo", H - 1, 12, ("spread", 1, 0))
    part("wo", H - 1, 14, ("pieces", 2, (2,)))
    part("mv", 0, "mid", ("pieces", 2, (3, 4, 5)))
    part("mv", 1, "mid", ("pieces", 2, (6, 7)))
    part("mv", 0, "end", ("sumsq", 1, 1))
    part("mv", 2, 0, ("spread", 1, 1))
    part("mv", 2, "mid", ("pieces", 3, (2, 3, 4)))
    part("mv", 3, "mid", ("pieces", 3, (5,)))
    part("mv", 3, "end", ("pieces", 2, LATE))
    part("mv", 3, "end", ("pieces", 3, (6, 7)))
    part("mv", 3, "end", ("pieces", 3, LATE))
    part("xo", H - 1, 10, ("sumsq", 2, 0))
    part("xo", H - 1, 12, ("spread", 2, 0))
    for i in range(4):
        part("xo", H - 1, 12 + i, ("pieces", 4, (2 * i, 2 * i + 1)))
    for h in range(1, H):
        for p in range(4):
            part("q", h, p, ("attn", h - 1, p))
    for h in range(H):
        late = int(h == H - 1)
        part("xo", h, late, ("attn", h, 4))
        part("xo", h, 3 + late, ("attn", h, 5))
    for p in range(4):
        part("xo", H - 2, (4, 7, 9, 12)[p], ("attn", H - 1, p))

    def run_parts(n, r, todo):
        for what, a, b in PARTS.get((n, r), []):
            todo[what](a, b)

    x_t = x[0].rearrange("(t p) d -> t p d", p=P)
    mem_t = mem[0].rearrange("(t p) d -> t p d", p=P)
    out_t = out[0].rearrange("(t p) d -> t p d", p=P)

    def cols(w, at, width=SW):
        return w[0, :, at:at + width].rearrange("(k p) n -> p k n", p=P)

    def rows(w, at):
        return w[0, at:at + SW, :].rearrange("(k p) n -> p k n", p=P)

    ctx = ExitStack()
    with ctx:
        def sb(name, shape, dt=F32):
            return ctx.enter_context(nc.sbuf_tensor(name, shape, dt))

        def sem(name):
            return ctx.enter_context(nc.semaphore(name))

        NORM_X, NORM_F, A_NORM, NORM_M, CONV = 0, KT, 2 * KT, 3 * KT, 4 * KT
        NVEC = CONV + TAPS * KT
        NT = HALF // P
        xT = sb("xT", [P, KT, S])
        XH = sb("XH", [P, KT, S], F32R)
        XL = sb("XL", [P, KT, S], F32R)
        raw = sb("raw", [P, KT * SW])
        WH = sb("WH", [P, 2, KT * SW], F32R)
        WL = sb("WL", [P, 2, KT * SW], F32R)
        QK = sb("QK", [P, 2, 2, S])
        VV = sb("VV", [P, 2, TT, DV + 1])
        SG = sb("SG", [P, 2, S])
        YH = sb("YH", [P, 2, S], F32R)
        YL = sb("YL", [P, 2, S], F32R)
        acc = sb("acc", [P, 2, HALF])
        ident = sb("ident", [P, P])
        ones = sb("ones", [P, P])
        causal = sb("causal", [P, P])
        vcols = sb("vcols", [P, NVEC])
        halo = sb("halo", [P, 2, TAPS - 1])
        gbias = sb("gbias", [P, 2 * H])
        half_neg = sb("half_neg", [P, NT])
        stat = sb("stat", [P, TT, 3])
        ig = sb("ig", [P, R])
        lf = sb("lf", [P, R])
        gt1 = sb("gt1", [P, R])
        gt2 = sb("gt2", [P, R])
        bcum = sb("bcum", [P, R])
        gtot = sb("gtot", [P, R])
        acol = sb("acol", [P, R])
        mlast = sb("mlast", [P, R])
        mprev = sb("mprev", [P, R])
        mulast = sb("mulast", [P, R])
        decay = sb("decay", [P, R])
        wa = sb("wa", [P, R])
        emm = sb("emm", [P, R])
        murow = sb("murow", [R, P])
        mprow = sb("mprow", [R, 1])
        wT = sb("wT", [P, P])
        wi = sb("wi", [P, P])
        qs = sb("qs", [P, P])
        ks = sb("ks", [P, DK])
        Cst = sb("Cst", [P, DV + 1])
        hs = sb("hs", [P, 2, DV])
        hsj = sb("hsj", [P, DV])
        nsum = sb("nsum", [P, NHALF, NT])
        nmean = sb("nmean", [P, NHALF, NT])
        nrms = sb("nrms", [P, NHALF, NT])
        yf = sb("yf", [P, 2, P])
        ccol = sb("ccol", [P, 2, 6])
        acol8 = sb("acol8", [P, 2, 8])
        mucol = gt2[:, :]
        PS = ctx.enter_context(nc.psum_tensor("PS", [P, 8, HALF], F32))
        X0, X1, X2, X3 = (PS[:, NB + i, :] for i in range(4))


        flat = lambda t: t.rearrange("p t d -> p (t d)")[:, 0:2 * S]
        xin = [flat(VV[:, t // 2]).rearrange("p (a d) -> p a d", a=2)[:, t % 2, :] for t in range(4)]
        raw_v = [flat(VV[:, par]) for par in range(2)]
        mxin = QK[:, 0]
        mxs = mxin
        gain_mem, mjunk = xin[0], xin[1]
        gain_out = SG[:, 0, :]
        tri = SG[:, 1, 0:P]
        cmax = SG[0:R, 1, HALF:HALF + 2 * (64 + P)].rearrange("r (a t) -> r a t", a=2)
        vrows = QK[0:NVEC, 0, 0, 0:P]
        wg_raw = QK[:, 0, 1, 0:KT * 2 * H].rearrange("p (k g) -> p k g", k=KT)
        MH = XH[:, 0:2, :].rearrange("p k s -> p (k s)").rearrange("p (k m) -> p k m", k=KT)
        ML = XL[:, 0:2, :].rearrange("p k s -> p (k s)").rearrange("p (k m) -> p k m", k=KT)
        KM = QK[:, 0].rearrange("p a s -> p (a s)").rearrange("p (k m) -> p k m", k=KT)
        VM = flat(VV[:, 0]).rearrange("p (a d) -> p a d", a=MT)
        QH = [flat(VV[:, 1]).rearrange("p (a s) -> p a s", a=2), SG[:, :, :]]
        PA = QK[:, 1].rearrange("p a s -> p (a s)").rearrange("p (m s) -> p m s", m=MT)
        ptok = acc[:, :, :]
        halves = lambda t: t.rearrange("p (a s) -> p a s", a=2)
        sqb = [None, halves(SG[:, 1, :]), halves(QK[:, 0, 0, :])]
        places = [SG[:, 0, 0:HALF], SG[:, 0, HALF:], acc[:, 0, :], acc[:, 1, :]]
        xnf = [places, places, [flat(VV[:, 1])[:, i * HALF:(i + 1) * HALF] for i in range(4)]]
        sqsum = [None, halves(QK[:, 1, 1, :]), SG[:, :, HALF:]]
        wgp = YH[:, 0, :].rearrange("p (k g) -> p k g", k=KT)
        grow = VV[0:4 * H, 1].rearrange("p t d -> p (t d)")[:, 0:S]
        fout = xin
        gsum = ks[:, 0:2 * R]
        junk = QK[:, 1, 1, :]

        s_const = sem("s_const")
        s_vec = sem("s_vec")
        s_gain = sem("s_gain")
        s_wg = sem("s_wg")
        s_gb = sem("s_gb")
        s_xin = [sem(f"s_xin{i}") for i in range(4)]
        s_min = [sem(f"s_min{i}") for i in range(2)]
        s_sq = sem("s_sq")
        s_rs = sem("s_rs")
        s_ms = sem("s_ms")
        s_xs = sem("s_xs")
        s_turn = sem("s_turn")
        s_xt = sem("s_xt")
        s_xh = sem("s_xh")
        s_xl = sem("s_xl")
        s_vturn = sem("s_vturn")
        s_vc = sem("s_vc")
        s_wgs = sem("s_wgs")
        s_wdma = sem("s_wdma")
        s_whi = sem("s_whi")
        s_wlo = sem("s_wlo")
        s_mm = sem("s_mm")
        s_fa = sem("s_fa")
        s_fd = sem("s_fd")
        s_conv = sem("s_conv")
        s_qk = sem("s_qk")
        s_gpe = sem("s_gpe")
        s_gd = sem("s_gd")
        s_ga = sem("s_ga")
        s_ones = sem("s_ones")
        s_gr = sem("s_gr")
        s_xta = sem("s_xta")
        s_wl0 = sem("s_wl0")
        s_wlod = sem("s_wlod")
        s_mh = sem("s_mh")
        s_ml = sem("s_ml")
        s_xlp = sem("s_xlp")
        s_wdma2 = sem("s_wdma2")
        s_ex1 = sem("s_ex1")
        s_sg = sem("s_sg")
        s_sacc = sem("s_sacc")
        s_mu = sem("s_mu")
        s_st = sem("s_st")
        s_wt = sem("s_wt")
        s_mask = sem("s_mask")
        s_wi = sem("s_wi")
        s_ks = sem("s_ks")
        s_pt = sem("s_pt")
        s_qs = sem("s_qs")
        s_b = sem("s_b")
        s_hs = sem("s_hs")
        s_cst = sem("s_cst")
        s_hsq = sem("s_hsq")
        s_hm = sem("s_hm")
        s_hr = sem("s_hr")
        s_hn = sem("s_hn")
        s_tr = sem("s_tr")
        s_yf = sem("s_yf")
        s_yh = sem("s_yh")
        s_yl = sem("s_yl")
        s_sc = sem("s_sc")
        s_mx = sem("s_mx")
        s_ex = sem("s_ex")
        s_pn = sem("s_pn")
        s_pt2 = sem("s_pt2")
        s_pa = sem("s_pa")
        s_pv = sem("s_pv")
        s_sqn = sem("s_sqn")
        s_ssq = sem("s_ssq")
        s_nm = sem("s_nm")
        s_ns = sem("s_ns")
        s_nr = sem("s_nr")
        s_rt = sem("s_rt")
        s_xnf = sem("s_xnf")
        s_hf = sem("s_hf")
        s_out = [sem(f"s_out{i}") for i in range(4)]
        s_dve = sem("s_dve")

        Y_FFN = H * TT + H * 4

        block = ctx.enter_context(nc.Block())

        TURN = [9, 10, 14, 16, 20, 23]
        FINISH = [11, 13, 16, 18, 23]

        def last_tile(r):
            if r < KT:
                return r, 0, HALF
            return r % KT, HALF + (r // KT - 1) * (HALF // 2), HALF // 2

        def out_banks(t):
            b = NB + 2 * (t % 2) if t < 6 else 2 * (t % 2)
            return PS[:, b:b + 2, :].rearrange("p a s -> p (a s)")

        def tile_of(t, k0, k1):
            b = X_BANK[t] + k0 // 4
            src = PS[:, b:b + (k1 - k0) // 4, :].rearrange("p a s -> p (a s)").rearrange("p (k s) -> p k s", k=k1 - k0)
            return xT[:, k0:k1, t * P:(t + 1) * P], src

        def lo_ready(eng, c, k):
            who, count = LO[c, k]
            eng.wait_ge({"dve": s_xl, "pool": s_xlp}[who], count)

        def norm_in(c, k):
            at = (c % 2) * HALF
            return XH[:, k, at:at + HALF], XL[:, k, at:at + HALF], xnf[c // 2][PAT[c, k] % 4]

        def strip_lo_ready(eng, n):
            eng.wait_ge(s_wlo, n + 1)
            if n in LO_SHARED:
                eng.wait_ge(s_wlod, LO_SHARED.index(n) + 1)

        def raw_of(n):
            return raw_v[RAW2[n]] if n in RAW2 else raw[:, :]

        def strip_src(kind, h):
            c3 = raw_of(AT[kind, h]).rearrange("p (k n) -> p k n", k=KT)
            r3 = raw_of(AT[kind, h]).rearrange("p (k n) -> p k n", k=2)
            if kind == "qk":
                return [(c3[:, :, 0:DK], cols(a_w_in, h * DK, DK)),
                        (c3[:, :, DK:SW], cols(a_w_in, (H + h) * DK, DK))]
            if kind in ("wo", "xo"):
                return [(r3, rows(a_w_out if kind == "wo" else x_w_o, h * SW))]
            w, at = {"v": (a_w_in, V0), "o": (a_w_in, O0), "mk": (x_w_kv, 0), "mv": (x_w_kv, D),
                     "q": (x_w_q, 0)}[kind]
            return [(c3, cols(w, at + h * SW))]

        @block.sync
        def _(sp):
            def load_strip(n):
                before = [m for m in range(n) if (m in RAW2) == (n in RAW2)]
                if before:
                    strip_lo_ready(sp, before[-1])
                if n == AT["mk", 1]:
                    sp.wait_ge(s_xs, MT)
                    sp.wait_ge(s_sq, TT + MT)
                if n == AT["mv", 0]:
                    sp.wait_ge(s_b, TT * H)
                for dst, src in strip_src(*STRIPS[n]):
                    sp.dma_start(dst, src).then_inc(s_wdma2 if n in RAW2 else s_wdma, 16)

            for t in range(TT):
                if t >= 4:
                    sp.wait_ge(s_turn, t - 3)
                    sp.wait_ge(s_sq, t - 3)
                sp.dma_start(xin[t % 4], x_t[t]).then_inc(s_xin[t % 4], 16)
                if t == 3:
                    for v, at, n in ((norm_x, NORM_X, KT), (norm_ffn, NORM_F, KT), (a_norm, A_NORM, KT), (norm_mix, NORM_M, KT)):
                        sp.dma_start(vrows[at:at + n, :], v[0].rearrange("(k p) -> k p", p=P)).then_inc(s_vec, 16)
                    sp.dma_start(vrows[CONV:CONV + TAPS * KT, :],
                                 a_conv_w[0].rearrange("j (k p) -> (j k) p", p=P)).then_inc(s_vec, 16)
                    load_strip(0)
                    sp.dma_start(wg_raw, cols(a_w_in, G0, 2 * H)).then_inc(s_wg, 16)
                    sp.dma_start(gbias[:, :], a_gate_b[0:1, :].to_broadcast([P, 2 * H])).then_inc(s_gb, 16)
            for n in range(1, NF):
                if n == AT["mk", 0]:
                    sp.wait_ge(s_b, TT * (H - 1))
                    sp.dma_start(gain_mem, norm_mem.rearrange("(o d) -> o d", o=1).to_broadcast([P, D])).then_inc(s_gain, 16)
                    for t in range(MT):
                        sp.dma_start(mxin[:, t, :], mem_t[t]).then_inc(s_min[t], 16)
                load_strip(n)

            def load_ffn(n, w, j, is_rows, i=None):
                k = 0 if i is None else i
                sp.wait_ge(s_wlo, n + PER_LOOP["strip"] * k)
                at = (j + 2 * k) * SW
                if is_rows:
                    src = w[0, bass.ds(at, SW), :].rearrange("(k p) n -> p k n", p=P)
                    dst = raw[:, :].rearrange("p (k n) -> p k n", k=2)
                else:
                    src = w[0, :, bass.ds(at, SW)].rearrange("(k p) n -> p k n", p=P)
                    dst = raw[:, :].rearrange("p (k n) -> p k n", k=KT)
                sp.dma_start(dst, src).then_inc(s_wdma, 16)

            load_ffn(NF, f_w_gate, 0, False)
            load_ffn(NF + 1, f_w_up, 0, False)
            with sp.Fori(0, NJ // 2) as i:
                for u in range(2):
                    n = NF + 2 + 3 * u
                    load_ffn(n, f_w_gate, 1 + u, False, i)
                    load_ffn(n + 1, f_w_down, u, True, i)
                    load_ffn(n + 2, f_w_up, 1 + u, False, i)
            load_ffn(len(STRIPS) - 1, f_w_down, NJ - 1, True)
            sp.wait_ge(s_hf, 4 * NJ)
            sp.dma_start(gain_out, norm_final.rearrange("(o d) -> o d", o=1).to_broadcast([P, D])).then_inc(s_gain, 16)
            for t in range(TT):
                sp.wait_ge(s_xs, MT + t + 1)
                sp.dma_start(out_t[t], fout[t % 4]).then_inc(s_out[t % 4], 16)
            for t in range(4):
                sp.wait_ge(s_out[t], 16 * TT // 4)

        @block.gpsimd
        def _(pool):
            gp = nc.gpsimd
            gp.memset(ident[:, :], 0.0).then_inc(s_const, 1)
            gp.memset(ones[:, :], 1.0).then_inc(s_const, 1)
            gp.memset(tri, 1.0).then_inc(s_const, 1)
            gp.memset(causal[:, :], -LOWEST).then_inc(s_const, 1)
            gp.memset(half_neg[:, :], -0.5).then_inc(s_const, 1)
            gp.memset(YH[:, 0, :].bitcast(F32), 0.0).then_inc(s_const, 1)
            gp.memset(cmax, LOWEST).then_inc(s_const, 1)
            pool.wait_ge(s_const, 7)
            gp.affine_select(out=ident[:, :], in_=ident[:, :], compare_op=ALU.not_equal, fill=1.0, base=0,
                             pattern=[[-1, P]], channel_multiplier=1).then_inc(s_const, 1)
            gp.affine_select(out=causal[:, :], in_=causal[:, :], compare_op=ALU.is_ge, fill=0.0, base=0,
                             pattern=[[1, P]], channel_multiplier=-1).then_inc(s_const, 1)
            gp.affine_select(out=tri, in_=tri, compare_op=ALU.is_ge, fill=0.0, base=0,
                             pattern=[[1, P]], channel_multiplier=-1).then_inc(s_const, 1)

            def rms(t, count):
                pool.wait_ge(s_sq, TT + count)
                gp.tensor_scalar(stat[:, t, 1:2], stat[:, t, 0:1], 1.0 / D, EPS, ALU.mult, ALU.add).then_inc(s_ms, 1)
                pool.wait_ge(s_ms, count)
                gp.tensor_tensor(stat[:, t, 2:3], stat[:, t, 1:2], half_neg[:, 0:1], ALU.pow).then_inc(s_rs, 1)

            def split_lo_half(n, u):
                pool.wait_ge(s_whi, n + 1)
                at = slice(u * KT * P, (u + 1) * KT * P)
                last = gp.tensor_tensor(WL[:, n % 2, at], raw_of(n)[:, at], WH[:, n % 2, at].bitcast(F32), ALU.subtract)
                if u or n in LO_SHARED:
                    last.then_inc(s_wlo, 1)
                elif n == 0:
                    last.then_inc(s_wl0, 1)

            def split_lo(n, i=None):
                k = 0 if i is None else i
                pool.wait_ge(s_whi, n + 1 + PER_LOOP["strip"] * k)
                gp.tensor_tensor(WL[:, n % 2, :], raw[:, :], WH[:, n % 2, :].bitcast(F32),
                                 ALU.subtract).then_inc(s_wlo, 1)

            def scan(h, p):
                if p >= 3:
                    e = h * TT + p - 3
                    pool.wait_ge(s_yh, e + 1)
                    at = (p - 3) * P
                    gp.tensor_tensor(YL[:, :, at:at + P], yf[:, :, :], YH[:, :, at:at + P].bitcast(F32),
                                     ALU.subtract).then_inc(s_yl, 1)
                if 1 <= p <= TT:
                    e = h * TT + p - 1
                    cc = ccol[:, e % 2, :]
                    pool.wait_ge(s_hsq, e + 1)
                    gp.tensor_scalar(cc[:, 3:4], cc[:, 2:3], 1.0 / DV, EPS, ALU.mult, ALU.add).then_inc(s_hm, 1)
                    pool.wait_ge(s_hm, e + 1)
                    if e >= 2:
                        pool.wait_ge(s_hn, e - 1)
                    gp.tensor_tensor(cc[:, 4:5], cc[:, 3:4], half_neg[:, 0:1], ALU.pow).then_inc(s_hr, 1)

            def memnorm(a, b):
                for t in range(MT):
                    rms(t, t + 1)

            def sumsq(which, half):
                c = 2 * which + half
                if which:
                    pool.wait_ge(s_ns, c - 1)
                else:
                    pool.wait_ge(s_sq, NT * (half + 1))
                gp.tensor_scalar(nmean[:, half, :], nsum[:, half, :], 1.0 / D, EPS, ALU.mult, ALU.add).then_inc(s_nm, 1)
                pool.wait_ge(s_nm, c + 1)
                if which:
                    pool.wait_ge(s_rt, c - 1)
                gp.tensor_tensor(nrms[:, half, :], nmean[:, half, :], half_neg[:, :], ALU.pow).then_inc(s_nr, 1)

            def pieces(c, ks):
                for k in ks:
                    if LO[c, k][0] == "pool":
                        hi, lo, full = norm_in(c, k)
                        pool.wait_ge(s_xh, PAT[c, k] + 1)
                        gp.tensor_tensor(lo, full, hi.bitcast(F32), ALU.subtract).then_inc(s_xlp, 1)

            todo = {"scan": scan, "memnorm": memnorm, "sumsq": sumsq, "pieces": pieces}
            for what in ("gates", "memturn", "spread", "attn"):
                todo[what] = lambda a, b: None

            sumsq(0, 0)
            split_lo_half(0, 0)
            pieces(0, range(4))
            split_lo_half(0, 1)
            pieces(0, range(4, KT - 1))
            sumsq(0, 1)
            pieces(0, (KT - 1,))
            pieces(1, range(KT))
            held = []
            for n in range(NF):
                kind, h = STRIPS[n]
                for r in range(NGROUPS[kind]):
                    run_parts(n, r, todo)
                    if r < 2:
                        split_lo_half(n + 1, r)
                    if NGROUPS[kind] == 1:
                        run_parts(n, "mid", todo)
                        if n + 1 not in LO_SHARED:
                            split_lo_half(n + 1, 1)
                run_parts(n, "end", todo)

            def ffn_lo(j, i=None, rs=range(4)):
                k = 0 if i is None else i
                for r in rs:
                    c = 4 * j + r
                    pool.wait_ge(s_yh, Y_FFN + c + 1 + 8 * k)
                    nt, at = r % 2, (r // 2) * HALF
                    gp.tensor_tensor(YL[:, nt, at:at + HALF], acc[:, r % 2, :],
                                     YH[:, nt, at:at + HALF].bitcast(F32), ALU.subtract).then_inc(s_yl, 1)

            split_lo(NF + 1)
            sumsq(2, 1)
            ffn_lo(0, rs=(0,))
            pieces(5, range(6))
            ffn_lo(0, rs=(1,))
            pieces(5, range(6, KT))
            split_lo(NF + 2)
            ffn_lo(0, rs=(2, 3))
            with pool.Fori(0, NJ // 2) as i:
                for u in range(2):
                    n = NF + 2 + 3 * u
                    split_lo(n + 1, i)
                    split_lo(n + 2, i)
                    split_lo(n + 3, i)
                    ffn_lo(1 + u, i)
            for t in range(TT):
                rms(t, MT + t + 1)

        @block.scalar
        def _(act):
            sc = nc.scalar

            def split_hi(n, i=None):
                k = 0 if i is None else i
                act.wait_ge((s_wdma, s_wdma2)[DMAS[n][0]], 16 * DMAS[n][1] + 16 * PER_LOOP["strip"] * k)
                if n >= 2:
                    act.wait_ge(s_mm, used(n - 2) + PER_LOOP["group"] * k)
                sc.activation(WH[:, n % 2, :], raw_of(n), ACT.Copy).then_inc(s_whi, 1)

            def square_tile(t, src, junk_out, count, dst=None):
                if count > 1:
                    act.wait_ge(s_sq, count - 1)
                sc.activation(junk_out, src, ACT.Square, accum_out=stat[:, t, 0:1] if dst is None else dst).then_inc(s_sq, 1)

            def gates(step, b):
                if step == 1:
                    act.wait_ge(s_gd, 1)
                    sc.activation(gt1[:, :], gt2[:, :], ACT.Exp).then_inc(s_ga, 1)
                    act.wait_ge(s_ga, 1)
                    sc.activation(gt2[:, :], gt1[:, :], ACT.Ln, bias=1.0).then_inc(s_ga, 1)
                if step == 4:
                    act.wait_ge(s_gd, 5)
                    sc.activation(decay[:, :], gt1[:, :], ACT.Exp).then_inc(s_ga, 1)
                    sc.activation(wa[:, :], gt2[:, :], ACT.Exp).then_inc(s_ga, 1)
                if step == 5:
                    act.wait_ge(s_gd, 6)
                    sc.activation(emm[:, :], mulast[:, :], ACT.Exp, scale=-1.0).then_inc(s_ga, 1)

            def scan(h, p):
                if p >= 3:
                    e = h * TT + p - 3
                    act.wait_ge(s_yf, e + 1)
                    if p == 3 and h >= 1:
                        act.wait_ge(s_mm, used(AT["wo", h - 1]))
                    at = (p - 3) * P
                    sc.activation(YH[:, :, at:at + P], yf[:, :, :], ACT.Copy).then_inc(s_yh, 1)
                if p < TT:
                    e = h * TT + p
                    if e == 0:
                        act.wait_ge(s_ga, 5)
                        act.wait_ge(s_gd, 6)
                    act.wait_ge(s_mu, e + 1)
                    if e >= 1:
                        act.wait_ge(s_pt, e)
                        act.wait_ge(s_qs, e)
                        act.wait_ge(s_b, e)
                    sc.activation(wT[:, :], X0[:, 0:P], ACT.Exp, scale=-1.0, bias=acol[:, e:e + 1]).then_inc(s_wt, 1)
                    sc.activation(wi[:, :], X0[:, 0:P], ACT.Exp, scale=-1.0, bias=mprev[:, e:e + 1]).then_inc(s_wi, 1)
                    sc.activation(ks[:, :], X0[:, P:2 * P], ACT.Copy, scale=wa[:, e:e + 1]).then_inc(s_ks, 1)
                if 1 <= p <= TT:
                    e = h * TT + p - 1
                    act.wait_ge(s_hs, e + 1)
                    if e >= 1:
                        act.wait_ge(s_hsq, e)
                    if e >= 2:
                        act.wait_ge(s_hm, e - 1)
                    sc.activation(hsj[:, :], hs[:, e % 2, :], ACT.Square, accum_out=ccol[:, e % 2, 2:3]).then_inc(s_hsq, 1)

            def memnorm(a, b):
                for t in range(MT):
                    act.wait_ge(s_min[t], 16)
                    if t == 0:
                        act.wait_ge(s_b, TT * (H - 1))
                    square_tile(t, mxin[:, t, :], mjunk, TT + t + 1)

            def memturn(a, b):
                act.wait_ge(s_mm, used(AT["o", H - 1]))
                for t in range(MT):
                    act.wait_ge(s_turn, TT + t + 1)
                    for q in range(2):
                        sc.activation(MH[:, 4 * q:4 * q + 4, t * P:(t + 1) * P],
                                      PS[:, NB + 2 * t + q, :].rearrange("p (k s) -> p k s", k=4),
                                      ACT.Copy).then_inc(s_mh, 1)

            def square(n, r):
                which, half, k = ("wo", "xo").index(STRIPS[n][0]) + 1, r // KT, r % KT
                adds = (KT - 1) * (2 * (which - 1) + half)
                act.wait_ge(s_fd, FREED[FIRST[n] + r][1])
                if r == 0 and which == 1:
                    act.wait_ge(s_yf, H * TT)
                if r == 0 and which == 2:
                    act.wait_ge(s_sc, H * 4)
                if k >= 3:
                    act.wait_ge(s_sacc, adds + k - 2)
                if k in (1, 2) and adds:
                    act.wait_ge(s_sacc, adds)
                sc.activation(sqb[which][:, k % 2, :] if k else sqsum[which][:, half, :],
                              xT[:, k, half * HALF:(half + 1) * HALF], ACT.Square).then_inc(s_sqn, 1)

            def pieces(c, ks):
                for k in ks:
                    if c == 2 and k == EARLY[0]:
                        act.wait_ge(s_mm, used(AT["o", H - 1]))
                    if c == 2 and k == LATE[0]:
                        act.wait_ge(s_mm, used(AT["mv", H - 1]))
                    if c == 4 and k == 0:
                        act.wait_ge(s_mm, used(AT["q", H - 1]))
                    act.wait_ge(s_xnf, PAT[c, k] + 1)
                    hi, lo, full = norm_in(c, k)
                    sc.activation(hi, full, ACT.Copy).then_inc(s_xh, 1)

            def attn(h, p):
                if p < 4:
                    e = 4 * h + p
                    act.wait_ge(s_mx, e + 1)
                    if e >= 2:
                        act.wait_ge(s_pt2, e - 1)
                    for j in range(2):
                        sc.activation(ptok[:, e % 2, j * M:(j + 1) * M], PS[:, NB + e % 2, j * M:(j + 1) * M], ACT.Exp,
                                      scale=XSCALE, bias=acol8[:, e % 2, 2 + j:3 + j],
                                      accum_out=acol8[:, e % 2, 4 + j:5 + j]).then_inc(s_ex, 1)
                if p in (3, 5):
                    for dt in range(2):
                        c = 4 * h + 2 * (p // 2 - 1) + dt
                        act.wait_ge(s_pv, c + 1)
                        if dt == 0:
                            n = AT["wo", H - 1] if h == 0 else AT["xo", h - 1]
                            act.wait_ge(s_mm, FIRST[n] + KT if p == 3 else used(n))
                        at = (p // 2 - 1) * HALF
                        sc.activation(YH[:, dt, at:at + HALF], (X3, X0)[dt], ACT.Copy).then_inc(s_yh, 1)

            todo = {"gates": gates, "scan": scan, "memnorm": memnorm, "memturn": memturn,
                    "pieces": pieces, "attn": attn}
            for what in ("sumsq", "spread"):
                todo[what] = lambda a, b: None

            def evac(n, r):
                kind, h = STRIPS[n]
                g = FIRST[n] + r
                bank = PS[:, g % NB, :]
                if kind == "qk":
                    c = 4 * h + r
                    act.wait_ge(s_conv, c + 1)
                    if r == 0 and h >= 2:
                        act.wait_ge(s_b, TT * (h - 1))
                    at = (r // 2) * HALF
                    sc.activation(QK[:, h % 2, r % 2, at:at + HALF], acc[:, r % 2, :], ACT.Tanh, scale=0.5).then_inc(s_ex1, 1)
                    return
                if kind not in BY_ACT:
                    return
                act.wait_ge(s_mm, g + 1)
                if kind == "v":
                    if r == 0 and h >= 2:
                        act.wait_ge(s_b, TT * (h - 1))
                    sc.activation(VV[:, h % 2, 2 * r:2 * r + 2, 0:DV], bank.rearrange("p (t d) -> p t d", t=2),
                                  ACT.Copy).then_inc(s_fa, 1)
                elif kind == "o":
                    if r == 0 and h == 0:
                        act.wait_ge(s_gd, 5)
                    if r == 0 and h >= 1:
                        act.wait_ge(s_yf, TT * h)
                    sc.activation(SG[:, r % 2, (r // 2) * HALF:(r // 2 + 1) * HALF], bank,
                                  ACT.Tanh, scale=0.5).then_inc(s_fa, 1)
                elif kind == "mk":
                    if h == 0:
                        act.wait_ge(s_turn, TT + MT)
                        act.wait_ge(s_xs, MT)
                    sc.activation(KM[:, 2 * h:2 * h + 2, :], bank.rearrange("p (t d) -> p t d", t=2),
                                  ACT.Copy).then_inc(s_fa, 1)
                elif kind == "mv":
                    sc.activation(VM[:, :, h * SW:(h + 1) * SW], bank.rearrange("p (t d) -> p t d", t=2),
                                  ACT.Copy).then_inc(s_fa, 1)
                elif kind == "q":
                    if r == 0 and h == 0:
                        act.wait_ge(s_b, TT * H)
                    if r == 0 and h == 1:
                        act.wait_ge(s_xl, LO[3, LATE[1]][1])
                    if r == 0 and h >= 2:
                        act.wait_ge(s_sc, 4 * (h - 1))
                    sc.activation(QH[h % 2][:, r % 2, (r // 2) * HALF:(r // 2 + 1) * HALF], bank,
                                  ACT.Copy).then_inc(s_fa, 1)

            def square_x(t):
                act.wait_ge(s_xin[t % 4], 16 * (t // 4 + 1))
                square_tile(t, xin[t % 4], junk, t + 1, nsum[:, t // NT, t % NT:t % NT + 1])

            def half_tile(t):
                act.wait_ge(s_turn, t + 1)
                dst, src = tile_of(t, 0, 4)
                sc.activation(dst, src, ACT.Copy).then_inc(s_xta, 1)

            square_x(0)
            square_x(1)
            square_x(2)
            square_x(3)
            split_hi(0)
            for k in range(KT):
                pieces(0, (k,))
                if k in (1, 3, 4, 5):
                    square_x({1: 4, 3: 5, 4: 6, 5: 7}[k])
                if k in (1, 3, 4, 5):
                    half_tile({1: 4, 3: 5, 4: 6, 5: 7}[k])
            pieces(1, range(KT))
            held = []
            for n in range(NF):
                kind, h = STRIPS[n]
                for r in range(NGROUPS[kind]):
                    run_parts(n, r, todo)
                    if r == 0:
                        split_hi(n + 1)
                        if held:
                            evac(*held.pop())
                    if NGROUPS[kind] == 1:
                        run_parts(n, "mid", todo)
                    if kind == "o" and h >= 1:
                        if r == 3:
                            for q in range(4):
                                evac(n, q)
                    elif (kind, h) == ("wo", H - 1) or (kind, h) == ("xo", H - 1) and r < KT:
                        square(n, r)
                    elif kind == "mv":
                        held.append((n, r))
                    else:
                        evac(n, r)
                run_parts(n, "end", todo)

            def silu_first(r):
                g = GI[NF, r]
                act.wait_ge(s_mm, g + 1)
                if r == 2:
                    act.wait_ge(s_ssq, 4)
                sc.activation(SG[:, r % 2, (r // 2) * HALF:(r // 2 + 1) * HALF], PS[:, g % NB, :], ACT.Silu).then_inc(s_fa, 1)

            def gate_evac(n, j, i):
                for r in range(4):
                    g = FIRST[n] + r
                    act.wait_ge(s_mm, g + 1 + PER_LOOP["group"] * i)
                    if r == 0:
                        act.wait_ge(s_hf, 4 * j + 8 * i)
                    sc.activation(SG[:, r % 2, (r // 2) * HALF:(r // 2 + 1) * HALF], PS[:, g % NB, :],
                                  ACT.Silu).then_inc(s_fa, 1)

            def ffn_hi(j, down, i=None, rs=range(4)):
                k = 0 if i is None else i
                for r in rs:
                    act.wait_ge(s_hf, 4 * j + r + 1 + 8 * k)
                    if r == 0:
                        act.wait_ge(s_mm, used(down) + PER_LOOP["group"] * k)
                    nt, at = r % 2, (r // 2) * HALF
                    sc.activation(YH[:, nt, at:at + HALF], acc[:, r % 2, :], ACT.Copy).then_inc(s_yh, 1)

            for r in range(KT, 2 * KT):
                square(NF - 1, r)
                if r == KT + 2:
                    split_hi(NF + 1)
            silu_first(0)
            silu_first(1)
            ffn_hi(0, NF - 1, rs=(0,))
            pieces(5, range(6))
            ffn_hi(0, NF - 1, rs=(1,))
            pieces(5, range(6, KT))
            silu_first(2)
            silu_first(3)
            split_hi(NF + 2)
            ffn_hi(0, NF - 1, rs=(2, 3))
            with act.Fori(0, NJ // 2) as i:
                for u in range(2):
                    n = NF + 2 + 3 * u
                    split_hi(n + 1, i)
                    gate_evac(n, 1 + u, i)
                    split_hi(n + 2, i)
                    split_hi(n + 3, i)
                    ffn_hi(1 + u, n + 1, i)
            for t in range(TT):
                act.wait_ge(s_turn, TT + MT + t + 1)
                square_tile(t, out_banks(t), junk, TT + MT + t + 1)

        @block.vector
        def _(dve):
            v = nc.vector
            steps = [0]

            def link(ins):
                steps[0] += 1
                ins.then_inc(s_dve, 1)
                dve.wait_ge(s_dve, steps[0])

            def gates(step, b):
                if step == 0:
                    dve.wait_ge(s_gpe, 1)
                    v.tensor_copy(grow.rearrange("p (a s) -> p a s", a=NHALF), PS[0:4 * H, NB:NB + 2, :]).then_inc(s_gr, 1)
                if step == 1:
                    dve.wait_ge(s_gpe, 2)
                    dve.wait_ge(s_gb, 16)
                    z = X2[:, 0:TT * 4 * H].rearrange("p (c g) -> p g c", g=4 * H)
                    zl = gsum.rearrange("p (g c) -> p g c", g=2 * H)
                    link(v.tensor_copy(zl, z[:, 2 * H:]))
                    link(v.tensor_tensor(zl, z[:, 0:2 * H], zl, ALU.add))
                    z = zl
                    gb = gbias[:, :].rearrange("p (g o) -> p g o", o=1).to_broadcast([P, 2 * H, TT])
                    v.tensor_tensor(ig[:, :].rearrange("p (g c) -> p g c", g=H), z[:, 0:H], gb[:, 0:H], ALU.add)
                    link(v.tensor_tensor(lf[:, :].rearrange("p (g c) -> p g c", g=H), z[:, H:], gb[:, H:], ALU.add))
                    v.scalar_tensor_tensor(out=gt2[:, :], in0=lf[:, :], scalar=-1.0, in1=lf[:, :], op0=ALU.mult,
                                           op1=ALU.min).then_inc(s_gd, 1)
                    link(v.tensor_scalar(lf[:, :], lf[:, :], 0.0, None, ALU.min))
                    dve.wait_ge(s_ga, 2)
                    v.tensor_tensor(lf[:, :], lf[:, :], gt2[:, :], ALU.subtract).then_inc(s_gd, 1)
                if step == 2:
                    dve.wait_ge(s_gpe, 3)
                    v.tensor_copy(bcum[:, :], X1[:, 0:R])
                    link(v.tensor_copy(gtot[:, :], X1[:, R:2 * R]))
                    v.tensor_tensor(acol[:, :], ig[:, :], bcum[:, :], ALU.subtract).then_inc(s_gd, 1)
                if step == 3:
                    dve.wait_ge(s_gpe, 4)
                    link(v.tensor_copy(cmax[:, 0, 64:], X2[0:R, 0:P]))
                    s, a = 1, 0
                    while s < P:
                        link(v.tensor_tensor(cmax[:, 1 - a, 64:], cmax[:, a, 64:], cmax[:, a, 64 - s:64 + P - s], ALU.max))
                        s, a = 2 * s, 1 - a
                    v.tensor_scalar(gt1[0:R, :], ident[0:R, 0:R], cmax[:, a, 64 + P - 1:64 + P], None,
                                    ALU.mult).then_inc(s_gd, 1)
                if step == 4:
                    dve.wait_ge(s_gpe, 5)
                    link(v.tensor_copy(mlast[:, :], X3[:, 0:R]))
                    hc = lambda t: t[:, :].rearrange("p (h c) -> p h c", h=H)
                    link(v.memset(hc(mprev)[:, :, 0:1], 0.0))
                    for c in range(TT - 1):
                        link(v.tensor_tensor(hc(mulast)[:, :, c:c + 1], hc(mprev)[:, :, c:c + 1], hc(mlast)[:, :, c:c + 1], ALU.max))
                        link(v.tensor_tensor(hc(mprev)[:, :, c + 1:c + 2], hc(mulast)[:, :, c:c + 1], hc(gtot)[:, :, c:c + 1], ALU.add))
                    link(v.tensor_tensor(mulast[:, :], mprev[:, :], mlast[:, :], ALU.max))
                    v.tensor_tensor(gt1[:, :], mprev[:, :], mulast[:, :], ALU.subtract)
                    link(v.tensor_tensor(gt2[:, :], acol[:, :], mulast[:, :], ALU.subtract))
                    link(v.tensor_tensor(ig[0:R, :], mprev[0:R, :], ident[0:R, 0:R], ALU.mult))
                    link(v.tensor_reduce(mprow[:, :], ig[0:R, :], AX, ALU.add))
                    a = 1
                    v.tensor_scalar(murow[:, :], cmax[:, a, 64:], mprow[:, 0:1], None, ALU.max).then_inc(s_gd, 1)
                if step == 5:
                    dve.wait_ge(s_gpe, 6)
                    dve.wait_ge(s_ga, 4)
                    v.tensor_copy(mucol, X3[:, R:2 * R])
                    v.tensor_tensor(mulast[:, :], bcum[:, :], X3[:, R:2 * R], ALU.add).then_inc(s_gd, 1)

            def scan(h, p):
                if 2 <= p <= TT + 1:
                    e = h * TT + p - 2
                    dve.wait_ge(s_hr, e + 1)
                    v.tensor_scalar(hs[:, e % 2, :], hs[:, e % 2, :], ccol[:, e % 2, 4:5], None, ALU.mult).then_inc(s_hn, 1)
                if p >= 3:
                    e, at = h * TT + p - 3, (p - 3) * P
                    dve.wait_ge(s_tr, e + 1)
                    dve.wait_ge(s_st, h * TT + min(p + 1, TT))
                    if p == 3:
                        dve.wait_ge(s_sg, 4 * (h + 1))
                    if e >= 1:
                        dve.wait_ge(s_yl, e)
                    for kk in range(2):
                        gain = vcols[:, A_NORM + 2 * h + kk:A_NORM + 2 * h + kk + 1]
                        last = v.scalar_tensor_tensor(out=yf[:, kk, :], in0=X1[:, kk * P:(kk + 1) * P], scalar=gain,
                                                      in1=SG[:, kk, at:at + P], op0=ALU.mult, op1=ALU.mult)
                    last.then_inc(s_yf, 1)
                if p < TT:
                    e = h * TT + p
                    dve.wait_ge(s_wt, e + 1)
                    v.tensor_tensor(wT[:, :], wT[:, :], causal[:, :], ALU.min).then_inc(s_mask, 1)
                    dve.wait_ge(s_st, e + 1)
                    dve.wait_ge(s_mask, e + 1)
                    if e >= 1:
                        dve.wait_ge(s_b, e)
                    v.scalar_tensor_tensor(out=wT[:, :], in0=X1[:, 2 * P:3 * P], scalar=QSCALE, in1=wT[:, :], op0=ALU.mult,
                                           op1=ALU.mult).then_inc(s_pt, 1)
                    dve.wait_ge(s_wi, e + 1)
                    if p == 0:
                        dve.wait_ge(s_qk, 4 * (h + 1))
                    v.scalar_tensor_tensor(out=qs[:, :], in0=QK[:, h % 2, 0, p * P:(p + 1) * P], scalar=QSCALE,
                                           in1=wi[:, :], op0=ALU.mult, op1=ALU.mult).then_inc(s_qs, 1)
                if 1 <= p <= TT:
                    e, c = h * TT + p - 1, p - 1
                    cc = ccol[:, e % 2, :]
                    dve.wait_ge(s_b, e + 1)
                    if c == 0:
                        v.tensor_copy(Cst[:, :], X3[:, 0:DV + 1]).then_inc(s_cst, 1)
                    elif c < TT - 1:
                        dve.wait_ge(s_cst, h * (TT - 1) + c)
                        v.scalar_tensor_tensor(out=Cst[:, :], in0=Cst[:, :], scalar=decay[:, e:e + 1],
                                               in1=X3[:, 0:DV + 1], op0=ALU.mult, op1=ALU.add).then_inc(s_cst, 1)
                    link(v.tensor_scalar(cc[:, 0:1], X2[:, DV:DV + 1], -1.0, emm[:, e:e + 1], ALU.mult, ALU.max))
                    link(v.tensor_tensor(cc[:, 1:2], X2[:, DV:DV + 1], cc[:, 0:1], ALU.max))
                    link(v.reciprocal(cc[:, 5:6], cc[:, 1:2]))
                    if e >= 2:
                        dve.wait_ge(s_tr, e - 1)
                    v.tensor_scalar(hs[:, e % 2, :], X2[:, 0:DV], cc[:, 5:6], None, ALU.mult).then_inc(s_hs, 1)

            def finish_qk(h, r):
                c, at = 4 * h + r, (r // 2) * HALF
                dst = QK[:, h % 2, r % 2, at:at + HALF]
                dve.wait_ge(s_ex1, c + 1)
                v.scalar_tensor_tensor(out=dst, in0=dst, scalar=1.0, in1=acc[:, r % 2, :], op0=ALU.add,
                                       op1=ALU.mult).then_inc(s_qk, 1)

            def finish_o(n, r):
                dst = SG[:, r % 2, (r // 2) * HALF:(r // 2 + 1) * HALF]
                dve.wait_ge(s_fa, FREED[FIRST[n] + r][1])
                v.tensor_scalar(dst, dst, 0.5, 0.5, ALU.mult, ALU.add).then_inc(s_sg, 1)

            def memnorm(a, b):
                dve.wait_ge(s_gain, 16)
                for t in range(MT):
                    dve.wait_ge(s_rs, t + 1)
                    v.scalar_tensor_tensor(out=mxs[:, t, :], in0=mxin[:, t, :], scalar=stat[:, t, 2:3], in1=gain_mem,
                                           op0=ALU.mult, op1=ALU.mult).then_inc(s_xs, 1)

            def memturn(a, b):
                for t in range(MT):
                    for q in range(2):
                        dve.wait_ge(s_mh, 2 * t + q + 1)
                        at = slice(t * P, (t + 1) * P)
                        v.tensor_tensor(ML[:, 4 * q:4 * q + 4, at], PS[:, NB + 2 * t + q, :].rearrange("p (k s) -> p k s", k=4),
                                        MH[:, 4 * q:4 * q + 4, at].bitcast(F32), ALU.subtract).then_inc(s_ml, 1)

            def add_squares(which, half, k):
                before = 2 * (which - 1) + half
                dve.wait_ge(s_sqn, KT * before + k + 1)
                if k > 1:
                    dve.wait_ge(s_sacc, (KT - 1) * before + k - 1)
                total = sqsum[which][:, half, :]
                v.tensor_tensor(total, total, sqb[which][:, k % 2, :], ALU.add).then_inc(s_sacc, 1)

            def sumsq(which, half):
                c = 2 * which + half
                dve.wait_ge(s_ssq, c - 1)
                dve.wait_ge(s_nm, c - 1)
                v.tensor_copy(nsum[:, half, :], X2[:, 0:NT]).then_inc(s_ns, 1)

            waiting = []

            def make_lo():
                c, k = waiting.pop()
                hi, lo, full = norm_in(c, k)
                dve.wait_ge(s_xh, PAT[c, k] + 1)
                v.tensor_tensor(lo, full, hi.bitcast(F32), ALU.subtract).then_inc(s_xl, 1)

            def pieces(c, ks):
                for k in ks:
                    i = PAT[c, k]
                    if k == (EARLY if c in (2, 3) else range(KT))[0]:
                        dve.wait_ge(s_rt, c + 1)
                        if c == 1:
                            dve.wait_ge(s_xta, 4)
                    if i >= 4:
                        lo_ready(dve, *PIECES[i - 4])
                    hi, lo, full = norm_in(c, k)
                    gain = (NORM_M, NORM_X, NORM_F)[c // 2] + k
                    v.scalar_tensor_tensor(out=full, in0=xT[:, k, (c % 2) * HALF:(c % 2 + 1) * HALF],
                                           scalar=vcols[:, gain:gain + 1], in1=PS[:, BC[c], :], op0=ALU.mult,
                                           op1=ALU.mult).then_inc(s_xnf, 1)
                    if waiting:
                        make_lo()
                    if LO[c, k][0] == "dve":
                        waiting.append((c, k))
                    if (c, k) in ((0, KT - 1), (1, KT - 1), (3, LATE[1])) and waiting:
                        make_lo()

            def attn(h, p):
                if 1 <= p <= 4:
                    e = 4 * h + p - 1
                    dve.wait_ge(s_ex, 2 * (e + 1))
                    link(v.reciprocal(acol8[:, e % 2, 6:8], acol8[:, e % 2, 4:6]))
                    for j in range(2):
                        last = v.tensor_scalar(ptok[:, e % 2, j * M:(j + 1) * M], ptok[:, e % 2, j * M:(j + 1) * M],
                                               acol8[:, e % 2, 6 + j:7 + j], None, ALU.mult)
                    last.then_inc(s_pn, 1)
                if p < 4:
                    e = 4 * h + p
                    dve.wait_ge(s_sc, e + 1)
                    link(v.tensor_reduce(acol8[:, e % 2, 0:2], PS[:, NB + e % 2, :].rearrange("p (j m) -> p j m", j=2), AX, ALU.max))
                    v.tensor_scalar(acol8[:, e % 2, 2:4], acol8[:, e % 2, 0:2], -XSCALE, None, ALU.mult).then_inc(s_mx, 1)
                if 1 <= p <= 4:
                    e = 4 * h + p - 1
                    dve.wait_ge(s_pt2, e + 1)
                    if h >= 1 and p == 1:
                        dve.wait_ge(s_pv, 4 * h)
                    if h == 0 and p == 1:
                        dve.wait_ge(s_ssq, 2)
                    v.tensor_copy(PA[:, :, (p - 1) * SW:p * SW], X2[:, :].rearrange("p (m s) -> p m s", m=MT)).then_inc(s_pa, 1)
                if p in (3, 5):
                    for dt in range(2):
                        c = 4 * h + 2 * (p // 2 - 1) + dt
                        dve.wait_ge(s_yh, H * TT + c + 1)
                        at = (p // 2 - 1) * HALF
                        v.tensor_tensor(YL[:, dt, at:at + HALF], (X3, X0)[dt], YH[:, dt, at:at + HALF].bitcast(F32),
                                        ALU.subtract).then_inc(s_yl, 1)

            todo = {"gates": gates, "scan": scan, "memnorm": memnorm, "memturn": memturn,
                    "sumsq": sumsq, "spread": lambda a, b: None, "pieces": pieces, "attn": attn}

            def add_residual(g, r, k=0):
                dve.wait_ge(s_mm, g + 1 + PER_LOOP["group"] * k)
                xt = xT[:, r % KT, (r // KT) * HALF:(r // KT + 1) * HALF]
                v.tensor_tensor(xt, PS[:, g % NB, :], xt, ALU.add).then_inc(s_fd, 1)

            def evac(n, r):
                kind, h = STRIPS[n]
                g = FIRST[n] + r
                if kind == "qk":
                    c, a, half = 4 * h + r, acc[:, r % 2, :], r // 2
                    bank = PS[:, g % NB, :]
                    tap = lambda j: vcols[:, CONV + KT * j + (r % 2) * H + h:CONV + KT * j + (r % 2) * H + h + 1]
                    dve.wait_ge(s_mm, g + 1)
                    if c >= 2:
                        dve.wait_ge(s_qk, c - 1)
                    link(v.tensor_scalar(a, bank, tap(TAPS - 1), None, ALU.mult))
                    for j in range(TAPS - 2, -1, -1):
                        lag = TAPS - 1 - j
                        ins = v.scalar_tensor_tensor(out=a[:, lag:], in0=bank[:, 0:HALF - lag], scalar=tap(j),
                                                     in1=a[:, lag:], op0=ALU.mult, op1=ALU.add)
                        if half:
                            link(ins)
                            ins = v.scalar_tensor_tensor(out=a[:, 0:lag], in0=halo[:, r % 2, TAPS - 1 - lag:], scalar=tap(j),
                                                         in1=a[:, 0:lag], op0=ALU.mult, op1=ALU.add)
                        if j:
                            link(ins)
                    ins.then_inc(s_conv, 1)
                    dve.wait_ge(s_conv, c + 1)
                    v.tensor_copy(halo[:, r % 2, :], bank[:, HALF - TAPS + 1:]).then_inc(s_fd, 1)
                    if r:
                        finish_qk(h, r - 1)
                elif kind == "v" and r == 0:
                    finish_qk(h, 3)
                elif kind == "o" and r == 3:
                    for q in range(4):
                        finish_o(n, q)
                elif kind not in BY_ACT:
                    add_residual(g, r)

            def out_of_psum(t, k0):
                dve.wait_ge(s_turn, t + 1)
                dst, src = tile_of(t, k0, KT)
                v.tensor_copy(dst, src).then_inc(s_xt, 1)

            for t in range(4):
                out_of_psum(t, 0)
            dve.wait_ge(s_vturn, 1)
            v.tensor_copy(vcols[:, :], PS[:, 2, 0:NVEC]).then_inc(s_vc, 1)
            dve.wait_ge(s_vc, 1)
            for k in range(KT):
                pieces(0, (k,))
                if k in (1, 3, 4, 5):
                    out_of_psum({1: 4, 3: 5, 4: 6, 5: 7}[k], 4)
            pieces(1, range(KT))
            dve.wait_ge(s_wg, 16)
            dve.wait_ge(s_const, 10)
            link(v.tensor_copy(wgp[:, :, 0:2 * H], wg_raw))
            v.tensor_tensor(wgp[:, :, 2 * H:4 * H], wg_raw, wgp[:, :, 0:2 * H].bitcast(F32), ALU.subtract).then_inc(s_wgs, 1)
            lo_ready(dve, 1, KT - 2)
            lo_ready(dve, 1, KT - 1)
            dve.wait_ge(s_sq, TT)
            for par in range(2):
                v.memset(VV[:, par, :, DV:DV + 1], 1.0).then_inc(s_ones, 1)
            for n in range(NF):
                kind, h = STRIPS[n]
                with_squares = kind in ("wo", "xo") and h == H - 1
                which = 1 if kind == "wo" else 2
                for r in range(NGROUPS[kind]):
                    run_parts(n, r, todo)
                    if kind == "mk":
                        run_parts(n, "mid", todo)
                    if n + 1 in LO_SHARED and r == 0:
                        dve.wait_ge(s_whi, n + 2)
                        v.tensor_tensor(WL[:, (n + 1) % 2, KT * P:], raw_of(n + 1)[:, KT * P:],
                                        WH[:, (n + 1) % 2, KT * P:].bitcast(F32), ALU.subtract).then_inc(s_wlod, 1)
                    if kind == "mv":
                        run_parts(n, "mid", todo)
                    evac(n, r)
                    if with_squares and (r - 1) % KT and 1 < r <= (2 * KT if which == 1 else KT):
                        add_squares(which, (r - 1) // KT, (r - 1) % KT)
                if with_squares and which == 1:
                    add_squares(1, 1, KT - 1)
                run_parts(n, "end", todo)

            def up_evac(n, j, i=None, rs=range(4)):
                k = 0 if i is None else i
                for r in rs:
                    g = GI[n, r]
                    dve.wait_ge(s_mm, g + 1 + PER_LOOP["group"] * k)
                    dve.wait_ge(s_fa, FREED[GI[AT["gate", j], r]][1] + PER_LOOP["act"] * k)
                    if j >= 1 or r >= 2:
                        dve.wait_ge(s_yl, Y_FFN + 4 * j + r - 1 + 8 * k)
                    ins = v.tensor_tensor(acc[:, r % 2, :], PS[:, g % NB, :],
                                          SG[:, r % 2, (r // 2) * HALF:(r // 2 + 1) * HALF], ALU.mult)
                    ins.then_inc(s_hf, 1)

            def down_evac(n, i=None):
                for r in range(16):
                    add_residual(FIRST[n] + r, r, 0 if i is None else i)

            for k in range(1, KT):
                add_squares(2, 1, k)
            sumsq(2, 1)
            up_evac(NF + 1, 0, rs=(0,))
            pieces(5, range(6))
            up_evac(NF + 1, 0, rs=(1,))
            pieces(5, range(6, KT))
            up_evac(NF + 1, 0, rs=(2, 3))
            with dve.Fori(0, NJ // 2) as i:
                for u in range(2):
                    n = NF + 2 + 3 * u
                    down_evac(n + 1, i)
                    up_evac(n + 2, 1 + u, i)
            def finish_out(t):
                dve.wait_ge(s_rs, MT + t + 1)
                if t >= 4:
                    dve.wait_ge(s_out[t % 4], 16 * (t // 4))
                v.scalar_tensor_tensor(out=fout[t % 4], in0=out_banks(t), scalar=stat[:, t, 2:3], in1=gain_out,
                                       op0=ALU.mult, op1=ALU.mult).then_inc(s_xs, 1)

            n = len(STRIPS) - 1
            dve.wait_ge(s_gain, 32)
            for r in range(24):
                ft, at, width = last_tile(r)
                dve.wait_ge(s_mm, FIRST[n] + r + 1)
                xt = xT[:, ft, at:at + width]
                v.tensor_tensor(xt, PS[:, (FIRST[n] + r) % NB, 0:width], xt, ALU.add).then_inc(s_fd, 1)
                if r in FINISH:
                    finish_out(FINISH.index(r))
            for t in range(len(FINISH), TT):
                finish_out(t)

        @block.tensor
        def _(pe):
            mm = nc.tensor.matmul

            def wait_strip(n, k=0):
                pe.wait_ge(s_whi, n + 1 + PER_LOOP["strip"] * k)
                if n in LO_SHARED:
                    strip_lo_ready(pe, n)
                else:
                    pe.wait_ge(s_wlo, n + 1 + PER_LOOP["strip"] * k)

            def wait_bank(g, k=0):
                if g >= NB:
                    who, count = FREED[g - NB]
                    if STRIPS[GROUPS[g][0]] == ("gate", 1) and who == "act":
                        who, count = FREED[GI[NF + 1, GROUPS[g][1]]]
                    pe.wait_ge({"act": s_fa, "dve": s_fd, "up": s_hf}[who], count + PER_LOOP[who] * k)

            def product(dst, tiles, before=None):
                for k, ((wh, wl), (xh, xl)) in enumerate(tiles):
                    if before is not None:
                        lo_ready(pe, before, (EARLY + LATE)[k])
                    mm(dst, wh, xh, start=(k == 0), stop=False)
                    mm(dst, wh, xl, start=False, stop=False)
                    last = mm(dst, wl, xh, start=False, stop=(k == len(tiles) - 1))
                return last

            def col(n, k, nt, width=P):
                at = k * SW + nt * width
                return WH[:, n % 2, at:at + width], WL[:, n % 2, at:at + width]

            def rowt(n, kk, ft):
                at = kk * D + ft * P
                return WH[:, n % 2, at:at + P], WL[:, n % 2, at:at + P]

            def xpart(k, at, width):
                return XH[:, k, at:at + width], XL[:, k, at:at + width]

            def mpart(k, at, width):
                return MH[:, k, at:at + width], ML[:, k, at:at + width]

            def group(n, r, k=0, before=None, mid=None):
                kind, h = STRIPS[n]
                g = GI[n, r]
                bank = PS[:, g % NB, :]
                wait_bank(g, k)
                if kind in ("wo", "xo", "down"):
                    at = (r // KT) * HALF
                    last = product(bank, [(rowt(n, kk, r % KT), (YH[:, kk, at:at + HALF], YL[:, kk, at:at + HALF]))
                                          for kk in range(2)])
                elif kind == "v":
                    for t in range(2):
                        at = (2 * r + t) * P
                        last = product(bank[:, t * DV:(t + 1) * DV], [(xpart(kk, at, P), col(n, kk, 0, SW)) for kk in range(KT)])
                elif kind == "mv":
                    for t in range(2):
                        if t:
                            mid()
                        last = product(bank[:, t * DV:(t + 1) * DV], [(mpart(kk, t * P, P), col(n, kk, 0, SW)) for kk in range(KT)])
                elif kind == "mk":
                    for t in range(2):
                        if t:
                            mid()
                        last = product(bank[:, t * M:(t + 1) * M], [(col(n, kk, t), mpart(kk, 0, M)) for kk in range(KT)])
                else:
                    at = (r // 2) * HALF
                    order = range(KT) if before is None else EARLY + LATE
                    last = product(bank, [(col(n, kk, r % 2), xpart(kk, at, HALF)) for kk in order], before)
                last.then_inc(s_mm, 1)

            def two_groups(n, half, c, between=None):
                for r in (2 * half, 2 * half + 1):
                    wait_bank(GI[n, r])
                for kk in range(KT):
                    if between is not None:
                        between(kk)
                    lo_ready(pe, c, kk)
                    xh, xl = xpart(kk, half * HALF, HALF)
                    for r in (2 * half, 2 * half + 1):
                        bank = PS[:, GI[n, r] % NB, :]
                        wh, wl = col(n, kk, r % 2)
                        mm(bank, wh, xh, start=(kk == 0), stop=False)
                        mm(bank, wh, xl, start=False, stop=False)
                        last = mm(bank, wl, xh, start=False, stop=(kk == KT - 1))
                        if kk == KT - 1:
                            last.then_inc(s_mm, 1)

            def gates(step, b):
                if step == 0:
                    pe.wait_ge(s_wgs, 1)
                    for half in range(NHALF):
                        for kk in range(KT):
                            xh, xl = xpart(kk, half * HALF, HALF)
                            mm(PS[:, NB + half, :], wgp[:, kk, :], xh, start=(kk == 0), stop=False)
                            last = mm(PS[:, NB + half, :], wgp[:, kk, :], xl, start=False, stop=(kk == KT - 1))
                    last.then_inc(s_gpe, 1)
                if step == 1:
                    pe.wait_ge(s_gr, 1)
                    for t in range(TT):
                        last = nc.tensor.transpose(X2[:, t * 4 * H:(t + 1) * 4 * H], grow[:, t * P:(t + 1) * P],
                                                   ident[0:4 * H, 0:4 * H])
                    last.then_inc(s_gpe, 1)
                if step == 2:
                    pe.wait_ge(s_gd, 2)
                    mm(X1[:, 0:R], tri, lf[:, :], start=True, stop=True)
                    mm(X1[:, R:2 * R], ones[:, :], lf[:, :], start=True, stop=True).then_inc(s_gpe, 1)
                if step == 3:
                    pe.wait_ge(s_gd, 3)
                    nc.tensor.transpose(X2[0:R, 0:P], acol[:, :], ident[:, :]).then_inc(s_gpe, 1)
                if step == 4:
                    pe.wait_ge(s_gd, 4)
                    mm(X3[:, 0:R], ones[0:R, :], gt1[0:R, :], start=True, stop=True).then_inc(s_gpe, 1)
                if step == 5:
                    pe.wait_ge(s_gd, 5)
                    nc.tensor.transpose(X3[:, R:2 * R], murow[:, :], ident[0:R, 0:R]).then_inc(s_gpe, 1)

            def scan(h, p):
                if p >= 3:
                    e = h * TT + p - 3
                    pe.wait_ge(s_hn, e + 1)
                    pe.wait_ge(s_pt, h * TT + min(p, TT))
                    if e >= 1:
                        pe.wait_ge(s_yf, e)
                    for kk in range(2):
                        last = nc.tensor.transpose(X1[:, kk * P:(kk + 1) * P], hs[:, e % 2, kk * P:(kk + 1) * P], ident[:, :])
                    last.then_inc(s_tr, 1)
                if p < TT:
                    e, at = h * TT + p, slice(p * P, (p + 1) * P)
                    if e >= 1:
                        pe.wait_ge(s_ks, e)
                        pe.wait_ge(s_pt, e)
                    if e == 0:
                        pe.wait_ge(s_gd, 6)
                    if p == 0:
                        pe.wait_ge(s_qk, 4 * (h + 1))
                        if h >= 1:
                            pe.wait_ge(s_yf, h * TT)
                        if h == H - 1:
                            pe.wait_ge(s_ml, 2 * MT)
                    k_t = QK[:, h % 2, 1, at]
                    nc.tensor.transpose(X0[:, 0:P], mucol[:, e:e + 1].to_broadcast([P, P]), ident[:, :])
                    nc.tensor.transpose(X0[:, P:2 * P], k_t, ident[:, :]).then_inc(s_mu, 1)
                    mm(X1[:, 2 * P:3 * P], k_t, QK[:, h % 2, 0, at], start=True, stop=True).then_inc(s_st, 1)
                if 1 <= p <= TT:
                    e, c = h * TT + p - 1, p - 1
                    pe.wait_ge(s_pt, e + 1)
                    pe.wait_ge(s_qs, e + 1)
                    pe.wait_ge(s_ks, e + 1)
                    if e >= 1:
                        pe.wait_ge(s_hs, e)
                    if c or h:
                        pe.wait_ge(s_cst, h * (TT - 1) + c)
                    if c == 0:
                        pe.wait_ge(s_fa, FREED[FIRST[AT["v", h]] + 3][1])
                        pe.wait_ge(s_ones, 2)
                    vc = VV[:, h % 2, c, :]
                    last = mm(X2[:, 0:DV + 1], wT[:, :], vc, start=True, stop=(c == 0))
                    if c:
                        last = mm(X2[:, 0:DV + 1], qs[:, :], Cst[:, :], start=False, stop=True)
                    if c < TT - 1:
                        last = mm(X3[:, 0:DV + 1], ks[:, :], vc, start=True, stop=True)
                    last.then_inc(s_b, 1)

            def memturn(a, b):
                for t in range(MT):
                    pe.wait_ge(s_xs, t + 1)
                    if t == 0:
                        pe.wait_ge(s_yf, TT * (H - 1))
                    for q in range(KT):
                        last = nc.tensor.transpose(PS[:, NB + 2 * t + q // 4, (q % 4) * P:(q % 4 + 1) * P],
                                                   mxs[:, t, q * P:(q + 1) * P], ident[:, :])
                    last.then_inc(s_turn, 1)

            def sumsq(which, half):
                c = 2 * which + half
                pe.wait_ge(s_sacc, (KT - 1) * (c - 1))
                if c == 2:
                    pe.wait_ge(s_yf, H * TT)
                else:
                    pe.wait_ge(s_ns, c - 2)
                if c == 4:
                    pe.wait_ge(s_pa, 4 * H)
                for t in range(NT):
                    last = mm(X2[:, t:t + 1], sqsum[which][:, half, t * P:(t + 1) * P], ones[:, 0:1], start=True, stop=True)
                last.then_inc(s_ssq, 1)

            def spread(which, half):
                c = 2 * which + half
                pe.wait_ge(s_nr, c + 1)
                if c == 1:
                    pe.wait_ge(s_xta, 3)
                    pe.wait_ge(s_xt, 7)
                if c == 2:
                    pe.wait_ge(s_ks, H * TT)
                if c == 4:
                    pe.wait_ge(s_yl, H * TT + 4 * H)
                for t in range(NT):
                    last = nc.tensor.transpose(PS[:, BC[c], t * P:(t + 1) * P], nrms[:, half, t:t + 1].to_broadcast([P, P]),
                                               ident[:, :])
                last.then_inc(s_rt, 1)

            def attn(h, p):
                if p < 4:
                    e = 4 * h + p
                    if e >= 2:
                        pe.wait_ge(s_ex, 2 * (e - 1))
                    else:
                        pe.wait_ge(s_xnf, PAT[3, LATE[1]] + 1)
                    if p == 0 and h:
                        pe.wait_ge(s_yl, H * TT + 4 * h)
                    if p == 0:
                        pe.wait_ge(s_fa, FREED[FIRST[AT["q", h]] + 3][1])
                    for j in range(2):
                        at = slice((2 * p + j) * P, (2 * p + j + 1) * P)
                        for kk in range(2):
                            last = mm(PS[:, NB + e % 2, j * M:(j + 1) * M], QH[h % 2][:, kk, at], KM[:, 2 * h + kk, :],
                                      start=(kk == 0), stop=(kk == 1))
                    last.then_inc(s_sc, 1)
                if 1 <= p <= 4:
                    e = 4 * h + p - 1
                    pe.wait_ge(s_pn, e + 1)
                    if e >= 1:
                        pe.wait_ge(s_pa, e)
                    for j in range(2):
                        for m in range(MT):
                            last = nc.tensor.transpose(X2[:, m * SW + j * P:m * SW + (j + 1) * P],
                                                       ptok[:, e % 2, j * M + m * P:j * M + (m + 1) * P], ident[:, :])
                    last.then_inc(s_pt2, 1)
                if p in (3, 5):
                    half = p // 2 - 1
                    pe.wait_ge(s_pa, 4 * h + 2 * half + 2)
                    for dt in range(2):
                        c = 4 * h + 2 * half + dt
                        if c == 0:
                            pe.wait_ge(s_yf, H * TT)
                        if c >= 2:
                            pe.wait_ge(s_yl, H * TT + c - 1)
                        if p == 3 and dt == 1:
                            pe.wait_ge(s_ex, 2 * (4 * h + 3))
                        for m in range(MT):
                            last = mm((X3, X0)[dt], VM[:, m, h * DV + dt * P:h * DV + (dt + 1) * P],
                                      PA[:, m, half * HALF:(half + 1) * HALF], start=(m == 0), stop=(m == MT - 1))
                        last.then_inc(s_pv, 1)

            todo = {"gates": gates, "scan": scan, "memnorm": lambda a, b: None, "memturn": memturn, "sumsq": sumsq,
                    "spread": spread, "pieces": lambda a, b: None, "attn": attn}

            def turn_x(t):
                pe.wait_ge(s_xin[t % 4], 16 * (t // 4 + 1))
                if t >= 3:
                    pe.wait_ge(s_xt, X_BEFORE[t] + 1)
                if t >= 6:
                    pe.wait_ge(s_xta, X_BEFORE[t] - 3)
                for q in range(KT):
                    last = nc.tensor.transpose(PS[:, X_BANK[t] + q // 4, (q % 4) * P:(q % 4 + 1) * P],
                                               xin[t % 4][:, q * P:(q + 1) * P], ident[:, :])
                last.then_inc(s_turn, 1)

            pe.wait_ge(s_const, 10)
            for t in range(4):
                turn_x(t)
            pe.wait_ge(s_vec, 80)
            nc.tensor.transpose(PS[:, 2, 0:NVEC], vrows, ident[0:NVEC, 0:NVEC]).then_inc(s_vturn, 1)
            spread(0, 0)
            turn_x(4)
            turn_x(5)

            def late_tiles(kk):
                if kk in (2, 4):
                    turn_x(5 + kk // 2)
                if kk == 4:
                    wait_strip(0)
                if kk == 7:
                    spread(0, 1)

            pe.wait_ge(s_wl0, 1)
            two_groups(0, 0, 0, late_tiles)
            two_groups(0, 1, 1)
            for n in range(NF):
                kind, h = STRIPS[n]
                for r in range(NGROUPS[kind]):
                    if n == 0:
                        continue
                    run_parts(n, r, todo)
                    if r == 0:
                        wait_strip(n)
                        if kind == "mk" and h == 0:
                            pe.wait_ge(s_ml, 2 * MT)
                    if kind == "wo" and r in (0, KT):
                        pe.wait_ge(s_yl, TT * h + TT // 2 * (r // KT + 1))
                    if kind == "xo" and r in (0, KT):
                        pe.wait_ge(s_yl, H * TT + 4 * h + 2 * (r // KT + 1))
                    if kind == "q" and h == 0 and r % 2 == 0:
                        group(n, r, before=2 + r // 2)
                    else:
                        group(n, r, mid=lambda: run_parts(n, "mid", todo))
                run_parts(n, "end", todo)

            def ffn_strip(n, i=None, lo=None):
                k = 0 if i is None else i
                wait_strip(n, k)
                if lo is not None:
                    pe.wait_ge(s_yl, lo + 8 * k)
                for r in range(NGROUPS[STRIPS[n][0]]):
                    group(n, r, k)

            wait_strip(NF)
            two_groups(NF, 0, 4)
            sumsq(2, 1)
            wait_strip(NF + 1)
            group(NF + 1, 0)
            spread(2, 1)
            group(NF + 1, 1)
            two_groups(NF, 1, 5)
            group(NF + 1, 2)
            group(NF + 1, 3)
            pe.wait_ge(s_fa, FREED[GI[NF, 3]][1])
            with pe.Fori(0, NJ // 2) as i:
                for u in range(2):
                    n = NF + 2 + 3 * u
                    ffn_strip(n, i)
                    ffn_strip(n + 1, i, lo=Y_FFN + 4 * (u + 1))
                    ffn_strip(n + 2, i)
            def turn_back(t):
                pe.wait_ge(s_fd, FREED[FIRST[len(STRIPS) - 1] + (7 if t < 4 else 15 if t < 6 else 23)][1])
                if 2 <= t < 6:
                    pe.wait_ge(s_xs, MT + t - 1)
                for q in range(KT):
                    last = nc.tensor.transpose(out_banks(t)[:, q * P:(q + 1) * P], xT[:, q, t * P:(t + 1) * P], ident[:, :])
                last.then_inc(s_turn, 1)

            n = len(STRIPS) - 1
            wait_strip(n)
            for r in range(24):
                if r in (0, KT):
                    pe.wait_ge(s_yl, Y_FFN + 4 * NJ - (0 if r else 2))
                if r in TURN:
                    turn_back(TURN.index(r))
                ft, at, width = last_tile(r)
                wait_bank(FIRST[n] + r)
                product(PS[:, (FIRST[n] + r) % NB, 0:width],
                        [(rowt(n, kk, ft), (YH[:, kk, at:at + width], YL[:, kk, at:at + width])) for kk in range(2)]).then_inc(s_mm, 1)
            for t in range(len(TURN), TT):
                turn_back(t)


_INS = ["x", "mem", "norm_mix", "norm_x", "norm_ffn", "norm_mem", "norm_final", "a_w_in", "a_conv_w", "a_gate_b",
        "a_norm", "a_w_out", "x_w_q", "x_w_kv", "x_w_o", "f_w_gate", "f_w_up", "f_w_down"]


def kernel(**inputs):
    import numpy as _np
    import concourse.bacc as _bacc
    from concourse import mybir as _mybir
    from concourse.bass_utils import run_bass_kernel_spmd as _run

    nc = _bacc.Bacc("TRN2", target_bir_lowering=False, num_devices=1)
    arrays, args = {}, []
    for name in _INS:
        a = _np.ascontiguousarray(inputs[name])
        arrays[f"in_{name}_dram"] = a
        args.append(nc.dram_tensor(f"in_{name}_dram", a.shape, _mybir.dt.from_np(a.dtype), kind="ExternalInput").ap())
    args.append(nc.dram_tensor("out_0_dram", inputs["x"].shape, _mybir.dt.float32, kind="ExternalOutput").ap())
    build_block(nc, *args)
    r = _run(nc, [arrays], core_ids=[0])
    return r.results[0]["out_0_dram"]
```
